# Optimizing a Trainium2 kernel written in Bass

```python
import math
import jax, jax.numpy as jnp
from jax import lax
import numpy as np

D_MODEL = 1024
BATCH = 1
SEQ = 512
DEPTH = 1

MEM_LEN = 256
HEAD_DIM = 64
N_FOX_HEADS = (D_MODEL // 2) // HEAD_DIM
N_MOBA_HEADS = (D_MODEL // 2) // HEAD_DIM
FOX_WIDTH = N_FOX_HEADS * HEAD_DIM
MOBA_WIDTH = N_MOBA_HEADS * HEAD_DIM
MIX_WIDTH = FOX_WIDTH + MOBA_WIDTH
IN_COLS = 3 * FOX_WIDTH + N_FOX_HEADS + 3 * MOBA_WIDTH
FOX_Q_BLOCK = 128
MOBA_BLOCK = 256
MOBA_TOP_K = 3
MOBA_Q_BLOCK = 32
N_CROSS_HEADS = 4
CROSS_HEAD_DIM = D_MODEL // N_CROSS_HEADS
D_FF = 128 * (-(-(8 * D_MODEL // 3) // 128))
CONV_WIDTH = 3
EPS = 1e-6

kernel_name = "hymba_fox_moba_convffn_layer"

def rmsnorm(x, g):
    xf = x.astype(jnp.float32)
    y = xf * lax.rsqrt(jnp.mean(xf * xf, axis=-1, keepdims=True) + EPS)
    return (y * g.astype(jnp.float32)).astype(x.dtype)

def to_heads(t, n_heads):
    b, s, _ = t.shape
    return t.reshape(b, s, n_heads, HEAD_DIM).transpose(0, 2, 1, 3)

def from_heads(t):
    b, h, s, d = t.shape
    return t.transpose(0, 2, 1, 3).reshape(b, s, h * d)

def fox_attention(q, k, v, log_f):
    B, H, S, dh = q.shape
    c = jnp.cumsum(log_f, axis=-1)
    scale = dh ** -0.5
    kpos = jnp.arange(S)

    def block(i):
        start = i * FOX_Q_BLOCK
        qb = lax.dynamic_slice_in_dim(q, start, FOX_Q_BLOCK, axis=2)
        cb = lax.dynamic_slice_in_dim(c, start, FOX_Q_BLOCK, axis=2)
        qpos = start + jnp.arange(FOX_Q_BLOCK)
        s = jnp.einsum('bhqd,bhkd->bhqk', qb, k, preferred_element_type=jnp.float32) * scale
        s = s + cb[..., :, None] - c[..., None, :]
        s = jnp.where(kpos[None, :] <= qpos[:, None], s, -jnp.inf)
        p = jax.nn.softmax(s, axis=-1)
        return jnp.einsum('bhqk,bhkd->bhqd', p.astype(v.dtype), v)

    out = lax.map(block, jnp.arange(S // FOX_Q_BLOCK))
    return jnp.moveaxis(out, 0, 2).reshape(B, H, S, dh)

def moba_attention(q, k, v, slopes):
    B, H, S, dh = q.shape
    n_blk = -(-S // MOBA_BLOCK)
    s_pad = n_blk * MOBA_BLOCK
    pad = ((0, 0), (0, 0), (0, s_pad - S), (0, 0))
    kb = jnp.pad(k, pad).reshape(B, H, n_blk, MOBA_BLOCK, dh)
    vb = jnp.pad(v, pad).reshape(B, H, n_blk, MOBA_BLOCK, dh)
    k_mean = jnp.mean(kb.astype(jnp.float32), axis=3)
    top_k = min(MOBA_TOP_K, n_blk)
    scale = dh ** -0.5
    offs = jnp.arange(MOBA_BLOCK)
    blk_ids = jnp.arange(n_blk)
    bidx = jnp.arange(B)[:, None, None, None]
    hidx = jnp.arange(H)[None, :, None, None]
    sl5 = slopes[None, :, None, None, None]
    sl4 = slopes[None, :, None, None]

    def chunk(i):
        start = i * MOBA_Q_BLOCK
        qb = lax.dynamic_slice_in_dim(q, start, MOBA_Q_BLOCK, axis=2)
        qpos = start + jnp.arange(MOBA_Q_BLOCK)
        own = start // MOBA_BLOCK
        gate = jnp.einsum('bhqd,bhnd->bhqn', qb.astype(jnp.float32), k_mean)
        gate = jnp.where(blk_ids < own, gate, -jnp.inf)
        _, sel = lax.top_k(gate, top_k)
        valid = sel < own
        k_sel = kb[bidx, hidx, sel]
        v_sel = vb[bidx, hidx, sel]
        s_sel = jnp.einsum('bhqd,bhqnkd->bhqnk', qb, k_sel,
                           preferred_element_type=jnp.float32) * scale
        dist_sel = (qpos[None, None, :, None, None]
                    - (sel[..., None] * MOBA_BLOCK + offs)).astype(jnp.float32)
        s_sel = jnp.where(valid[..., None], s_sel - sl5 * dist_sel, -jnp.inf)
        s_sel = s_sel.reshape(B, H, MOBA_Q_BLOCK, top_k * MOBA_BLOCK)
        k_own = kb[:, :, own]
        v_own = vb[:, :, own]
        s_own = jnp.einsum('bhqd,bhkd->bhqk', qb, k_own,
                           preferred_element_type=jnp.float32) * scale
        dist_own = (qpos[:, None] - (own * MOBA_BLOCK + offs)[None, :]).astype(jnp.float32)
        s_own = jnp.where(dist_own >= 0, s_own - sl4 * dist_own, -jnp.inf)
        p = jax.nn.softmax(jnp.concatenate([s_sel, s_own], axis=-1), axis=-1).astype(v.dtype)
        p_sel = p[..., :top_k * MOBA_BLOCK].reshape(B, H, MOBA_Q_BLOCK, top_k, MOBA_BLOCK)
        p_own = p[..., top_k * MOBA_BLOCK:]
        return (jnp.einsum('bhqnk,bhqnkd->bhqd', p_sel, v_sel)
                + jnp.einsum('bhqk,bhkd->bhqd', p_own, v_own))

    out = lax.map(chunk, jnp.arange(S // MOBA_Q_BLOCK))
    return jnp.moveaxis(out, 0, 2).reshape(B, H, S, dh)

def alibi_slopes(n_heads):
    return 2.0 ** (-8.0 * jnp.arange(1, n_heads + 1, dtype=jnp.float32) / n_heads)

def hybrid_mixer(a, w_in, b_forget, g_fox, g_moba, w_out):
    proj = a @ w_in
    cuts = [int(c) for c in np.cumsum([FOX_WIDTH, FOX_WIDTH, FOX_WIDTH, N_FOX_HEADS,
                                       MOBA_WIDTH, MOBA_WIDTH])]
    q_f, k_f, v_f, f_logit, q_m, k_m, v_m = jnp.split(proj, cuts, axis=-1)
    log_f = jax.nn.log_sigmoid(f_logit.astype(jnp.float32)
                               + b_forget.astype(jnp.float32)).transpose(0, 2, 1)
    o_f = fox_attention(to_heads(q_f, N_FOX_HEADS), to_heads(k_f, N_FOX_HEADS),
                        to_heads(v_f, N_FOX_HEADS), log_f)
    o_m = moba_attention(to_heads(q_m, N_MOBA_HEADS), to_heads(k_m, N_MOBA_HEADS),
                         to_heads(v_m, N_MOBA_HEADS), alibi_slopes(N_MOBA_HEADS))
    y = jnp.concatenate([rmsnorm(from_heads(o_f), g_fox),
                         rmsnorm(from_heads(o_m), g_moba)], axis=-1)
    return y @ w_out

def memory_cross_attention(a, mem_n, w_q, w_kv, w_o):
    B, S, _ = a.shape
    M = mem_n.shape[1]
    q = (a @ w_q).reshape(B, S, N_CROSS_HEADS, CROSS_HEAD_DIM)
    k, v = jnp.split(mem_n @ w_kv, 2, axis=-1)
    k = k.reshape(B, M, N_CROSS_HEADS, CROSS_HEAD_DIM)
    v = v.reshape(B, M, N_CROSS_HEADS, CROSS_HEAD_DIM)
    s = jnp.einsum('bshd,bmhd->bhsm', q, k,
                   preferred_element_type=jnp.float32) * CROSS_HEAD_DIM ** -0.5
    p = jax.nn.softmax(s, axis=-1).astype(v.dtype)
    o = jnp.einsum('bhsm,bmhd->bshd', p, v).reshape(B, S, D_MODEL)
    return o @ w_o

def conv_glu_ffn(a, w_up, conv_w, conv_b, w_down):
    S = a.shape[1]
    g, u = jnp.split(a @ w_up, 2, axis=-1)
    gp = jnp.pad(g, ((0, 0), (CONV_WIDTH - 1, 0), (0, 0)))
    gc = conv_b + sum(conv_w[j] * gp[:, j:j + S] for j in range(CONV_WIDTH))
    return (jax.nn.silu(gc) * u) @ w_down

def setup_inputs(seed: int = 0) -> dict:
    key = jax.random.key(seed)
    ks = jax.random.split(key, 24)
    f32 = jnp.float32
    nrm = lambda k, shape, s: jax.random.normal(k, shape, f32) * s
    gain = lambda k, shape: 1.0 + 0.02 * jax.random.normal(k, shape, f32)
    L = DEPTH
    return {
        "x": jax.random.normal(ks[0], (BATCH, SEQ, D_MODEL), f32),
        "mem": jax.random.normal(ks[1], (BATCH, MEM_LEN, D_MODEL), f32),
        "g_mix": gain(ks[2], (L, D_MODEL)),
        "w_in": nrm(ks[3], (L, D_MODEL, IN_COLS), D_MODEL ** -0.5),
        "b_forget": 3.0 + 0.5 * jax.random.normal(ks[4], (L, N_FOX_HEADS), f32),
        "g_fox": gain(ks[5], (L, FOX_WIDTH)),
        "g_moba": gain(ks[6], (L, MOBA_WIDTH)),
        "w_out": nrm(ks[7], (L, MIX_WIDTH, D_MODEL), MIX_WIDTH ** -0.5),
        "g_cross": gain(ks[8], (L, D_MODEL)),
        "g_mem": gain(ks[9], (L, D_MODEL)),
        "w_q_mem": nrm(ks[10], (L, D_MODEL, D_MODEL), D_MODEL ** -0.5),
        "w_kv_mem": nrm(ks[11], (L, D_MODEL, 2 * D_MODEL), D_MODEL ** -0.5),
        "w_o_mem": nrm(ks[12], (L, D_MODEL, D_MODEL), D_MODEL ** -0.5),
        "g_ffn": gain(ks[13], (L, D_MODEL)),
        "w_up": nrm(ks[14], (L, D_MODEL, 2 * D_FF), D_MODEL ** -0.5),
        "conv_w": nrm(ks[15], (L, CONV_WIDTH, D_FF), CONV_WIDTH ** -0.5),
        "conv_b": nrm(ks[16], (L, D_FF), 0.02),
        "w_down": nrm(ks[17], (L, D_FF, D_MODEL), D_FF ** -0.5),
        "g_final": gain(ks[18], (D_MODEL,)),
    }

def reference(x, mem, g_mix, w_in, b_forget, g_fox, g_moba, w_out, g_cross, g_mem,
              w_q_mem, w_kv_mem, w_o_mem, g_ffn, w_up, conv_w, conv_b, w_down, g_final):
    h = x
    for l in range(DEPTH):
        h = h + hybrid_mixer(rmsnorm(h, g_mix[l]), w_in[l], b_forget[l],
                             g_fox[l], g_moba[l], w_out[l])
        h = h + memory_cross_attention(rmsnorm(h, g_cross[l]), rmsnorm(mem, g_mem[l]),
                                       w_q_mem[l], w_kv_mem[l], w_o_mem[l])
        h = h + conv_glu_ffn(rmsnorm(h, g_ffn[l]), w_up[l], conv_w[l], conv_b[l], w_down[l])
    return rmsnorm(h, g_final)


_drawn_inputs = setup_inputs


def setup_inputs(seed=0):
    import zlib

    import numpy as np

    out = dict(_drawn_inputs(seed))
    spreads = {}
    factors = {'g_fox': 5.136,
     'g_moba': 5.024,
     'g_cross': 8.0,
     'g_mem': 8.0,
     'g_ffn': 4.792,
     'conv_b': 7.341,
     'g_final': 2.907}
    for name, (base, spread) in spreads.items():
        noise = np.random.default_rng([zlib.crc32(name.encode()), seed]).standard_normal(out[name].shape)
        drawn = base * np.exp(spread * noise) if base else spread * noise
        out[name] = __import__('jax').numpy.asarray(drawn.astype(out[name].dtype))
    for name, factor in factors.items():
        out[name] = (out[name] * factor).astype(out[name].dtype)
    return out
```

```python
from contextlib import ExitStack

import concourse.bass as bass
from concourse import mybir

F32 = mybir.dt.float32
F32R = mybir.dt.float32r
ALU = mybir.AluOpType
ACT = mybir.ActivationFunctionType
AX_X = mybir.AxisListType.X

P = 128
EPS = 1e-6
BIG = 1.0e30
FLT_MAX = 3.0e38


def hymba_layer(nc, x, mem, g_mix, w_in, b_forget, g_fox, g_moba, w_out, g_cross, g_mem, w_q_mem,
                w_kv_mem, w_o_mem, g_ffn, w_up, conv_w, conv_b, w_down, g_final, out):
    SEQ, D = x.shape[1], x.shape[2]
    MEM = mem.shape[1]
    NH = b_forget.shape[1]
    GW = g_fox.shape[1]
    HD = GW // NH
    FF = conv_b.shape[1]
    TAPS = conv_w.shape[1]
    NT = SEQ // P
    MT = MEM // P
    KT = D // P
    FT = FF // P
    CROSS_D = 256
    NX = D // CROSS_D
    NPAIR = 2 * GW // P
    FOXP = GW // P
    UNITS = 2 * NT
    H2 = D // 512
    assert (SEQ, D, MEM, HD, NH, NT, KT, H2) == (512, 1024, 256, 64, 8, 4, 8, 2) and TAPS == 3

    x_t = x[0].rearrange("(i p) d -> p i d", p=P)
    mem_t = mem[0].rearrange("(i p) d -> p i d", p=P)
    out_t = out[0].rearrange("(i p) d -> p i d", p=P)
    w_in, w_out, w_q_mem, w_kv_mem, w_o_mem = w_in[0], w_out[0], w_q_mem[0], w_kv_mem[0], w_o_mem[0]
    w_up, w_down = w_up[0], w_down[0]

    CH = 1024

    def f_chunk(w, col):
        return w[:, col:col + P].rearrange("(k p) n -> p k n", p=P)

    def t_chunk(w, k, half):
        return w[k * P:(k + 2) * P, half * 512:half * 512 + 512].rearrange("(k p) n -> p k n", p=P)

    MOBA0 = 3 * GW + NH
    chunks = []
    for pair in range(NPAIR):
        base = pair * P if pair < FOXP else MOBA0 + (pair - FOXP) * P
        chunks += [f_chunk(w_in, base + j * GW) for j in range(3)]
    KV0 = len(chunks)
    chunks += [f_chunk(w_kv_mem, m * P) for m in range(KT)]
    VM0 = len(chunks)
    chunks += [t_chunk(w_kv_mem[:, D:], k, h) for h in range(H2) for k in range(0, KT, 2)]
    WO0 = len(chunks)
    chunks += [t_chunk(w_out, k, h) for h in range(H2) for k in range(0, KT, 2)]
    WQ0 = len(chunks)
    chunks += [f_chunk(w_q_mem, m * P) for m in range(KT)]
    XO0 = len(chunks)
    chunks += [t_chunk(w_o_mem, k, h) for h in range(H2) for k in range(0, KT, 2)]
    UP0 = len(chunks)
    for j in range(FT):
        chunks += [f_chunk(w_up, j * P), f_chunk(w_up, FF + j * P)]
    DN0 = len(chunks)
    chunks += [t_chunk(w_down, k, h) for h in range(H2) for k in range(0, FT, 2)]
    NCH = len(chunks)
    RING = 3

    c_dram = nc.dram_tensor("c_scratch", (NH, SEQ), F32, kind="Internal").ap()

    with ExitStack() as ctx:
        def sb(name, shape, dt=F32):
            return ctx.enter_context(nc.sbuf_tensor(name, shape, dt))

        def sem(name):
            return ctx.enter_context(nc.semaphore(name))

        bank = [ctx.enter_context(nc.psum_tensor(f"bank{b}", [P, 512], F32)) for b in range(8)]
        PJ, SC, PT, OB = bank[0:2], bank[2:4], bank[4:6], bank[6:8]

        tok = sb("tok", [P, NT, D])
        misc = sb("misc", [P, NT, D])
        act_h = sb("act_h", [P, KT, SEQ], F32R)
        act_l = sb("act_l", [P, KT, SEQ], F32R)
        w_raw = sb("w_raw", [P, RING, CH])
        w_h = sb("w_h", [P, RING, CH], F32R)
        w_l = sb("w_l", [P, RING, CH], F32R)
        big = sb("big", [P, 2 * FT * SEQ], F32R)
        row = sb("row", [P, D])
        v_raw = row[:, 0:SEQ]
        dist = row[:, SEQ:2 * SEQ]
        fmask = sb("fmask", [P, P])
        ident = sb("ident", [P, P])
        vec_rows = sb("vec_rows", [P, P])
        vec = sb("vec", [P, P])
        wf_raw = sb("wf_raw", [P, KT, NH])
        wf_h = sb("wf_h", [P, KT, NH], F32R)
        wf_l = sb("wf_l", [P, KT, NH], F32R)
        z_tok = sb("z_tok", [P, NT, NH])
        b_col = sb("b_col", [NH, 1])
        minima = sb("minima", [P, NPAIR * UNITS])
        sums = sb("sums", [P, NPAIR * UNITS])
        inv_sums = sb("inv_sums", [P, NPAIR * UNITS])
        NSTAGE = 6
        ss = sb("ss", [P, NSTAGE, 8])
        ms = sb("ms", [P, NSTAGE, 8])
        ln_ms = sb("ln_ms", [P, NSTAGE, 8])
        r0 = sb("r0", [P, NSTAGE, 8])
        nt_ = sb("nt_", [P, NSTAGE, 8])
        nt2 = sb("nt2", [P, NSTAGE, 8])
        rinv = sb("rinv", [P, NSTAGE, 8])

        def part(lo, shape):
            n = 1
            for s in shape:
                n *= s
            v = big[:, lo:lo + n]
            if len(shape) == 2:
                v = v.rearrange("p (a b) -> p a b", a=shape[0])
            if len(shape) == 3:
                v = v.rearrange("p (a b c) -> p a b c", a=shape[0], b=shape[1])
            return v

        qk_h, qk_l = part(0, [2, 2, SEQ]), part(2048, [2, 2, SEQ])
        km_h, km_l = part(4096, [KT, MEM]), part(6144, [KT, MEM])
        vm_h, vm_l = part(8192, [MT, D]), part(10240, [MT, D])
        v_h, v_l = part(12288, [2, NT, P]), part(13312, [2, NT, P])
        mn_h, mn_l = part(14336, [KT, MEM]), part(16384, [KT, MEM])
        ox_h, ox_l = part(12288, [KT, SEQ]), part(16384, [KT, SEQ])
        pt_h, pt_l = part(20480, [2, SEQ]), part(21504, [2, SEQ])
        ff_h, ff_l = part(0, [FT, SEQ]), part(FT * SEQ, [FT, SEQ])

        flat = misc[:, :, :].rearrange("p a b -> p (a b)")
        lg = flat[:, 0:1024].rearrange("p (a b) -> p a b", a=2)
        pr = flat[:, 1024:2048].rearrange("p (a b) -> p a b", a=2)
        cb = flat[:, 2048:3072].rearrange("p (a b) -> p a b", a=2)
        cbd = flat[:, 3072:4096].rearrange("p (a b) -> p a b", a=2)
        fz = [flat[0:NH, 2048 + 512 * j:2560 + 512 * j] for j in range(4)]

        VEC = {}
        at = 0
        for name, src in (("mix", g_mix), ("mem", g_mem), ("fox", g_fox), ("moba", g_moba),
                          ("cross", g_cross), ("ffn", g_ffn), ("cw", conv_w), ("cb", conv_b)):
            n = 1
            for s in src.shape:
                n *= s
            VEC[name] = (at, n // P, src)
            at += n // P
        assert at <= P
        VROWS = at

        def col(name, k):
            return vec[:, VEC[name][0] + k:VEC[name][0] + k + 1]

        w_landed = [sem(f"w_landed{s}") for s in range(RING)]
        w_hi, w_lo, w_used = sem("w_hi"), sem("w_lo"), sem("w_used")
        x_landed = [sem(f"x_landed{i}") for i in range(NT)]
        mem_landed, vec_landed = sem("mem_landed"), sem("vec_landed")
        wf_landed, b_landed = sem("wf_landed"), sem("b_landed")
        c_stored = sem("c_stored")
        c_landed = [sem(f"c_landed{s}") for s in range(2)]
        x2_landed, gf_landed, out_stored = sem("x2_landed"), sem("gf_landed"), sem("out_stored")
        ident_ready, masks_ready = sem("ident_ready"), sem("masks_ready")
        vec_turned, vec_ready = sem("vec_turned"), sem("vec_ready")
        sq_act = [sem(f"sq_act{s}") for s in range(NSTAGE)]
        sq_dve = [sem(f"sq_dve{s}") for s in range(NSTAGE)]
        ms_ready = [sem(f"ms_ready{s}") for s in range(NSTAGE)]
        guess = [sem(f"guess{s}") for s in range(NSTAGE)]
        newton = [sem(f"newton{s}") for s in range(NSTAGE)]
        nrm_act = [sem(f"nrm_act{s}") for s in range(NSTAGE)]
        nrm_dve = [sem(f"nrm_dve{s}") for s in range(NSTAGE)]
        turned = [sem(f"turned{s}") for s in range(NSTAGE)]
        act_hi = [sem(f"act_hi{s}") for s in range(NSTAGE)]
        act_lo = [sem(f"act_lo{s}") for s in range(NSTAGE)]
        wf_hi, wf_lo = sem("wf_hi"), sem("wf_lo")
        z_done, z_copied, z_turned = sem("z_done"), sem("z_copied"), sem("z_turned")
        f_act, f_dve = sem("f_act"), sem("f_dve")
        proj_hi, proj_lo = sem("proj_hi"), sem("proj_lo")
        v_copied, v_turned, v_hi, v_lo = sem("v_copied"), sem("v_turned"), sem("v_hi"), sem("v_lo")
        s_done, bias_ready, lg_ready = sem("s_done"), sem("bias_ready"), sem("lg_ready")
        off_ready = sem("off_ready")
        p_ready, p_turned = sem("p_ready"), sem("p_turned")
        pt_hi, pt_lo, pv_done = sem("pt_hi"), sem("pt_lo"), sem("pv_done")
        inv_ready, y_ready = sem("inv_ready"), sem("y_ready")
        km_hi, km_lo = sem("km_hi"), sem("km_lo")
        vm_hi, vm_lo = sem("vm_hi"), sem("vm_lo")
        out_done = [sem(f"out_done{s}") for s in range(3)]
        added = [sem(f"added{s}") for s in range(3)]
        xq_hi, xq_lo = sem("xq_hi"), sem("xq_lo")
        xs_done, xmin, xp_ready = sem("xs_done"), sem("xmin"), sem("xp_ready")
        xinv, xp_norm, xp_turned = sem("xinv"), sem("xp_norm"), sem("xp_turned")
        xpt_hi, xpt_lo = sem("xpt_hi"), sem("xpt_lo")
        xo_done, xo_hi, xo_lo = sem("xo_done"), sem("xo_hi"), sem("xo_lo")
        g_scaled, g_conv1, g_conv2 = sem("g_scaled"), sem("g_conv1"), sem("g_conv2")
        g_silu, h_ready, h_hi, h_lo = sem("g_silu"), sem("h_ready"), sem("h_hi"), sem("h_lo")
        fin_ready = sem("fin_ready")

        S_X, S_MEM, S_Y, S_H1, S_H2, S_FIN = range(NSTAGE)
        TILES = {S_X: NT, S_MEM: MT, S_Y: NT, S_H1: NT, S_H2: NT, S_FIN: NT}
        ENTRIES = {s: 2 * NT if s == S_Y else TILES[s] for s in range(NSTAGE)}

        def entry(buf, s, e):
            if s == S_Y:
                return buf[:, e // 2, (e % 2) * GW:(e % 2 + 1) * GW]
            return buf[:, e, :]

        def gain(s, k):
            if s == S_Y:
                return col("fox", k) if k < FOXP else col("moba", k - FOXP)
            return col({S_X: "mix", S_MEM: "mem", S_H1: "cross", S_H2: "ffn"}[s], k)

        def dst(s, k):
            return (mn_h[:, k, :], mn_l[:, k, :]) if s == S_MEM else (act_h[:, k, :], act_l[:, k, :])

        TURN = {S_X: bank[4:8], S_MEM: bank[2:6], S_Y: bank[2:6], S_H1: bank[4:8], S_H2: bank[4:8]}

        def src_ready(eng, s, e):
            if s == S_X:
                eng.wait_ge(x_landed[e], 16)
            elif s == S_MEM:
                eng.wait_ge(mem_landed, 16)
            elif s == S_Y:
                eng.wait_ge(y_ready, NPAIR)
            else:
                eng.wait_ge(added[s - S_H1], NT * (H2 - 1) + e + 1)

        def half_of(s):
            return ENTRIES[s] // 2

        def norm_stats_act(act, s):
            for e in range(half_of(s)):
                src_ready(act, s, e)
                if s == S_MEM:
                    act.wait_ge(turned[S_X], KT)
                nc.scalar.activation(entry(misc, s, e), entry(tok, s, e), ACT.Square,
                                     accum_out=ss[:, s, e:e + 1]).then_inc(sq_act[s], 1)

        def norm_stats_dve(dve, s):
            for e in range(half_of(s), ENTRIES[s]):
                src_ready(dve, s, e)
                if s == S_MEM:
                    dve.wait_ge(turned[S_X], KT)
                nc.vector.tensor_tensor_reduce(entry(misc, s, e), entry(tok, s, e), entry(tok, s, e), 1.0, 0.0,
                                               ALU.mult, ALU.add, ss[:, s, e:e + 1]).then_inc(sq_dve[s], 1)
            n = ENTRIES[s]
            dve.wait_ge(sq_act[s], half_of(s))
            dve.wait_ge(sq_dve[s], n - half_of(s))
            nc.vector.tensor_scalar(ms[:, s, 0:n], ss[:, s, 0:n], 1.0 / (GW if s == S_Y else D), EPS,
                                    ALU.mult, ALU.add).then_inc(ms_ready[s], 1)

        def norm_guess_act(act, s):
            n = ENTRIES[s]
            act.wait_ge(ms_ready[s], 1)
            nc.scalar.activation(ln_ms[:, s, 0:n], ms[:, s, 0:n], ACT.Ln).then_inc(guess[s], 1)
            act.wait_ge(guess[s], 1)
            nc.scalar.activation(r0[:, s, 0:n], ln_ms[:, s, 0:n], ACT.Exp, scale=-0.5).then_inc(guess[s], 1)

        def norm_newton_dve(dve, s):
            n = ENTRIES[s]
            dve.wait_ge(guess[s], 2)
            nc.vector.tensor_tensor(nt_[:, s, 0:n], r0[:, s, 0:n], r0[:, s, 0:n], ALU.mult).then_inc(newton[s], 1)
            dve.wait_ge(newton[s], 1)
            nc.vector.scalar_tensor_tensor(out=nt2[:, s, 0:n], in0=nt_[:, s, 0:n], scalar=-0.5,
                                           in1=ms[:, s, 0:n], op0=ALU.mult, op1=ALU.mult).then_inc(newton[s], 1)
            dve.wait_ge(newton[s], 2)
            nc.vector.scalar_tensor_tensor(out=rinv[:, s, 0:n], in0=nt2[:, s, 0:n], scalar=1.5,
                                           in1=r0[:, s, 0:n], op0=ALU.add, op1=ALU.mult).then_inc(newton[s], 1)
            dve.wait_ge(newton[s], 3)

        def norm_apply_act(act, s):
            act.wait_ge(newton[s], 3)
            for e in range(half_of(s)):
                nc.scalar.activation(entry(misc, s, e), entry(tok, s, e), ACT.Copy,
                                     scale=rinv[:, s, e:e + 1]).then_inc(nrm_act[s], 1)

        def norm_apply_dve(dve, s):
            for e in range(half_of(s), ENTRIES[s]):
                nc.vector.tensor_scalar(entry(misc, s, e), entry(tok, s, e), rinv[:, s, e:e + 1], None,
                                        ALU.mult).then_inc(nrm_dve[s], 1)

        def norm_turn_pe(pe, s):
            pe.wait_ge(nrm_act[s], half_of(s))
            pe.wait_ge(nrm_dve[s], ENTRIES[s] - half_of(s))
            for k in range(KT):
                if k >= 4:
                    pe.wait_ge(act_lo[s], k - 3)
                for i in range(TILES[s]):
                    last = nc.tensor.transpose(TURN[s][k % 4][:, i * P:(i + 1) * P],
                                               misc[:, i, k * P:(k + 1) * P], ident[:, :])
                last.then_inc(turned[s], 1)

        def norm_hi_act(act, s):
            w = TILES[s] * P
            for k in range(KT):
                act.wait_ge(turned[s], k + 1)
                nc.scalar.activation(dst(s, k)[0], TURN[s][k % 4][:, 0:w], ACT.Copy,
                                     scale=gain(s, k)).then_inc(act_hi[s], 1)

        def norm_lo_dve(dve, s):
            w = TILES[s] * P
            for k in range(KT):
                dve.wait_ge(act_hi[s], k + 1)
                nc.vector.scalar_tensor_tensor(out=dst(s, k)[1], in0=TURN[s][k % 4][:, 0:w], scalar=gain(s, k),
                                               in1=dst(s, k)[0].bitcast(F32), op0=ALU.mult,
                                               op1=ALU.subtract).then_inc(act_lo[s], 1)

        def w_split_act(act, c):
            act.wait_ge(w_landed[c % RING], 16 * (c // RING + 1))
            if c >= RING:
                act.wait_ge(w_used, c - RING + 1)
            nc.scalar.activation(w_h[:, c % RING, :], w_raw[:, c % RING, :], ACT.Copy).then_inc(w_hi, 1)

        def w_split_dve(dve, c):
            dve.wait_ge(w_hi, c + 1)
            nc.vector.tensor_tensor(w_l[:, c % RING, :], w_raw[:, c % RING, :],
                                    w_h[:, c % RING, :].bitcast(F32), ALU.subtract).then_inc(w_lo, 1)

        def mm3(o, sh, sl, mh, ml, start, stop):
            nc.tensor.matmul(o, sl, mh, start=start, stop=False)
            nc.tensor.matmul(o, sh, ml, start=False, stop=False)
            return nc.tensor.matmul(o, sh, mh, start=False, stop=stop)

        OUT0, OUT_K = (WO0, XO0, DN0), (KT // 2, KT // 2, FT // 2)

        def out_bank(s, half, i):
            return bank[4 * half + i] if s < 2 else bank[4 * (1 - half) + i]

        def w_tile(c, k, w):
            return (w_h[:, c % RING, k * w:(k + 1) * w], w_l[:, c % RING, k * w:(k + 1) * w])

        PER_STEP = 3 * KT // UNITS

        def unit(n):
            pair, u = divmod(n, UNITS)
            return pair, u // NT, u % NT

        NU = NPAIR * UNITS

        KV_STEPS = {}
        for u in range(4):
            KV_STEPS[NU - UNITS + u] = [KV0 + 2 * u, KV0 + 2 * u + 1]
        for u in range(4, 8):
            KV_STEPS[NU - UNITS + u] = [VM0 + u - 4]
        KV_STEPS[NU] = [VM0 + 4]
        KV_STEPS[NU + 1] = [VM0 + 5]
        KV_TAIL = [VM0 + 6, VM0 + 7]

        SPLIT_STEPS = {}
        for pair in range(NPAIR):
            if pair < NPAIR - 1:
                SPLIT_STEPS[pair * UNITS + 1] = [3 * (pair + 1) + 2]
            SPLIT_STEPS[pair * UNITS + 4] = [3 * (pair + 2)]
            SPLIT_STEPS[pair * UNITS + 7] = [3 * (pair + 2) + 1]
        for u in (1, 4, 7):
            SPLIT_STEPS.pop(NU - UNITS + u, None)
        done = KV0 + 2
        for n in range(NU - UNITS, NU + 2):
            upto = max(KV_STEPS.get(n + 1, KV_TAIL)) + 1
            SPLIT_STEPS[n] = list(range(done, upto))
            done = upto

        block = ctx.enter_context(nc.Block())

        @block.sync
        def _(sp):
            for i in range(NT):
                sp.dma_start(tok[:, i, :], x_t[:, i, :]).then_inc(x_landed[i], 16)
            for c in range(NCH):
                if c >= RING:
                    sp.wait_ge(w_lo, c - RING + 1)
                v = w_raw[:, c % RING, :].rearrange("p (k n) -> p k n", k=chunks[c].shape[1])
                sp.dma_start(v, chunks[c]).then_inc(w_landed[c % RING], 16)

        @block.gpsimd
        def _(pool):
            nc.gpsimd.memset(ident[:, :], 0.0).then_inc(ident_ready, 1)
            pool.wait_ge(ident_ready, 1)
            nc.gpsimd.affine_select(out=ident[:, :], in_=ident[:, :], compare_op=ALU.not_equal, fill=1.0,
                                    base=0, pattern=[[-1, P]], channel_multiplier=1).then_inc(ident_ready, 1)
            nc.gpsimd.iota(dist[:, :], pattern=[[-1, SEQ]], base=SEQ - P, channel_multiplier=1,
                           allow_small_or_imprecise_dtypes=True).then_inc(masks_ready, 1)
            nc.gpsimd.memset(fmask[:, :], 0.0).then_inc(masks_ready, 1)
            pool.wait_ge(masks_ready, 2)
            nc.gpsimd.affine_select(out=dist[:, :], in_=dist[:, :], compare_op=ALU.is_ge, fill=BIG,
                                    base=SEQ - P, pattern=[[-1, SEQ]], channel_multiplier=1).then_inc(masks_ready, 1)
            nc.gpsimd.affine_select(out=fmask[:, :], in_=fmask[:, :], compare_op=ALU.is_ge, fill=BIG,
                                    base=0, pattern=[[-1, P]], channel_multiplier=1).then_inc(masks_ready, 1)
            pool.wait_ge(nrm_act[S_X], half_of(S_X))
            pool.wait_ge(nrm_dve[S_X], half_of(S_X))
            pool.dma_start(tok[:, 0:MT, :], mem_t).then_inc(mem_landed, 16)
            pool.wait_ge(f_dve, 4)
            pool.dma_start(c_dram, fz[3]).then_inc(c_stored, 16)
            pool.wait_ge(c_stored, 16)
            for h in range(2 * NH):
                if h >= 2:
                    pool.wait_ge(lg_ready, NT * (h - 1))
                if h < NH:
                    pool.dma_start(cb[:, h % 2, :], c_dram[h, :].partition_broadcast(P)).then_inc(c_landed[h % 2], 16)
                    pool.wait_ge(c_landed[h % 2], 16 * (h // 2 + 1))
                    pool.wait_ge(masks_ready, 4)
                    nc.gpsimd.tensor_tensor(cbd[:, h % 2, :].rearrange("p (i j) -> p i j", j=P),
                                            cb[:, h % 2, :].rearrange("p (i j) -> p i j", j=P),
                                            fmask[:, :].unsqueeze(1).to_broadcast([P, NT, P]),
                                            ALU.add).then_inc(bias_ready, 1)
                else:
                    nc.gpsimd.tensor_scalar(cb[:, h % 2, :], dist[:, :], 2.0 ** (-8.0 * (h - NH + 1) / NH), 0.0,
                                            ALU.mult, ALU.add).then_inc(bias_ready, 1)
            pool.wait_ge(nrm_act[S_Y], half_of(S_Y))
            pool.wait_ge(nrm_dve[S_Y], half_of(S_Y))
            pool.dma_start(tok[:, :, :], x_t).then_inc(x2_landed, 16)
            pool.wait_ge(v_turned, NPAIR)
            pool.wait_ge(bias_ready, 2 * NH)
            pool.dma_start(row[:, :], g_final.partition_broadcast(P)).then_inc(gf_landed, 16)

        @block.scalar
        def _(act):
            for name, (r, n, src) in VEC.items():
                v = src.rearrange("a (k p) -> (a k) p", p=P) if len(src.shape) == 2 else \
                    src.rearrange("a b (k p) -> (a b k) p", p=P)
                act.dma_start(vec_rows[r:r + n, :], v).then_inc(vec_landed, 16)
            act.dma_start(wf_raw[:, :, :], w_in[:, 3 * GW:3 * GW + NH].rearrange("(k p) n -> p k n", p=P))\
               .then_inc(wf_landed, 16)
            act.dma_start(b_col[:, :], b_forget.rearrange("a n -> n a")).then_inc(b_landed, 16)

            def evac_qk(pair, j):
                act.wait_ge(w_used, 3 * pair + j + 1)
                if pair >= 2:
                    act.wait_ge(s_done, UNITS * (pair - 1))
                nc.scalar.activation(qk_h[:, pair % 2, j, :], PJ[j][:, :], ACT.Copy,
                                     scale=-HD ** -0.5 if j == 0 else 1.0).then_inc(proj_hi, 1)

            def copy_v(pair):
                act.wait_ge(w_used, 3 * pair + 3)
                if pair >= 1:
                    act.wait_ge(v_turned, pair)
                nc.scalar.activation(v_raw[:, :], PJ[0][:, :], ACT.Copy).then_inc(v_copied, 1)

            def evac_v(pair):
                act.wait_ge(v_turned, pair + 1)
                if pair >= 2:
                    act.wait_ge(pv_done, UNITS * (pair - 1))
                nc.scalar.activation(v_h[:, pair % 2, :, :].rearrange("p a b -> p (a b)"), PJ[1][:, :],
                                     ACT.Copy).then_inc(v_hi, 1)

            norm_stats_act(act, S_X)
            norm_guess_act(act, S_X)
            norm_apply_act(act, S_X)
            act.wait_ge(vec_ready, 1)
            w_split_act(act, 0)
            norm_hi_act(act, S_X)
            act.wait_ge(wf_landed, 16)
            nc.scalar.activation(wf_h[:, :, :], wf_raw[:, :, :], ACT.Copy).then_inc(wf_hi, 1)
            for c in range(1, 3):
                w_split_act(act, c)
            act.wait_ge(z_done, 1)
            nc.scalar.activation(z_tok[:, :, :].rearrange("p a b -> p (a b)"), SC[0][:, 0:NT * NH],
                                 ACT.Copy).then_inc(z_copied, 1)
            evac_qk(0, 0)
            norm_stats_act(act, S_MEM)
            norm_guess_act(act, S_MEM)
            norm_apply_act(act, S_MEM)
            act.wait_ge(z_turned, 1)
            act.wait_ge(b_landed, 16)
            act.wait_ge(turned[S_X], KT)
            nc.scalar.activation(fz[0], SC[1][0:NH, :], ACT.Abs, bias=b_col[:, :]).then_inc(f_act, 1)
            act.wait_ge(f_act, 1)
            nc.scalar.activation(fz[1], fz[0], ACT.Exp, scale=-1.0).then_inc(f_act, 1)
            act.wait_ge(f_act, 2)
            act.wait_ge(f_dve, 1)
            nc.scalar.activation(fz[0], fz[1], ACT.Ln, bias=1.0).then_inc(f_act, 1)

            evac_qk(0, 1)
            copy_v(0)
            norm_hi_act(act, S_MEM)
            evac_v(0)
            w_split_act(act, 3)
            w_split_act(act, 4)

            def probs(n):
                _, _, i = unit(n)
                w = P * (i + 1)
                act.wait_ge(lg_ready, n + 1)
                if n >= 2:
                    act.wait_ge(p_turned, n - 1)
                nc.scalar.activation(pr[:, n % 2, 0:w], lg[:, n % 2, 0:w], ACT.Exp, scale=-1.0,
                                     bias=minima[:, n:n + 1], accum_out=sums[:, n:n + 1]).then_inc(p_ready, 1)

            def pt_split(n):
                _, _, i = unit(n)
                w = P * (i + 1)
                act.wait_ge(p_turned, n + 1)
                if n >= 2:
                    act.wait_ge(pv_done, n - 1)
                nc.scalar.activation(pt_h[:, n % 2, 0:w], PT[n % 2][:, 0:w], ACT.Copy).then_inc(pt_hi, 1)

            def evac_km(m):
                act.wait_ge(w_used, KV0 + m + 1)
                nc.scalar.activation(km_h[:, m, :], PJ[m % 2][:, 0:MEM], ACT.Copy).then_inc(km_hi, 1)

            def evac_vm(h):
                act.wait_ge(w_used, VM0 + (KT // 2) * (h + 1))
                for m in range(MT):
                    nc.scalar.activation(vm_h[:, m, h * 512:(h + 1) * 512], PJ[m][:, :], ACT.Copy)\
                       .then_inc(vm_hi, 1)

            for n in range(NU + 2):
                pair, u = divmod(n, UNITS)
                if n < NU:
                    probs(n)
                if 1 <= n <= NU:
                    pt_split(n - 1)
                if u == 0 and 1 <= pair < NPAIR:
                    evac_v(pair)
                if pair < NPAIR - 1:
                    if u == 2:
                        evac_qk(pair + 1, 0)
                    if u == 5:
                        evac_qk(pair + 1, 1)
                for c in SPLIT_STEPS.get(n, []):
                    w_split_act(act, c)
                if pair < NPAIR - 1 and u == 7:
                    copy_v(pair + 1)
                for c in KV_STEPS.get(n, []):
                    if c < VM0:
                        evac_km(c - KV0)
                    if c == VM0 + 3:
                        evac_vm(0)
            norm_stats_act(act, S_Y)
            norm_guess_act(act, S_Y)
            norm_apply_act(act, S_Y)
            evac_vm(1)
            w_split_act(act, WO0)
            norm_hi_act(act, S_Y)
            for c in range(WO0 + 1, WQ0 + 1):
                w_split_act(act, c)
            norm_stats_act(act, S_H1)
            norm_guess_act(act, S_H1)
            norm_apply_act(act, S_H1)
            w_split_act(act, WQ0 + 1)
            norm_hi_act(act, S_H1)

            def evac_xq(t):
                act.wait_ge(w_used, WQ0 + t + 1)
                if t >= 4:
                    act.wait_ge(xs_done, NT * (t // 2 - 1))
                nc.scalar.activation(qk_h[:, (t // 2) % 2, t % 2, :], PJ[t % 2][:, :], ACT.Copy,
                                     scale=-CROSS_D ** -0.5).then_inc(xq_hi, 1)

            def xprobs(m):
                act.wait_ge(xmin, m + 1)
                if m >= 2:
                    act.wait_ge(xp_turned, m - 1)
                nc.scalar.activation(pr[:, m % 2, 0:MEM], SC[m % 2][:, 0:MEM], ACT.Exp, scale=-1.0,
                                     bias=minima[:, m:m + 1], accum_out=sums[:, m:m + 1]).then_inc(xp_ready, 1)

            def xpt_split(h):
                act.wait_ge(xp_turned, NT * (h + 1))
                if h >= 1:
                    act.wait_ge(xo_done, 2 * h)
                for t in range(MT):
                    nc.scalar.activation(pt_h[:, t, :], PT[t][:, :], ACT.Copy).then_inc(xpt_hi, 1)

            def evac_xo(h):
                for d in range(2):
                    act.wait_ge(xo_done, 2 * h + d + 1)
                    nc.scalar.activation(ox_h[:, 2 * h + d, :], OB[d][:, :], ACT.Copy).then_inc(xo_hi, 1)

            w_split_act(act, WQ0 + 2)
            evac_xq(0)
            w_split_act(act, WQ0 + 3)
            evac_xq(1)
            for m in range(NX * NT + 2):
                h, i = divmod(m, NT)
                if m < NX * NT:
                    xprobs(m)
                if i == 0 and h >= 1:
                    xpt_split(h - 1)
                if i == 1 and h >= 1:
                    evac_xo(h - 1)
                if h < NX - 1:
                    if i == 1:
                        w_split_act(act, WQ0 + 2 * (h + 1) + 2)
                        evac_xq(2 * (h + 1))
                    if i == 3:
                        w_split_act(act, WQ0 + 2 * (h + 1) + 3)
                        evac_xq(2 * (h + 1) + 1)
            for c in range(XO0 + 2, UP0 + 1):
                w_split_act(act, c)
            norm_stats_act(act, S_H2)
            norm_guess_act(act, S_H2)
            norm_apply_act(act, S_H2)
            w_split_act(act, UP0 + 1)
            norm_hi_act(act, S_H2)

            def gate_scale(j):
                act.wait_ge(w_used, UP0 + 2 * j + 1)
                if j >= 2:
                    act.wait_ge(h_ready, j - 1)
                nc.scalar.activation(lg[:, j % 2, :], bank[(2 * j) % 4][:, :], ACT.Identity,
                                     scale=col("cw", 2 * FT + j), bias=col("cb", j)).then_inc(g_scaled, 1)

            def gate_silu(j):
                act.wait_ge(g_conv2, j + 1)
                nc.scalar.activation(pr[:, j % 2, :], lg[:, j % 2, :], ACT.Silu).then_inc(g_silu, 1)

            def hidden_hi(j):
                act.wait_ge(h_ready, j + 1)
                nc.scalar.activation(ff_h[:, j, :], cb[:, j % 2, :], ACT.Copy).then_inc(h_hi, 1)

            for j in range(FT + 2):
                if j < FT:
                    w_split_act(act, UP0 + 2 * j + 2)
                    gate_scale(j)
                if 1 <= j <= FT:
                    gate_silu(j - 1)
                if j >= 2:
                    hidden_hi(j - 2)
                if j < FT:
                    w_split_act(act, UP0 + 2 * j + 3)
            for c in range(DN0 + 2, NCH):
                w_split_act(act, c)
            norm_stats_act(act, S_FIN)
            norm_guess_act(act, S_FIN)
            for i in range(NT):
                act.wait_ge(fin_ready, i + 1)
                act.dma_start(out_t[:, i, :], misc[:, i, :]).then_inc(out_stored, 16)
            act.wait_ge(out_stored, 16 * NT)

        @block.vector
        def _(dve):
            def evac_qk(pair, j):
                dve.wait_ge(proj_hi, 2 * pair + j + 1)
                o, hi, b = qk_l[:, pair % 2, j, :], qk_h[:, pair % 2, j, :].bitcast(F32), PJ[j][:, :]
                if j == 0:
                    nc.vector.scalar_tensor_tensor(out=o, in0=b, scalar=-HD ** -0.5, in1=hi, op0=ALU.mult,
                                                   op1=ALU.subtract).then_inc(proj_lo, 1)
                else:
                    nc.vector.tensor_tensor(o, b, hi, ALU.subtract).then_inc(proj_lo, 1)

            def evac_v(pair):
                dve.wait_ge(v_hi, pair + 1)
                nc.vector.tensor_tensor(v_l[:, pair % 2, :, :].rearrange("p a b -> p (a b)"), PJ[1][:, :],
                                        v_h[:, pair % 2, :, :].rearrange("p a b -> p (a b)").bitcast(F32),
                                        ALU.subtract).then_inc(v_lo, 1)

            dve.wait_ge(vec_turned, 1)
            nc.vector.tensor_copy(vec[:, 0:VROWS], bank[7][:, 0:VROWS]).then_inc(vec_ready, 1)
            norm_stats_dve(dve, S_X)
            norm_newton_dve(dve, S_X)
            norm_apply_dve(dve, S_X)
            dve.wait_ge(vec_ready, 1)
            w_split_dve(dve, 0)
            norm_lo_dve(dve, S_X)
            dve.wait_ge(wf_hi, 1)
            nc.vector.tensor_tensor(wf_l[:, :, :], wf_raw[:, :, :], wf_h[:, :, :].bitcast(F32),
                                    ALU.subtract).then_inc(wf_lo, 1)
            for c in range(1, 3):
                w_split_dve(dve, c)
            evac_qk(0, 0)
            norm_stats_dve(dve, S_MEM)
            norm_newton_dve(dve, S_MEM)
            norm_apply_dve(dve, S_MEM)
            dve.wait_ge(z_turned, 1)
            dve.wait_ge(b_landed, 16)
            dve.wait_ge(f_act, 1)
            nc.vector.tensor_scalar(fz[2], SC[1][0:NH, :], b_col[:, :], 0.0, ALU.add, ALU.min).then_inc(f_dve, 1)
            dve.wait_ge(f_dve, 1)
            dve.wait_ge(f_act, 3)
            nc.vector.tensor_tensor(fz[2], fz[2], fz[0], ALU.subtract).then_inc(f_dve, 1)
            nc.vector.memset(fz[1], 1.0).then_inc(f_dve, 1)
            dve.wait_ge(f_dve, 3)
            nc.vector.tensor_tensor_scan(fz[3], fz[1], fz[2], 0.0, ALU.mult, ALU.add).then_inc(f_dve, 1)

            evac_qk(0, 1)
            norm_lo_dve(dve, S_MEM)
            evac_v(0)
            w_split_dve(dve, 3)
            w_split_dve(dve, 4)

            def logits(n):
                pair, hh, i = unit(n)
                h = 2 * pair + hh
                w = P * (i + 1)
                dve.wait_ge(s_done, n + 1)
                dve.wait_ge(bias_ready, h + 1)
                if n >= 2:
                    dve.wait_ge(p_ready, n - 1)
                if pair >= FOXP:
                    nc.vector.tensor_tensor_reduce(lg[:, n % 2, 0:w], SC[n % 2][:, 0:w],
                                                   cb[:, h % 2, SEQ - w:SEQ], 1.0, FLT_MAX, ALU.add, ALU.min,
                                                   minima[:, n:n + 1]).then_inc(lg_ready, 1)
                    return
                init = FLT_MAX
                if i:
                    nc.vector.tensor_tensor_reduce(lg[:, n % 2, 0:w - P], SC[n % 2][:, 0:w - P],
                                                   cb[:, h % 2, 0:w - P], 1.0, FLT_MAX, ALU.add, ALU.min,
                                                   inv_sums[:, n:n + 1]).then_inc(off_ready, 1)
                    dve.wait_ge(off_ready, (n // NT) * (NT - 1) + i)
                    init = inv_sums[:, n:n + 1]
                nc.vector.tensor_tensor_reduce(lg[:, n % 2, w - P:w], SC[n % 2][:, w - P:w],
                                               cbd[:, h % 2, w - P:w], 1.0, init, ALU.add, ALU.min,
                                               minima[:, n:n + 1]).then_inc(lg_ready, 1)

            def pt_split(n):
                _, _, i = unit(n)
                w = P * (i + 1)
                dve.wait_ge(pt_hi, n + 1)
                nc.vector.tensor_tensor(pt_l[:, n % 2, 0:w], PT[n % 2][:, 0:w],
                                        pt_h[:, n % 2, 0:w].bitcast(F32), ALU.subtract).then_inc(pt_lo, 1)

            def evac_y(pair):
                a = UNITS * pair
                dve.wait_ge(p_ready, a + UNITS)
                if pair < FOXP:
                    dve.wait_ge(lg_ready, a + UNITS)
                nc.vector.reciprocal(inv_sums[:, a:a + UNITS], sums[:, a:a + UNITS]).then_inc(inv_ready, 1)
                dve.wait_ge(inv_ready, pair + 1)
                dve.wait_ge(pv_done, a + UNITS)
                if pair == 0:
                    dve.wait_ge(nrm_act[S_MEM], half_of(S_MEM))
                    dve.wait_ge(nrm_dve[S_MEM], half_of(S_MEM))
                nc.vector.tensor_tensor(
                    tok[:, :, pair * P:(pair + 1) * P].rearrange("p i (h d) -> p i h d", h=2),
                    OB[pair % 2][:, :].rearrange("p (i h d) -> p i h d", i=NT, h=2),
                    inv_sums[:, a:a + UNITS].rearrange("p (h i) -> p i h", h=2).unsqueeze(3)
                    .to_broadcast([P, NT, 2, HD]), ALU.mult).then_inc(y_ready, 1)

            def evac_km(m):
                dve.wait_ge(km_hi, m + 1)
                nc.vector.tensor_tensor(km_l[:, m, :], PJ[m % 2][:, 0:MEM], km_h[:, m, :].bitcast(F32),
                                        ALU.subtract).then_inc(km_lo, 1)

            def evac_vm(h):
                for m in range(MT):
                    dve.wait_ge(vm_hi, MT * h + m + 1)
                    nc.vector.tensor_tensor(vm_l[:, m, h * 512:(h + 1) * 512], PJ[m][:, :],
                                            vm_h[:, m, h * 512:(h + 1) * 512].bitcast(F32),
                                            ALU.subtract).then_inc(vm_lo, 1)

            for n in range(NU + 2):
                pair, u = divmod(n, UNITS)
                if n < NU:
                    logits(n)
                if 1 <= n <= NU:
                    pt_split(n - 1)
                if u == 0 and 1 <= pair < NPAIR:
                    evac_v(pair)
                if pair < NPAIR - 1:
                    if u == 2:
                        evac_qk(pair + 1, 0)
                    if u == 5:
                        evac_qk(pair + 1, 1)
                for c in SPLIT_STEPS.get(n, []):
                    w_split_dve(dve, c)
                if u == 1 and pair >= 1:
                    evac_y(pair - 1)
                for c in KV_STEPS.get(n, []):
                    if c < VM0:
                        evac_km(c - KV0)
                    if c == VM0 + 3:
                        evac_vm(0)
            norm_stats_dve(dve, S_Y)
            norm_newton_dve(dve, S_Y)
            norm_apply_dve(dve, S_Y)
            evac_vm(1)
            w_split_dve(dve, WO0)
            norm_lo_dve(dve, S_Y)

            def add_tiles(s, half):
                if s == 0 and half == 0:
                    dve.wait_ge(x2_landed, 16)
                for i in range(NT):
                    if i < NT - 1:
                        dve.wait_ge(out_done[s], (NT - 1) * half + i + 1)
                    else:
                        dve.wait_ge(w_used, OUT0[s] + (half + 1) * OUT_K[s])
                    t = tok[:, i, half * 512:(half + 1) * 512]
                    nc.vector.tensor_tensor(t, out_bank(s, half, i)[:, :], t, ALU.add).then_inc(added[s], 1)

            def out_splits(s, lo, hi, between):
                for c in range(lo, hi):
                    w_split_dve(dve, c)
                    if c == between:
                        add_tiles(s, 0)

            out_splits(0, WO0 + 1, WQ0 + 1, WO0 + 6)
            add_tiles(0, 1)
            norm_stats_dve(dve, S_H1)
            norm_newton_dve(dve, S_H1)
            norm_apply_dve(dve, S_H1)
            w_split_dve(dve, WQ0 + 1)
            norm_lo_dve(dve, S_H1)

            def evac_xq(t):
                dve.wait_ge(xq_hi, t + 1)
                nc.vector.scalar_tensor_tensor(out=qk_l[:, (t // 2) % 2, t % 2, :], in0=PJ[t % 2][:, :],
                                               scalar=-CROSS_D ** -0.5,
                                               in1=qk_h[:, (t // 2) % 2, t % 2, :].bitcast(F32),
                                               op0=ALU.mult, op1=ALU.subtract).then_inc(xq_lo, 1)

            def xmins(m):
                dve.wait_ge(xs_done, m + 1)
                nc.vector.tensor_reduce(minima[:, m:m + 1], SC[m % 2][:, 0:MEM], AX_X, ALU.min).then_inc(xmin, 1)

            def xnorm(m):
                dve.wait_ge(xp_ready, m + 1)
                nc.vector.reciprocal(inv_sums[:, m:m + 1], sums[:, m:m + 1]).then_inc(xinv, 1)
                dve.wait_ge(xinv, m + 1)
                nc.vector.tensor_scalar(pr[:, m % 2, 0:MEM], pr[:, m % 2, 0:MEM], inv_sums[:, m:m + 1], None,
                                        ALU.mult).then_inc(xp_norm, 1)

            def xpt_split(h):
                for t in range(MT):
                    dve.wait_ge(xpt_hi, MT * h + t + 1)
                    nc.vector.tensor_tensor(pt_l[:, t, :], PT[t][:, :], pt_h[:, t, :].bitcast(F32),
                                            ALU.subtract).then_inc(xpt_lo, 1)

            def evac_xo(h):
                for d in range(2):
                    dve.wait_ge(xo_hi, 2 * h + d + 1)
                    nc.vector.tensor_tensor(ox_l[:, 2 * h + d, :], OB[d][:, :],
                                            ox_h[:, 2 * h + d, :].bitcast(F32), ALU.subtract).then_inc(xo_lo, 1)

            w_split_dve(dve, WQ0 + 2)
            evac_xq(0)
            w_split_dve(dve, WQ0 + 3)
            evac_xq(1)
            for m in range(NX * NT + 2):
                h, i = divmod(m, NT)
                if m < NX * NT:
                    xmins(m)
                    xnorm(m)
                if i == 0 and h >= 1:
                    xpt_split(h - 1)
                if i == 1 and h >= 1:
                    evac_xo(h - 1)
                if h < NX - 1:
                    if i == 1:
                        w_split_dve(dve, WQ0 + 2 * (h + 1) + 2)
                        evac_xq(2 * (h + 1))
                    if i == 3:
                        w_split_dve(dve, WQ0 + 2 * (h + 1) + 3)
                        evac_xq(2 * (h + 1) + 1)
            out_splits(1, XO0 + 2, UP0 + 1, XO0 + 6)
            add_tiles(1, 1)
            norm_stats_dve(dve, S_H2)
            norm_newton_dve(dve, S_H2)
            norm_apply_dve(dve, S_H2)
            w_split_dve(dve, UP0 + 1)
            norm_lo_dve(dve, S_H2)

            def conv(j):
                g, b = lg[:, j % 2, :], bank[(2 * j) % 4]
                dve.wait_ge(g_scaled, j + 1)
                nc.vector.scalar_tensor_tensor(out=g[:, 1:SEQ], in0=b[:, 0:SEQ - 1], scalar=col("cw", FT + j),
                                               in1=g[:, 1:SEQ], op0=ALU.mult, op1=ALU.add).then_inc(g_conv1, 1)
                dve.wait_ge(g_conv1, j + 1)
                nc.vector.scalar_tensor_tensor(out=g[:, 2:SEQ], in0=b[:, 0:SEQ - 2], scalar=col("cw", j),
                                               in1=g[:, 2:SEQ], op0=ALU.mult, op1=ALU.add).then_inc(g_conv2, 1)

            def gated(j):
                dve.wait_ge(g_silu, j + 1)
                dve.wait_ge(w_used, UP0 + 2 * j + 2)
                if j >= 2:
                    dve.wait_ge(h_lo, j - 1)
                nc.vector.tensor_tensor(cb[:, j % 2, :], bank[(2 * j + 1) % 4][:, :], pr[:, j % 2, :],
                                        ALU.mult).then_inc(h_ready, 1)

            def hidden_lo(j):
                dve.wait_ge(h_hi, j + 1)
                nc.vector.tensor_tensor(ff_l[:, j, :], cb[:, j % 2, :], ff_h[:, j, :].bitcast(F32),
                                        ALU.subtract).then_inc(h_lo, 1)

            for j in range(FT + 2):
                if j < FT:
                    w_split_dve(dve, UP0 + 2 * j + 2)
                    conv(j)
                if 1 <= j <= FT:
                    gated(j - 1)
                if j >= 2:
                    hidden_lo(j - 2)
                if j < FT:
                    w_split_dve(dve, UP0 + 2 * j + 3)
            out_splits(2, DN0 + 2, NCH, DN0 + FT // 2 + 2)
            add_tiles(2, 1)
            norm_stats_dve(dve, S_FIN)
            norm_newton_dve(dve, S_FIN)
            dve.wait_ge(gf_landed, 16)
            for i in range(NT):
                nc.vector.scalar_tensor_tensor(out=misc[:, i, :], in0=tok[:, i, :], scalar=rinv[:, S_FIN, i:i + 1],
                                               in1=row[:, :], op0=ALU.mult, op1=ALU.mult).then_inc(fin_ready, 1)

        @block.tensor
        def _(pe):
            def f_triples(c, o, a, w, ks, fresh=None):
                for k in ks:
                    if fresh is not None:
                        pe.wait_ge(fresh, k + 1)
                    wh, wl = w_tile(c, k, P)
                    last = mm3(o, wh, wl, a[0][:, k, 0:w], a[1][:, k, 0:w], k == 0, k == KT - 1)
                if k == KT - 1:
                    last.then_inc(w_used, 1)

            def t_triples(c, outs, a, k0, kn, signal=None):
                for i, o in enumerate(outs):
                    for k in range(2):
                        wh, wl = w_tile(c, k, 512)
                        t = slice(i * P, (i + 1) * P)
                        last = mm3(o[:, :], a[0][:, k0 + k, t], a[1][:, k0 + k, t], wh, wl,
                                   k0 + k == 0, k0 + k == kn - 1)
                    if i == len(outs) - 1:
                        last.then_inc(w_used, 1)
                    elif signal is not None and k0 + 2 == kn:
                        last.then_inc(signal, 1)

            def v_turn(pair):
                pe.wait_ge(v_copied, pair + 1)
                pe.wait_ge(proj_lo, 2 * pair + 2)
                for i in range(NT):
                    last = nc.tensor.transpose(PJ[1][:, i * P:(i + 1) * P], v_raw[:, i * P:(i + 1) * P],
                                               ident[:, :])
                last.then_inc(v_turned, 1)

            acts, mem_acts = (act_h, act_l), (mn_h, mn_l)

            pe.wait_ge(ident_ready, 2)
            pe.wait_ge(vec_landed, 16 * len(VEC))
            nc.tensor.transpose(bank[7][:, 0:VROWS], vec_rows[0:VROWS, :], ident[0:VROWS, 0:VROWS])\
              .then_inc(vec_turned, 1)
            pe.wait_ge(vec_ready, 1)
            norm_turn_pe(pe, S_X)

            pe.wait_ge(w_lo, 1)
            f_triples(0, PJ[0][:, :], acts, SEQ, range(KT), fresh=act_lo[S_X])
            pe.wait_ge(wf_lo, 1)
            for i in range(NT):
                for k in range(KT):
                    t = slice(i * P, (i + 1) * P)
                    last = mm3(SC[0][:, i * NH:(i + 1) * NH], act_h[:, k, t], act_l[:, k, t],
                               wf_h[:, k, :], wf_l[:, k, :], k == 0, k == KT - 1)
            last.then_inc(z_done, 1)
            pe.wait_ge(w_lo, 2)
            f_triples(1, PJ[1][:, :], acts, SEQ, range(KT))
            pe.wait_ge(z_copied, 1)
            for i in range(NT):
                last = nc.tensor.transpose(SC[1][0:NH, i * P:(i + 1) * P], z_tok[:, i, :], ident[:, :])
            last.then_inc(z_turned, 1)
            pe.wait_ge(w_lo, 3)
            pe.wait_ge(proj_lo, 1)
            f_triples(2, PJ[0][:, :], acts, SEQ, range(KT))
            pe.wait_ge(f_dve, 1)
            norm_turn_pe(pe, S_MEM)
            v_turn(0)
            pe.wait_ge(act_lo[S_MEM], KT)

            def scores(n):
                pair, hh, i = unit(n)
                pe.wait_ge(proj_lo, 2 * pair + 2)
                if n >= 2:
                    pe.wait_ge(lg_ready, n - 1)
                r, t, w = slice(hh * HD, (hh + 1) * HD), slice(i * P, (i + 1) * P), P * (i + 1)
                s = pair % 2
                mm3(SC[n % 2][:, 0:w], qk_h[r, s, 0, t], qk_l[r, s, 0, t], qk_h[r, s, 1, 0:w],
                    qk_l[r, s, 1, 0:w], True, True).then_inc(s_done, 1)

            def p_turn(n):
                _, _, i = unit(n)
                pe.wait_ge(p_ready, n + 1)
                if n >= 2:
                    pe.wait_ge(pt_lo, n - 1)
                for k in range(i + 1):
                    last = nc.tensor.transpose(PT[n % 2][:, k * P:(k + 1) * P],
                                               pr[:, n % 2, k * P:(k + 1) * P], ident[:, :])
                last.then_inc(p_turned, 1)

            def pv(n):
                pair, hh, i = unit(n)
                pe.wait_ge(pt_lo, n + 1)
                pe.wait_ge(v_lo, pair + 1)
                if pair >= 2:
                    pe.wait_ge(y_ready, pair - 1)
                c0 = (2 * i + hh) * HD
                for k in range(i + 1):
                    t, d = slice(k * P, (k + 1) * P), slice(hh * HD, (hh + 1) * HD)
                    last = mm3(OB[pair % 2][:, c0:c0 + HD], pt_h[:, n % 2, t], pt_l[:, n % 2, t],
                               v_h[:, pair % 2, k, d], v_l[:, pair % 2, k, d], k == 0, k == i)
                last.then_inc(pv_done, 1)

            def project(pair, lo, hi):
                for m in range(lo, hi):
                    j, k = divmod(m, KT)
                    if k == 0:
                        pe.wait_ge(w_lo, 3 * pair + j + 1)
                        if j == 0:
                            pe.wait_ge(v_copied, pair)
                        if j == 1:
                            pe.wait_ge(v_lo, pair)
                        if j == 2:
                            pe.wait_ge(proj_lo, 2 * pair + 1)
                    f_triples(3 * pair + j, PJ[j % 2][:, :], acts, SEQ, [k])

            def mem_chunk(c):
                pe.wait_ge(w_lo, c + 1)
                if c < VM0:
                    m = c - KV0
                    if m == 0:
                        pe.wait_ge(v_copied, NPAIR)
                    if m == 1:
                        pe.wait_ge(v_lo, NPAIR)
                    if m >= 2:
                        pe.wait_ge(km_lo, m - 1)
                    f_triples(c, PJ[m % 2][:, 0:MEM], mem_acts, MEM, range(KT))
                else:
                    h, k = divmod(c - VM0, KT // 2)
                    if k == 0:
                        pe.wait_ge(km_lo, KT)
                        if h:
                            pe.wait_ge(vm_lo, MT * h)
                    t_triples(c, PJ, mem_acts, 2 * k, KT)

            for n in range(NU + 2):
                pair, u = divmod(n, UNITS)
                lo = PER_STEP * u
                todo = KV_STEPS.get(n, [])
                if n < NU:
                    scores(n)
                if u == 0 and 1 <= pair < NPAIR:
                    v_turn(pair)
                if pair < NPAIR - 1:
                    project(pair + 1, lo, lo + 2)
                if len(todo) > 1:
                    mem_chunk(todo[0])
                if 1 <= n <= NU:
                    p_turn(n - 1)
                if pair < NPAIR - 1:
                    project(pair + 1, lo + 2, lo + PER_STEP)
                if todo:
                    mem_chunk(todo[-1])
                if n >= 2:
                    pv(n - 2)
            for c in KV_TAIL:
                mem_chunk(c)

            def token_out(s, a, ready, per_chunk):
                for c in range(2 * OUT_K[s]):
                    half, k = divmod(c, OUT_K[s])
                    pe.wait_ge(w_lo, OUT0[s] + c + 1)
                    if half == 0 and per_chunk:
                        pe.wait_ge(ready, 2 * k + 2)
                    t_triples(OUT0[s] + c, [out_bank(s, half, i) for i in range(NT)], a, 2 * k,
                              2 * OUT_K[s], out_done[s])

            norm_turn_pe(pe, S_Y)
            pe.wait_ge(vm_lo, MT * H2)
            pe.wait_ge(act_lo[S_Y], KT)
            token_out(0, acts, None, False)

            norm_turn_pe(pe, S_H1)
            pe.wait_ge(w_lo, WQ0 + 1)
            f_triples(WQ0, PJ[0][:, :], acts, SEQ, range(KT), fresh=act_lo[S_H1])
            pe.wait_ge(w_lo, WQ0 + 2)
            f_triples(WQ0 + 1, PJ[1][:, :], acts, SEQ, range(KT))

            def xscores(m):
                h, i = divmod(m, NT)
                pe.wait_ge(xq_lo, 2 * h + 2)
                if m >= 2:
                    pe.wait_ge(xp_ready, m - 1)
                t = slice(i * P, (i + 1) * P)
                for d in range(2):
                    last = mm3(SC[m % 2][:, 0:MEM], qk_h[:, h % 2, d, t], qk_l[:, h % 2, d, t],
                               km_h[:, 2 * h + d, :], km_l[:, 2 * h + d, :], d == 0, d == 1)
                last.then_inc(xs_done, 1)

            def xp_turn(m):
                h, i = divmod(m, NT)
                pe.wait_ge(xp_norm, m + 1)
                if i == 0 and h >= 1:
                    pe.wait_ge(xpt_lo, MT * h)
                for t in range(MT):
                    last = nc.tensor.transpose(PT[t][:, i * P:(i + 1) * P], pr[:, m % 2, t * P:(t + 1) * P],
                                               ident[:, :])
                last.then_inc(xp_turned, 1)

            def xpv(h):
                pe.wait_ge(xpt_lo, MT * (h + 1))
                if h >= 1:
                    pe.wait_ge(xo_lo, 2 * h)
                for d in range(2):
                    f = slice((2 * h + d) * P, (2 * h + d + 1) * P)
                    for t in range(MT):
                        last = mm3(OB[d][:, :], vm_h[:, t, f], vm_l[:, t, f], pt_h[:, t, :], pt_l[:, t, :],
                                   t == 0, t == MT - 1)
                    last.then_inc(xo_done, 1)

            for m in range(NX * NT + 2):
                h, i = divmod(m, NT)
                t = 2 * (h + 1) + i // 2
                ks = range((i % 2) * KT // 2, (i % 2 + 1) * KT // 2)
                if m < NX * NT:
                    xscores(m)
                if h < NX - 1:
                    if i % 2 == 0:
                        pe.wait_ge(w_lo, WQ0 + t + 1)
                        pe.wait_ge(xq_lo, t - 1)
                    f_triples(WQ0 + t, PJ[t % 2][:, :], acts, SEQ, ks)
                if 1 <= m <= NX * NT:
                    xp_turn(m - 1)
                if i == 1 and h >= 1:
                    xpv(h - 1)
            token_out(1, (ox_h, ox_l), xo_lo, True)

            norm_turn_pe(pe, S_H2)
            for j in range(FT):
                for g in range(2):
                    pe.wait_ge(w_lo, UP0 + 2 * j + g + 1)
                    if j >= 2:
                        pe.wait_ge(h_ready if g else g_conv2, j - 1)
                    f_triples(UP0 + 2 * j + g, bank[(2 * j + g) % 4][:, :], acts, SEQ, range(KT),
                              fresh=act_lo[S_H2] if j == 0 and g == 0 else None)
            token_out(2, (ff_h, ff_l), h_lo, True)


_INS = ["x", "mem", "g_mix", "w_in", "b_forget", "g_fox", "g_moba", "w_out", "g_cross", "g_mem", "w_q_mem",
        "w_kv_mem", "w_o_mem", "g_ffn", "w_up", "conv_w", "conv_b", "w_down", "g_final"]


def kernel(**inputs):
    import numpy as _np
    import concourse.bacc as _bacc
    from concourse.bass_utils import run_bass_kernel_spmd as _run

    nc = _bacc.Bacc("TRN2", target_bir_lowering=False, num_devices=1)
    arrays, args = {}, []
    for name in _INS:
        a = _np.ascontiguousarray(inputs[name])
        arrays[f"in_{name}"] = a
        args.append(nc.dram_tensor(f"in_{name}", a.shape, mybir.dt.from_np(a.dtype), kind="ExternalInput").ap())
    args.append(nc.dram_tensor("out_0", inputs["x"].shape, F32, kind="ExternalOutput").ap())
    hymba_layer(nc, *args)
    r = _run(nc, [arrays], core_ids=[0])
    return r.results[0]["out_0"]
```

```python
from contextlib import ExitStack

import concourse.bass as bass
from concourse import mybir

F32 = mybir.dt.float32
F32R = mybir.dt.float32r
I32 = mybir.dt.int32
ALU = mybir.AluOpType
ACT = mybir.ActivationFunctionType
AX_X = mybir.AxisListType.X

P = 128
EPS = 1e-6
BIG = 1.0e30
FLT_MAX = 3.0e38


def hymba_layer(nc, x, mem, g_mix, w_in, b_forget, g_fox, g_moba, w_out, g_cross, g_mem, w_q_mem,
                w_kv_mem, w_o_mem, g_ffn, w_up, conv_w, conv_b, w_down, g_final, out):
    SEQ, D = x.shape[1], x.shape[2]
    MEM = mem.shape[1]
    NH = b_forget.shape[1]
    GW = g_fox.shape[1]
    HD = GW // NH
    FF = conv_b.shape[1]
    TAPS = conv_w.shape[1]
    NT = SEQ // P
    MT = MEM // P
    KT = D // P
    FT = FF // P
    CROSS_D = 256
    NX = D // CROSS_D
    NPAIR = 2 * GW // P
    FOXP = GW // P
    UNITS = 2 * NT
    H2 = D // 512
    assert (SEQ, D, MEM, HD, NH, NT, KT, H2) == (512, 1024, 256, 64, 8, 4, 8, 2) and TAPS == 3

    x_t = x[0].rearrange("(i p) d -> p i d", p=P)
    mem_t = mem[0].rearrange("(i p) d -> p i d", p=P)
    out_t = out[0].rearrange("(i p) d -> p i d", p=P)
    w_in, w_out, w_q_mem, w_kv_mem, w_o_mem = w_in[0], w_out[0], w_q_mem[0], w_kv_mem[0], w_o_mem[0]
    w_up, w_down = w_up[0], w_down[0]

    CH = 1024

    def f_chunk(w, col):
        return w[:, col:col + P].rearrange("(k p) n -> p k n", p=P)

    def t_chunk(w, k, half):
        return w[k * P:(k + 2) * P, half * 512:half * 512 + 512].rearrange("(k p) n -> p k n", p=P)

    MOBA0 = 3 * GW + NH
    chunks = []
    for pair in range(NPAIR):
        base = pair * P if pair < FOXP else MOBA0 + (pair - FOXP) * P
        chunks += [f_chunk(w_in, base + j * GW) for j in range(3)]
    KV0 = len(chunks)

    def km_pos(m):
        return KV0 + 2 * m

    def vm_pos(v):
        return KV0 + 2 * v + 1

    mem_chunks = {km_pos(m): ("k", m) for m in range(KT)}
    mem_chunks.update({vm_pos(v): ("v", v) for v in range(KT)})
    for c in range(KV0, KV0 + 2 * KT):
        kind, m = mem_chunks[c]
        chunks += [f_chunk(w_kv_mem, m * P) if kind == "k" else
                   t_chunk(w_kv_mem[:, D:], 2 * (m % (KT // 2)), m // (KT // 2))]
    WO0 = len(chunks)
    chunks += [t_chunk(w_out, k, h) for h in range(H2) for k in range(0, KT, 2)]
    WQ0 = len(chunks)
    chunks += [f_chunk(w_q_mem, m * P) for m in range(KT)]
    XO0 = len(chunks)
    chunks += [t_chunk(w_o_mem, k, h) for h in range(H2) for k in range(0, KT, 2)]
    UP0 = len(chunks)
    for j in range(FT):
        chunks += [f_chunk(w_up, j * P), f_chunk(w_up, FF + j * P)]
    DN0 = len(chunks)
    chunks += [t_chunk(w_down, k, h) for h in range(H2) for k in range(0, FT, 2)]
    NCH = len(chunks)
    RING = 3

    c_dram = nc.dram_tensor("c_scratch", (NH, SEQ), F32, kind="Internal").ap()

    with ExitStack() as ctx:
        def sb(name, shape, dt=F32):
            return ctx.enter_context(nc.sbuf_tensor(name, shape, dt))

        def sem(name):
            return ctx.enter_context(nc.semaphore(name))

        bank = [ctx.enter_context(nc.psum_tensor(f"bank{b}", [P, 512], F32)) for b in range(8)]
        PJ, SC, PT, OB = bank[0:2], bank[2:4], bank[4:6], bank[6:8]
        YB, VB = bank[6], bank[7]

        tok = sb("tok", [P, NT, D])
        misc = sb("misc", [P, NT, D])
        act_h = sb("act_h", [P, KT, SEQ], F32R)
        act_l = sb("act_l", [P, KT, SEQ], F32R)
        w_raw = sb("w_raw", [P, RING, CH])
        w_h = sb("w_h", [P, RING, CH], F32R)
        w_l = sb("w_l", [P, RING, CH], F32R)
        big = sb("big", [P, 2 * FT * SEQ], F32R)
        row = sb("row", [P, D])
        v_raw = row[:, 0:SEQ]
        dist = row[:, SEQ:2 * SEQ]
        fmask = sb("fmask", [P, P])
        ident = sb("ident", [P, P])
        ones = sb("ones", [P, 1])
        r_row = sb("r_row", [P, SEQ])
        scaled = sb("scaled", [P, SEQ])
        y_sq = sb("y_sq", [P, SEQ])
        y_acc = sb("y_acc", [P, 2, SEQ])
        vec = sb("vec", [P, P])
        wf_raw = sb("wf_raw", [P, KT, NH])
        wf_h = sb("wf_h", [P, KT, NH], F32R)
        wf_l = sb("wf_l", [P, KT, NH], F32R)
        b_col = sb("b_col", [NH, 1])
        minima = sb("minima", [P, NPAIR * UNITS])
        sums = sb("sums", [P, NPAIR * UNITS])
        inv_sums = sb("inv_sums", [P, NPAIR * UNITS])
        NSTAGE = 6
        ss = sb("ss", [P, NSTAGE, 8])
        s_sum = sb("s_sum", [P, NSTAGE, 8])
        ms = sb("ms", [P, NSTAGE, 8])
        seed = sb("seed", [P, NSTAGE, 8], I32)
        NEWTON = 3
        rs = sb("rs", [P, NSTAGE, NEWTON + 1, 8])
        t_rr = sb("t_rr", [P, NSTAGE, 8])
        t_ms = sb("t_ms", [P, NSTAGE, 8])
        past_min = sb("past_min", [P, NPAIR * UNITS])
        rneg = sb("rneg", [P, NT])
        xbias = sb("xbias", [P, NX * NT])

        def part(lo, shape):
            n = 1
            for s in shape:
                n *= s
            v = big[:, lo:lo + n]
            if len(shape) == 2:
                v = v.rearrange("p (a b) -> p a b", a=shape[0])
            if len(shape) == 3:
                v = v.rearrange("p (a b c) -> p a b c", a=shape[0], b=shape[1])
            return v

        qk_h, qk_l = part(0, [2, 2, SEQ]), part(2048, [2, 2, SEQ])
        km_h, km_l = part(4096, [KT, MEM]), part(6144, [KT, MEM])
        vm_h, vm_l = part(8192, [MT, D]), part(10240, [MT, D])
        v_h, v_l = part(12288, [2, NT, P]), part(13312, [2, NT, P])
        mn_h, mn_l = part(14336, [KT, MEM]), part(16384, [KT, MEM])
        ox_h, ox_l = part(12288, [KT, SEQ]), part(16384, [KT, SEQ])
        pt_h, pt_l = part(18432, [NT, SEQ]), part(20480, [NT, SEQ])
        xp_h, xp_l = part(20480, [MT, SEQ]), part(21504, [MT, SEQ])
        ff_h, ff_l = part(0, [FT, SEQ]), part(FT * SEQ, [FT, SEQ])

        flat = misc[:, :, :].rearrange("p a b -> p (a b)")
        lg = flat[:, 0:1024].rearrange("p (a b) -> p a b", a=2)
        pr = flat[:, 1024:2048].rearrange("p (a b) -> p a b", a=2)
        cb = flat[:, 2048:3072].rearrange("p (a b) -> p a b", a=2)
        cbd = flat[:, 3072:4096].rearrange("p (a b) -> p a b", a=2)
        gr, gc, gs, ur = (flat[:, 1024 * j:1024 * (j + 1)].rearrange("p (a b) -> p a b", a=2) for j in range(4))
        vec_rows = y_acc[:, 1, 0:P]
        y_fm = tok[:, :, :].rearrange("p a b -> p (a b)").rearrange("p (k t) -> p k t", k=KT)
        fz = [flat[0:NH, 2048 + 512 * j:2560 + 512 * j] for j in range(4)]

        VEC = {}
        at = 0
        for name, src in (("mix", g_mix), ("mem", g_mem), ("fox", g_fox), ("moba", g_moba),
                          ("cross", g_cross), ("ffn", g_ffn), ("cw", conv_w), ("cb", conv_b)):
            n = 1
            for s in src.shape:
                n *= s
            VEC[name] = (at, n // P, src)
            at += n // P
        assert at <= P
        VROWS = at

        def col(name, k):
            return vec[:, VEC[name][0] + k:VEC[name][0] + k + 1]

        w_landed = [sem(f"w_landed{s}") for s in range(RING)]
        w_hi, w_lo, w_used = sem("w_hi"), sem("w_lo"), sem("w_used")
        x_landed = [sem(f"x_landed{i}") for i in range(NT)]
        mem_landed, mix_landed, vec_landed = sem("mem_landed"), sem("mix_landed"), sem("vec_landed")
        wf_landed, b_landed = sem("wf_landed"), sem("b_landed")
        c_stored = sem("c_stored")
        c_landed = [sem(f"c_landed{s}") for s in range(2)]
        x2_landed, gf_landed, out_stored = sem("x2_landed"), sem("gf_landed"), sem("out_stored")
        ident_ready, masks_ready = sem("ident_ready"), sem("masks_ready")
        vec_turned, vec_ready = sem("vec_turned"), sem("vec_ready")
        sq_act = [sem(f"sq_act{s}") for s in range(NSTAGE)]
        sq_dve = [sem(f"sq_dve{s}") for s in range(NSTAGE)]
        rms = [sem(f"rms{s}") for s in range(NSTAGE)]
        nrm_act, nrm_dve = sem("nrm_act"), sem("nrm_dve")
        turned = [sem(f"turned{s}") for s in range(NSTAGE)]
        act_hi = [sem(f"act_hi{s}") for s in range(NSTAGE)]
        act_lo = [sem(f"act_lo{s}") for s in range(NSTAGE)]
        wf_hi, wf_lo = sem("wf_hi"), sem("wf_lo")
        r_spread, r_turned, r_row_ready = sem("r_spread"), sem("r_turned"), sem("r_row_ready")
        z_done, z_scaled = sem("z_done"), sem("z_scaled")
        f_act, f_dve = sem("f_act"), sem("f_dve")
        proj_scaled, proj_hi, proj_lo = sem("proj_scaled"), sem("proj_hi"), sem("proj_lo")
        v_scaled, v_turned, v_hi, v_lo = sem("v_scaled"), sem("v_turned"), sem("v_hi"), sem("v_lo")
        s_done, bias_ready, lg_ready = sem("s_done"), sem("bias_ready"), sem("lg_ready")
        off_ready = sem("off_ready")
        p_ready, p_turned = sem("p_ready"), sem("p_turned")
        pt_hi, pt_lo, pv_done = sem("pt_hi"), sem("pt_lo"), sem("pv_done")
        inv_ready, p_norm, y_ready = sem("inv_ready"), sem("p_norm"), sem("y_ready")
        y_squared, y_summed, y_stat = sem("y_squared"), sem("y_summed"), sem("y_stat")
        km_hi, km_lo = sem("km_hi"), sem("km_lo")
        vm_hi, vm_lo = sem("vm_hi"), sem("vm_lo")
        out_done = [sem(f"out_done{s}") for s in range(3)]
        added = [sem(f"added{s}") for s in range(3)]
        xq_hi, xq_lo = sem("xq_hi"), sem("xq_lo")
        xs_done, xmin, xb_ready, xp_ready = sem("xs_done"), sem("xmin"), sem("xb_ready"), sem("xp_ready")
        xinv, xp_norm, xp_turned = sem("xinv"), sem("xp_norm"), sem("xp_turned")
        xpt_hi, xpt_lo = sem("xpt_hi"), sem("xpt_lo")
        xo_done, xo_hi, xo_lo = sem("xo_done"), sem("xo_hi"), sem("xo_lo")
        g_normed, u_normed, g_scaled, g_conv1, g_conv2 = sem("g_normed"), sem("u_normed"), sem("g_scaled"), sem("g_conv1"), sem("g_conv2")
        g_silu, h_ready, h_hi, h_lo = sem("g_silu"), sem("h_ready"), sem("h_hi"), sem("h_lo")
        gained, fin_act, fin_dve = sem("gained"), sem("fin_act"), sem("fin_dve")

        S_X, S_MEM, S_Y, S_H1, S_H2, S_FIN = range(NSTAGE)
        TILES = {S_X: NT, S_MEM: MT, S_H1: NT, S_H2: NT}
        SRC = {S_X: tok, S_MEM: misc, S_H1: tok, S_H2: tok}

        def gain(s, k):
            if s == S_Y:
                return col("fox", k) if k < FOXP else col("moba", k - FOXP)
            return col({S_X: "mix", S_MEM: "mem", S_H1: "cross", S_H2: "ffn"}[s], k)

        def dst(s, k):
            return (mn_h[:, k, :], mn_l[:, k, :]) if s == S_MEM else (act_h[:, k, :], act_l[:, k, :])

        def turn_bank(s, k):
            if s == S_MEM:
                return bank[2 + k % 4]
            return bank[k]

        def src_ready(eng, s, e):
            if s == S_X:
                eng.wait_ge(x_landed[e], 16)
            else:
                eng.wait_ge(mem_landed, 16)

        def row_stats_act(act, s):
            for e in range(TILES[s] // 2):
                src_ready(act, s, e)
                nc.scalar.activation(misc[:, e, :], tok[:, e, :], ACT.Square,
                                     accum_out=ss[:, s, e:e + 1]).then_inc(sq_act[s], 1)

        def row_stats_dve(dve, s):
            for e in range(TILES[s] // 2, TILES[s]):
                src_ready(dve, s, e)
                nc.vector.tensor_tensor_reduce(misc[:, e, :], tok[:, e, :], tok[:, e, :], 1.0, 0.0,
                                               ALU.mult, ALU.add, ss[:, s, e:e + 1]).then_inc(sq_dve[s], 1)

        def half_stats_act(act, s, half):
            for i in range(NT):
                e = NT * half + i
                act.wait_ge(added[s - S_H1], ADDS[s - S_H1] // H2 * (half + 1) - NT + i + 1)
                o = out_bank(2, half, i)[:, :] if s == S_FIN else misc[:, i, half * 512:(half + 1) * 512]
                nc.scalar.activation(o, tok[:, i, half * 512:(half + 1) * 512], ACT.Square,
                                     accum_out=ss[:, s, e:e + 1]).then_inc(sq_act[s], 1)

        def inv_rms_dve(dve, s, sums_in, n, width):
            m = ms[:, s, 0:n]
            nc.vector.tensor_scalar(m, sums_in, 1.0 / width, EPS, ALU.mult, ALU.add).then_inc(rms[s], 1)
            dve.wait_ge(rms[s], 1)
            nc.vector.tensor_scalar(seed[:, s, 0:n], m.bitcast(I32), 1, None, ALU.logical_shift_right)\
              .then_inc(rms[s], 1)
            dve.wait_ge(rms[s], 2)
            nc.vector.tensor_scalar(rs[:, s, 0, 0:n].bitcast(I32), seed[:, s, 0:n], -1.0, float(0x5f3759df),
                                    ALU.mult, ALU.add).then_inc(rms[s], 1)
            for t in range(NEWTON):
                r = rs[:, s, t, 0:n]
                dve.wait_ge(rms[s], 3 * t + 3)
                nc.vector.tensor_tensor(t_rr[:, s, 0:n], r, r, ALU.mult).then_inc(rms[s], 1)
                dve.wait_ge(rms[s], 3 * t + 4)
                nc.vector.scalar_tensor_tensor(out=t_ms[:, s, 0:n], in0=t_rr[:, s, 0:n], scalar=-0.5, in1=m,
                                               op0=ALU.mult, op1=ALU.mult).then_inc(rms[s], 1)
                dve.wait_ge(rms[s], 3 * t + 5)
                nc.vector.scalar_tensor_tensor(out=rs[:, s, t + 1, 0:n], in0=t_ms[:, s, 0:n], scalar=1.5,
                                               in1=r, op0=ALU.add, op1=ALU.mult).then_inc(rms[s], 1)
            dve.wait_ge(rms[s], RMS_DONE)

        RMS_DONE = 3 + 3 * NEWTON

        def inv(s, e):
            return rs[:, s, NEWTON, e:e + 1]

        def halves_dve(dve, s):
            dve.wait_ge(sq_act[s], H2 * NT)
            nc.vector.tensor_tensor(s_sum[:, s, 0:NT], ss[:, s, 0:NT], ss[:, s, NT:2 * NT],
                                    ALU.add).then_inc(sq_dve[s], 1)
            dve.wait_ge(sq_dve[s], 1)
            inv_rms_dve(dve, s, s_sum[:, s, 0:NT], NT, D)

        def turn_pe(pe, s, ks):
            for k in ks:
                if k >= 4 and s == S_MEM:
                    pe.wait_ge(act_lo[s], k - 3)
                for i in range(TILES[s]):
                    last = nc.tensor.transpose(turn_bank(s, k)[:, i * P:(i + 1) * P],
                                               SRC[s][:, i, k * P:(k + 1) * P], ident[:, :])
                last.then_inc(turned[s], 1)

        def turn_hi_act(act, s, ks):
            w = TILES[s] * P
            for k in ks:
                act.wait_ge(turned[s], k + 1)
                nc.scalar.activation(dst(s, k)[0], turn_bank(s, k)[:, 0:w], ACT.Copy,
                                     scale=gain(s, k)).then_inc(act_hi[s], 1)

        def turn_lo_dve(dve, s, ks):
            w = TILES[s] * P
            for k in ks:
                dve.wait_ge(act_hi[s], k + 1)
                nc.vector.scalar_tensor_tensor(out=dst(s, k)[1], in0=turn_bank(s, k)[:, 0:w], scalar=gain(s, k),
                                               in1=dst(s, k)[0].bitcast(F32), op0=ALU.mult,
                                               op1=ALU.subtract).then_inc(act_lo[s], 1)

        def spread_r_dve(dve, s, scratch):
            nc.vector.tensor_copy(scratch.rearrange("p (i j) -> p i j", i=NT),
                                  rs[:, s, NEWTON, 0:NT].unsqueeze(2).to_broadcast([P, NT, P]))\
              .then_inc(r_spread, 1)

        def turn_r_pe(pe, count, o, scratch):
            pe.wait_ge(r_spread, count)
            for i in range(NT):
                last = nc.tensor.transpose(o[:, i * P:(i + 1) * P], scratch[:, i * P:(i + 1) * P],
                                           ident[:, :])
            last.then_inc(r_turned, 1)

        def copy_r_act(act, count, o):
            act.wait_ge(r_turned, count)
            nc.scalar.activation(r_row[:, :], o[:, :], ACT.Copy).then_inc(r_row_ready, 1)

        def w_split_act(act, c):
            act.wait_ge(w_landed[c % RING], 16 * (c // RING + 1))
            if c >= RING:
                act.wait_ge(w_used, c - RING + 1)
            nc.scalar.activation(w_h[:, c % RING, :], w_raw[:, c % RING, :], ACT.Copy).then_inc(w_hi, 1)

        def w_split_dve(dve, c):
            dve.wait_ge(w_hi, c + 1)
            nc.vector.tensor_tensor(w_l[:, c % RING, :], w_raw[:, c % RING, :],
                                    w_h[:, c % RING, :].bitcast(F32), ALU.subtract).then_inc(w_lo, 1)

        def mm3(o, sh, sl, mh, ml, start, stop):
            nc.tensor.matmul(o, sl, mh, start=start, stop=False)
            nc.tensor.matmul(o, sh, ml, start=False, stop=False)
            return nc.tensor.matmul(o, sh, mh, start=False, stop=stop)

        OUT0, OUT_K = (WO0, XO0, DN0), (KT // 2, KT // 2, FT // 2)

        ADDS = (2 * H2 * NT, H2 * NT, H2 * NT)

        def out_bank(s, half, i):
            return bank[4 * half + i] if s < 2 else bank[4 * (1 - half) + i]

        def w_tile(c, k, w):
            return (w_h[:, c % RING, k * w:(k + 1) * w], w_l[:, c % RING, k * w:(k + 1) * w])

        PER_STEP = 3 * KT // UNITS

        def unit(n):
            pair, u = divmod(n, UNITS)
            return pair, u // NT, u % NT

        NU = NPAIR * UNITS

        SPLIT_STEPS = {}
        for pair in range(NPAIR - 1):
            SPLIT_STEPS[pair * UNITS + 1] = 3 * (pair + 1) + 2
            SPLIT_STEPS[pair * UNITS + 4] = 3 * (pair + 2)
            SPLIT_STEPS[pair * UNITS + 7] = 3 * (pair + 2) + 1

        LAST = NU - UNITS

        def first_chunk(n):
            return KV0 + 2 * (n - LAST)

        def km_bank(m):
            return VB[:, 0:MEM]

        def mix_bank(group, i):
            return bank[4 * group + (i + 2) % NT]

        block = ctx.enter_context(nc.Block())

        @block.sync
        def _(sp):
            for i in range(NT):
                sp.dma_start(tok[:, i, :], x_t[:, i, :]).then_inc(x_landed[i], 16)
            for c in range(NCH):
                if c == RING:
                    sp.dma_start(wf_raw[:, :, :], w_in[:, 3 * GW:3 * GW + NH].rearrange("(k p) n -> p k n", p=P))\
                      .then_inc(wf_landed, 16)
                    sp.dma_start(b_col[:, :], b_forget.rearrange("a n -> n a")).then_inc(b_landed, 16)
                    for name, (r, n, src) in VEC.items():
                        rows = src.rearrange("a (k p) -> (a k) p", p=P) if len(src.shape) == 2 else \
                            src.rearrange("a b (k p) -> (a b k) p", p=P)
                        if name != "mix":
                            sp.dma_start(vec_rows[r:r + n, :], rows).then_inc(vec_landed, 16)
                if c >= RING:
                    sp.wait_ge(w_lo, c - RING + 1)
                v = w_raw[:, c % RING, :].rearrange("p (k n) -> p k n", k=chunks[c].shape[1])
                sp.dma_start(v, chunks[c]).then_inc(w_landed[c % RING], 16)

        @block.gpsimd
        def _(pool):
            nc.gpsimd.memset(ident[:, :], 0.0).then_inc(ident_ready, 1)
            pool.wait_ge(ident_ready, 1)
            nc.gpsimd.affine_select(out=ident[:, :], in_=ident[:, :], compare_op=ALU.not_equal, fill=1.0,
                                    base=0, pattern=[[-1, P]], channel_multiplier=1).then_inc(ident_ready, 1)
            nc.gpsimd.iota(dist[:, :], pattern=[[-1, SEQ]], base=SEQ - P, channel_multiplier=1,
                           allow_small_or_imprecise_dtypes=True).then_inc(masks_ready, 1)
            nc.gpsimd.memset(fmask[:, :], 0.0).then_inc(masks_ready, 1)
            pool.wait_ge(masks_ready, 2)
            nc.gpsimd.affine_select(out=dist[:, :], in_=dist[:, :], compare_op=ALU.is_ge, fill=BIG,
                                    base=SEQ - P, pattern=[[-1, SEQ]], channel_multiplier=1).then_inc(masks_ready, 1)
            nc.gpsimd.affine_select(out=fmask[:, :], in_=fmask[:, :], compare_op=ALU.is_ge, fill=BIG,
                                    base=0, pattern=[[-1, P]], channel_multiplier=1).then_inc(masks_ready, 1)
            nc.gpsimd.memset(ones[:, :], 1.0).then_inc(masks_ready, 1)
            pool.wait_ge(turned[S_X], KT)
            pool.wait_ge(sq_act[S_X], NT // 2)
            pool.wait_ge(sq_dve[S_X], NT // 2)
            pool.dma_start(tok[:, 0:MT, :], mem_t).then_inc(mem_landed, 16)
            pool.wait_ge(f_dve, 4)
            pool.dma_start(c_dram, fz[3]).then_inc(c_stored, 16)
            pool.wait_ge(c_stored, 16)

            def bias(h):
                if h >= 2:
                    pool.wait_ge(lg_ready, NT * (h - 1))
                if h < NH:
                    pool.dma_start(cb[:, h % 2, :], c_dram[h, :].partition_broadcast(P))\
                        .then_inc(c_landed[h % 2], 16)
                    pool.wait_ge(c_landed[h % 2], 16 * (h // 2 + 1))
                    nc.gpsimd.tensor_tensor(cbd[:, h % 2, :].rearrange("p (i j) -> p i j", j=P),
                                            cb[:, h % 2, :].rearrange("p (i j) -> p i j", j=P),
                                            fmask[:, :].unsqueeze(1).to_broadcast([P, NT, P]),
                                            ALU.add).then_inc(bias_ready, 1)
                else:
                    nc.gpsimd.tensor_scalar(cb[:, h % 2, :], dist[:, :], 2.0 ** (-8.0 * (h - NH + 1) / NH), 0.0,
                                            ALU.mult, ALU.add).then_inc(bias_ready, 1)

            def sum_squares(pair):
                pool.wait_ge(y_ready, 2 * (pair + 1))
                first, g = pair % FOXP == 0, pair // FOXP
                if not first and pair % FOXP >= 2:
                    pool.wait_ge(y_summed, pair - 1 - g)
                o = y_acc[:, g, :] if first else y_sq[:, :]
                nc.gpsimd.tensor_tensor(o, y_fm[:, pair, :], y_fm[:, pair, :], ALU.mult)\
                  .then_inc(y_squared, 1)
                if first:
                    return
                pool.wait_ge(y_squared, pair + 1)
                nc.gpsimd.tensor_tensor(y_acc[:, g, :], y_acc[:, g, :], y_sq[:, :], ALU.add)\
                  .then_inc(y_summed, 1)

            pool.wait_ge(masks_ready, 5)
            bias(0)
            bias(1)
            for pair in range(NPAIR):
                if pair < NPAIR - 1:
                    bias(2 * pair + 2)
                    bias(2 * pair + 3)
                sum_squares(pair)
            pool.wait_ge(act_lo[S_Y], KT)
            pool.wait_ge(y_squared, NPAIR)
            pool.dma_start(tok[:, :, :], x_t).then_inc(x2_landed, 16)
            pool.wait_ge(v_turned, NPAIR)
            pool.wait_ge(bias_ready, 2 * NH)
            pool.dma_start(row[:, :], g_final.partition_broadcast(P)).then_inc(gf_landed, 16)

        @block.scalar
        def _(act):
            act.dma_start(vec_rows[0:KT, :], g_mix.rearrange("a (k p) -> (a k) p", p=P)).then_inc(mix_landed, 16)

            def proj_hi_part(pair, j):
                act.wait_ge(proj_scaled, 2 * pair + j + 1)
                if pair >= 2:
                    act.wait_ge(s_done, UNITS * (pair - 1))
                nc.scalar.activation(qk_h[:, pair % 2, j, :], scaled[:, :], ACT.Copy,
                                     scale=-HD ** -0.5 if j == 0 else 1.0).then_inc(proj_hi, 1)

            def v_hi_part(pair):
                act.wait_ge(v_turned, pair + 1)
                if pair >= 2:
                    act.wait_ge(pv_done, 2 * (pair - 1))
                nc.scalar.activation(v_h[:, pair % 2, :, :].rearrange("p a b -> p (a b)"), PJ[1][:, :],
                                     ACT.Copy).then_inc(v_hi, 1)

            row_stats_act(act, S_X)
            act.wait_ge(vec_ready, 1)
            turn_hi_act(act, S_X, range(1))
            w_split_act(act, 0)
            turn_hi_act(act, S_X, range(1, KT))
            act.wait_ge(wf_landed, 16)
            nc.scalar.activation(wf_h[:, :, :], wf_raw[:, :, :], ACT.Copy).then_inc(wf_hi, 1)
            w_split_act(act, 1)
            copy_r_act(act, 1, bank[3])
            w_split_act(act, 2)
            proj_hi_part(0, 0)
            row_stats_act(act, S_MEM)
            act.wait_ge(z_scaled, 1)
            act.wait_ge(b_landed, 16)
            nc.scalar.activation(fz[0], fz[3], ACT.Abs, bias=b_col[:, :]).then_inc(f_act, 1)
            act.wait_ge(f_act, 1)
            nc.scalar.activation(fz[1], fz[0], ACT.Exp, scale=-1.0).then_inc(f_act, 1)
            act.wait_ge(f_act, 2)
            nc.scalar.activation(fz[0], fz[1], ACT.Ln, bias=1.0).then_inc(f_act, 1)
            act.wait_ge(rms[S_MEM], RMS_DONE)
            nc.scalar.activation(misc[:, 0, :], tok[:, 0, :], ACT.Copy, scale=inv(S_MEM, 0)).then_inc(nrm_act, 1)
            proj_hi_part(0, 1)
            act.wait_ge(vec_ready, 2)
            w_split_act(act, 3)
            turn_hi_act(act, S_MEM, range(KT))
            v_hi_part(0)
            w_split_act(act, 4)

            def probs(n):
                _, _, i = unit(n)
                w = P * (i + 1)
                act.wait_ge(lg_ready, n + 1)
                if n >= 2:
                    act.wait_ge(p_turned, n - 1)
                nc.scalar.activation(pr[:, n % 2, 0:w], lg[:, n % 2, 0:w], ACT.Exp, scale=-1.0,
                                     bias=minima[:, n:n + 1], accum_out=sums[:, n:n + 1]).then_inc(p_ready, 1)

            def probs_norm(n):
                _, _, i = unit(n)
                w = P * (i + 1)
                act.wait_ge(inv_ready, n + 1)
                nc.scalar.activation(pr[:, n % 2, 0:w], pr[:, n % 2, 0:w], ACT.Copy,
                                     scale=inv_sums[:, n:n + 1]).then_inc(p_norm, 1)

            def pt_split(n):
                i = n % NT
                act.wait_ge(p_turned, n + 1)
                if i == 0 and n >= NT:
                    act.wait_ge(pv_done, n // NT)
                nc.scalar.activation(pt_h[:, 0:i + 1, i * P:(i + 1) * P],
                                     PT[n % 2][:, 0:(i + 1) * P].rearrange("p (k j) -> p k j", j=P),
                                     ACT.Copy).then_inc(pt_hi, 1)

            def y_copy(h):
                act.wait_ge(pv_done, h + 1)
                if h == 0:
                    act.wait_ge(nrm_act, 1)
                    act.wait_ge(nrm_dve, 1)
                hh = h % 2
                nc.scalar.activation(y_fm[hh * HD:(hh + 1) * HD, h // 2, :], YB[0:HD, :],
                                     ACT.Copy).then_inc(y_ready, 1)

            def y_hi(pair):
                act.wait_ge(y_ready, 2 * (pair + 1))
                if pair == 0:
                    act.wait_ge(w_used, KV0)
                nc.scalar.activation(act_h[:, pair, :], y_fm[:, pair, :], ACT.Copy,
                                     scale=gain(S_Y, pair)).then_inc(act_hi[S_Y], 1)

            def km_hi_part(m):
                act.wait_ge(w_used, km_pos(m) + 1)
                nc.scalar.activation(km_h[:, m, :], km_bank(m), ACT.Copy).then_inc(km_hi, 1)

            def vm_hi_part(h):
                act.wait_ge(w_used, vm_pos(KT // 2 * (h + 1) - 1) + 1)
                for m in range(MT):
                    nc.scalar.activation(vm_h[:, m, h * 512:(h + 1) * 512], PJ[m][:, :], ACT.Copy)\
                       .then_inc(vm_hi, 1)

            for n in range(NU):
                pair, u = divmod(n, UNITS)
                probs(n)
                if n >= LAST:
                    w_split_act(act, first_chunk(n + 1))
                if n >= 1:
                    pt_split(n - 1)
                probs_norm(n)
                if u == 0 and pair >= 1:
                    v_hi_part(pair)
                if pair < NPAIR - 1 and u == 2:
                    proj_hi_part(pair + 1, 0)
                if pair < NPAIR - 1 and u == 5:
                    proj_hi_part(pair + 1, 1)
                if n in SPLIT_STEPS:
                    w_split_act(act, SPLIT_STEPS[n])
                if n >= LAST:
                    km_hi_part(u)
                    w_split_act(act, first_chunk(n + 1) + 1)
                if n == LAST + 3:
                    vm_hi_part(0)
                if n % NT == 1 and n >= NT:
                    y_copy(n // NT - 1)
                if n >= LAST and u >= 1:
                    y_hi(u - 1)
            pt_split(NU - 1)
            vm_hi_part(1)
            w_split_act(act, WO0 + 2)
            y_copy(2 * NPAIR - 1)
            y_hi(NPAIR - 1)
            for c in range(WO0 + 3, WQ0):
                w_split_act(act, c)
            half_stats_act(act, S_H1, 0)
            turn_hi_act(act, S_H1, range(KT // 2))
            w_split_act(act, WQ0)
            half_stats_act(act, S_H1, 1)
            turn_hi_act(act, S_H1, range(KT // 2, KT))
            w_split_act(act, WQ0 + 1)

            def xq_hi_part(t):
                act.wait_ge(w_used, WQ0 + t + 1)
                if t >= 4:
                    act.wait_ge(xs_done, NT * (t // 2 - 1))
                nc.scalar.activation(qk_h[:, (t // 2) % 2, t % 2, :], PJ[t % 2][:, :], ACT.Copy,
                                     scale=-CROSS_D ** -0.5).then_inc(xq_hi, 1)

            def xprobs(m):
                act.wait_ge(xb_ready, m + 2)
                if m >= 2:
                    act.wait_ge(xp_turned, m - 1)
                nc.scalar.activation(pr[:, m % 2, 0:MEM], SC[m % 2][:, 0:MEM], ACT.Exp,
                                     scale=rneg[:, m % NT:m % NT + 1], bias=xbias[:, m:m + 1],
                                     accum_out=sums[:, m:m + 1]).then_inc(xp_ready, 1)

            def xpt_split(h):
                act.wait_ge(xp_turned, NT * (h + 1))
                if h >= 1:
                    act.wait_ge(xo_done, 2 * h)
                for t in range(MT):
                    nc.scalar.activation(xp_h[:, t, :], PT[t][:, :], ACT.Copy).then_inc(xpt_hi, 1)

            def xo_hi_part(h):
                for d in range(2):
                    act.wait_ge(xo_done, 2 * h + d + 1)
                    nc.scalar.activation(ox_h[:, 2 * h + d, :], OB[d][:, :], ACT.Copy).then_inc(xo_hi, 1)

            w_split_act(act, WQ0 + 2)
            xq_hi_part(0)
            w_split_act(act, WQ0 + 3)
            xq_hi_part(1)
            for m in range(NX * NT + 2):
                h, i = divmod(m, NT)
                if m < NX * NT:
                    xprobs(m)
                if i == 0 and h >= 1:
                    xpt_split(h - 1)
                if i == 1 and h >= 1:
                    xo_hi_part(h - 1)
                if h < NX - 1:
                    if i == 1:
                        w_split_act(act, WQ0 + 2 * (h + 1) + 2)
                        xq_hi_part(2 * (h + 1))
                    if i == 3:
                        w_split_act(act, WQ0 + 2 * (h + 1) + 3)
                        xq_hi_part(2 * (h + 1) + 1)
            for c in range(XO0 + 2, UP0):
                w_split_act(act, c)
                if c == XO0 + KT // 2 + 2:
                    half_stats_act(act, S_H2, 0)
            turn_hi_act(act, S_H2, range(KT // 2))
            w_split_act(act, UP0)
            half_stats_act(act, S_H2, 1)
            turn_hi_act(act, S_H2, range(KT // 2, KT))
            w_split_act(act, UP0 + 1)
            copy_r_act(act, 2, bank[7])

            def gate_scale(j):
                act.wait_ge(g_normed, j + 1)
                if j >= 2:
                    act.wait_ge(g_silu, j - 1)
                nc.scalar.activation(gc[:, j % 2, :], gr[:, j % 2, :], ACT.Identity,
                                     scale=col("cw", 2 * FT + j), bias=col("cb", j)).then_inc(g_scaled, 1)

            def gate_silu(j):
                act.wait_ge(g_conv2, j + 1)
                if j >= 2:
                    act.wait_ge(h_ready, j - 1)
                nc.scalar.activation(gs[:, j % 2, :], gc[:, j % 2, :], ACT.Silu).then_inc(g_silu, 1)

            def hidden_hi(j):
                act.wait_ge(h_ready, j + 1)
                nc.scalar.activation(ff_h[:, j, :], ur[:, j % 2, :], ACT.Copy).then_inc(h_hi, 1)

            for j in range(FT + 2):
                if j < FT:
                    w_split_act(act, UP0 + 2 * j + 2)
                    gate_scale(j)
                if 1 <= j <= FT:
                    gate_silu(j - 1)
                if j >= 2:
                    hidden_hi(j - 2)
                if j < FT:
                    w_split_act(act, UP0 + 2 * j + 3)
            for c in range(DN0 + 2, NCH):
                w_split_act(act, c)
                if c == DN0 + FT // 2 + 2:
                    half_stats_act(act, S_FIN, 0)
            half_stats_act(act, S_FIN, 1)
            for i in range(0, NT, 2):
                act.wait_ge(rms[S_FIN], RMS_DONE)
                act.wait_ge(gained, NT * H2)
                nc.scalar.activation(tok[:, i, :], misc[:, i, :], ACT.Copy, scale=inv(S_FIN, i)).then_inc(fin_act, 1)
                act.wait_ge(fin_act, i // 2 + 1)
                act.dma_start(out_t[:, i, :], tok[:, i, :]).then_inc(out_stored, 16)
            for i in range(1, NT, 2):
                act.wait_ge(fin_dve, i // 2 + 1)
                act.dma_start(out_t[:, i, :], tok[:, i, :]).then_inc(out_stored, 16)
            act.wait_ge(out_stored, 16 * NT)

        @block.vector
        def _(dve):
            def proj_scale(pair, j):
                dve.wait_ge(w_used, 3 * pair + j + 1)
                if pair or j:
                    dve.wait_ge(proj_lo, 2 * pair + j)
                nc.vector.tensor_tensor(scaled[:, :], PJ[j][:, :], r_row[:, :], ALU.mult)\
                  .then_inc(proj_scaled, 1)

            def proj_lo_part(pair, j):
                dve.wait_ge(proj_hi, 2 * pair + j + 1)
                o, hi = qk_l[:, pair % 2, j, :], qk_h[:, pair % 2, j, :].bitcast(F32)
                if j == 0:
                    nc.vector.scalar_tensor_tensor(out=o, in0=scaled[:, :], scalar=-HD ** -0.5, in1=hi,
                                                   op0=ALU.mult, op1=ALU.subtract).then_inc(proj_lo, 1)
                else:
                    nc.vector.tensor_tensor(o, scaled[:, :], hi, ALU.subtract).then_inc(proj_lo, 1)

            def v_scale(pair):
                dve.wait_ge(w_used, 3 * pair + 3)
                if pair >= 1:
                    dve.wait_ge(v_turned, pair)
                nc.vector.tensor_tensor(v_raw, VB[:, :], r_row[:, :], ALU.mult).then_inc(v_scaled, 1)

            def v_lo_part(pair):
                dve.wait_ge(v_hi, pair + 1)
                nc.vector.tensor_tensor(v_l[:, pair % 2, :, :].rearrange("p a b -> p (a b)"), PJ[1][:, :],
                                        v_h[:, pair % 2, :, :].rearrange("p a b -> p (a b)").bitcast(F32),
                                        ALU.subtract).then_inc(v_lo, 1)

            dve.wait_ge(vec_turned, 1)
            nc.vector.tensor_copy(vec[:, 0:KT], bank[7][:, 0:KT]).then_inc(vec_ready, 1)
            row_stats_dve(dve, S_X)
            dve.wait_ge(vec_ready, 1)
            turn_lo_dve(dve, S_X, range(1))
            w_split_dve(dve, 0)
            turn_lo_dve(dve, S_X, range(1, KT))
            dve.wait_ge(sq_act[S_X], NT // 2)
            dve.wait_ge(sq_dve[S_X], NT // 2)
            inv_rms_dve(dve, S_X, ss[:, S_X, 0:NT], NT, D)
            spread_r_dve(dve, S_X, scaled[:, :])
            dve.wait_ge(wf_hi, 1)
            nc.vector.tensor_tensor(wf_l[:, :, :], wf_raw[:, :, :], wf_h[:, :, :].bitcast(F32),
                                    ALU.subtract).then_inc(wf_lo, 1)
            dve.wait_ge(vec_turned, 2)
            nc.vector.tensor_copy(vec[:, KT:VROWS], bank[4][:, KT:VROWS]).then_inc(vec_ready, 1)
            w_split_dve(dve, 1)
            dve.wait_ge(r_turned, 1)
            dve.wait_ge(r_row_ready, 1)
            proj_scale(0, 0)
            w_split_dve(dve, 2)
            proj_lo_part(0, 0)
            dve.wait_ge(z_done, 1)
            nc.vector.tensor_tensor(fz[3], SC[0][0:NH, :], r_row[0:NH, :], ALU.mult).then_inc(z_scaled, 1)
            dve.wait_ge(z_scaled, 1)
            dve.wait_ge(b_landed, 16)
            nc.vector.tensor_scalar(fz[2], fz[3], b_col[:, :], 0.0, ALU.add, ALU.min).then_inc(f_dve, 1)
            row_stats_dve(dve, S_MEM)
            nc.vector.memset(y_sq[0:NH, :], 1.0).then_inc(f_dve, 1)
            dve.wait_ge(f_dve, 2)
            dve.wait_ge(f_act, 3)
            nc.vector.tensor_tensor(fz[2], fz[2], fz[0], ALU.subtract).then_inc(f_dve, 1)
            dve.wait_ge(f_dve, 3)
            nc.vector.tensor_tensor_scan(fz[3], y_sq[0:NH, :], fz[2], 0.0, ALU.mult, ALU.add).then_inc(f_dve, 1)
            dve.wait_ge(sq_act[S_MEM], MT // 2)
            dve.wait_ge(sq_dve[S_MEM], MT // 2)
            inv_rms_dve(dve, S_MEM, ss[:, S_MEM, 0:MT], MT, D)
            nc.vector.tensor_scalar(misc[:, 1, :], tok[:, 1, :], inv(S_MEM, 1), None, ALU.mult).then_inc(nrm_dve, 1)
            proj_scale(0, 1)
            proj_lo_part(0, 1)
            v_scale(0)
            w_split_dve(dve, 3)
            turn_lo_dve(dve, S_MEM, range(KT))
            v_lo_part(0)
            w_split_dve(dve, 4)

            def logits(n):
                pair, hh, i = unit(n)
                h = 2 * pair + hh
                w = P * (i + 1)
                dve.wait_ge(s_done, n + 1)
                dve.wait_ge(bias_ready, h + 1)
                if n >= 2:
                    dve.wait_ge(p_ready, n - 1)
                if pair >= FOXP:
                    nc.vector.tensor_tensor_reduce(lg[:, n % 2, 0:w], SC[n % 2][:, 0:w],
                                                   cb[:, h % 2, SEQ - w:SEQ], 1.0, FLT_MAX, ALU.add, ALU.min,
                                                   minima[:, n:n + 1]).then_inc(lg_ready, 1)
                    return
                init = FLT_MAX
                if i:
                    nc.vector.tensor_tensor_reduce(lg[:, n % 2, 0:w - P], SC[n % 2][:, 0:w - P],
                                                   cb[:, h % 2, 0:w - P], 1.0, FLT_MAX, ALU.add, ALU.min,
                                                   past_min[:, n:n + 1]).then_inc(off_ready, 1)
                    dve.wait_ge(off_ready, (n // NT) * (NT - 1) + i)
                    init = past_min[:, n:n + 1]
                nc.vector.tensor_tensor_reduce(lg[:, n % 2, w - P:w], SC[n % 2][:, w - P:w],
                                               cbd[:, h % 2, w - P:w], 1.0, init, ALU.add, ALU.min,
                                               minima[:, n:n + 1]).then_inc(lg_ready, 1)

            def inv_sum(n):
                dve.wait_ge(p_ready, n + 1)
                nc.vector.reciprocal(inv_sums[:, n:n + 1], sums[:, n:n + 1]).then_inc(inv_ready, 1)

            def pt_split(n):
                i = n % NT
                dve.wait_ge(pt_hi, n + 1)
                t = slice(i * P, (i + 1) * P)
                nc.vector.tensor_tensor(pt_l[:, 0:i + 1, t],
                                        PT[n % 2][:, 0:(i + 1) * P].rearrange("p (k j) -> p k j", j=P),
                                        pt_h[:, 0:i + 1, t].bitcast(F32), ALU.subtract).then_inc(pt_lo, 1)

            def y_lo(pair):
                dve.wait_ge(act_hi[S_Y], pair + 1)
                nc.vector.scalar_tensor_tensor(out=act_l[:, pair, :], in0=y_fm[:, pair, :], scalar=gain(S_Y, pair),
                                               in1=act_h[:, pair, :].bitcast(F32), op0=ALU.mult,
                                               op1=ALU.subtract).then_inc(act_lo[S_Y], 1)

            def km_lo_part(m):
                dve.wait_ge(km_hi, m + 1)
                nc.vector.tensor_tensor(km_l[:, m, :], km_bank(m), km_h[:, m, :].bitcast(F32),
                                        ALU.subtract).then_inc(km_lo, 1)

            def vm_lo_part(h):
                for m in range(MT):
                    dve.wait_ge(vm_hi, MT * h + m + 1)
                    nc.vector.tensor_tensor(vm_l[:, m, h * 512:(h + 1) * 512], PJ[m][:, :],
                                            vm_h[:, m, h * 512:(h + 1) * 512].bitcast(F32),
                                            ALU.subtract).then_inc(vm_lo, 1)

            for n in range(NU):
                pair, u = divmod(n, UNITS)
                logits(n)
                if pair < NPAIR - 1 and u == 3:
                    proj_lo_part(pair + 1, 0)
                if pair < NPAIR - 1 and u == 6:
                    proj_lo_part(pair + 1, 1)
                inv_sum(n)
                if n >= LAST:
                    w_split_dve(dve, first_chunk(n + 1))
                if n >= 1:
                    pt_split(n - 1)
                if u == 0 and pair >= 1:
                    v_lo_part(pair)
                if pair < NPAIR - 1 and u == 2:
                    proj_scale(pair + 1, 0)
                if pair < NPAIR - 1 and u == 5:
                    proj_scale(pair + 1, 1)
                if pair < NPAIR - 1 and u == 7:
                    v_scale(pair + 1)
                if n in SPLIT_STEPS:
                    w_split_dve(dve, SPLIT_STEPS[n])
                if n >= LAST:
                    km_lo_part(u)
                    w_split_dve(dve, first_chunk(n + 1) + 1)
                if n == LAST + 3:
                    vm_lo_part(0)
                if n >= LAST and u >= 1:
                    y_lo(u - 1)
            pt_split(NU - 1)
            vm_lo_part(1)
            w_split_dve(dve, WO0 + 2)
            y_lo(NPAIR - 1)

            def add_tiles(s, half, group=None):
                if s == 0:
                    step, last = 2 * half + group, WO0 + (KT // 2) * half + (KT // 4) * (group + 1)
                    if step == 0:
                        dve.wait_ge(x2_landed, 16)
                else:
                    step, last = half, OUT0[s] + (half + 1) * OUT_K[s]
                for i in range(NT):
                    if i < NT - 1:
                        dve.wait_ge(out_done[s], (NT - 1) * step + i + 1)
                    else:
                        dve.wait_ge(w_used, last)
                    t = tok[:, i, half * 512:(half + 1) * 512]
                    if s == 0:
                        if group == 1:
                            dve.wait_ge(added[0], NT * (step - 1) + i + 1)
                        nc.vector.scalar_tensor_tensor(out=t, in0=mix_bank(group, i)[:, :],
                                                       scalar=inv(S_Y, NT * group + i), in1=t, op0=ALU.mult,
                                                       op1=ALU.add).then_inc(added[0], 1)
                    else:
                        nc.vector.tensor_tensor(t, out_bank(s, half, i)[:, :], t, ALU.add).then_inc(added[s], 1)

            for half in range(H2):
                for group in range(2):
                    for k in range(KT // 4):
                        c = WO0 + 3 + half * KT // 2 + group * KT // 4 + k
                        if c < WQ0:
                            w_split_dve(dve, c)
                    if (half, group) == (0, 0):
                        dve.wait_ge(y_stat, 1)
                        inv_rms_dve(dve, S_Y, bank[7][:, 0:2 * NT], 2 * NT, GW)
                    if (half, group) == (1, 1):
                        turn_lo_dve(dve, S_H1, range(KT // 2))
                        w_split_dve(dve, WQ0)
                    add_tiles(0, half, group)
            turn_lo_dve(dve, S_H1, range(KT // 2, KT))
            w_split_dve(dve, WQ0 + 1)
            halves_dve(dve, S_H1)
            nc.vector.tensor_scalar(rneg[:, :], rs[:, S_H1, NEWTON, 0:NT], -1.0, None, ALU.mult)\
              .then_inc(xb_ready, 1)

            def xq_lo_part(t):
                dve.wait_ge(xq_hi, t + 1)
                nc.vector.scalar_tensor_tensor(out=qk_l[:, (t // 2) % 2, t % 2, :], in0=PJ[t % 2][:, :],
                                               scalar=-CROSS_D ** -0.5,
                                               in1=qk_h[:, (t // 2) % 2, t % 2, :].bitcast(F32),
                                               op0=ALU.mult, op1=ALU.subtract).then_inc(xq_lo, 1)

            def xmins(m):
                dve.wait_ge(xs_done, m + 1)
                nc.vector.tensor_reduce(minima[:, m:m + 1], SC[m % 2][:, 0:MEM], AX_X, ALU.min).then_inc(xmin, 1)
                dve.wait_ge(xmin, m + 1)
                nc.vector.tensor_scalar(xbias[:, m:m + 1], minima[:, m:m + 1], inv(S_H1, m % NT), None,
                                        ALU.mult).then_inc(xb_ready, 1)

            def xnorm(m):
                dve.wait_ge(xp_ready, m + 1)
                nc.vector.reciprocal(inv_sums[:, m:m + 1], sums[:, m:m + 1]).then_inc(xinv, 1)
                dve.wait_ge(xinv, m + 1)
                nc.vector.tensor_scalar(pr[:, m % 2, 0:MEM], pr[:, m % 2, 0:MEM], inv_sums[:, m:m + 1], None,
                                        ALU.mult).then_inc(xp_norm, 1)

            def xpt_split(h):
                for t in range(MT):
                    dve.wait_ge(xpt_hi, MT * h + t + 1)
                    nc.vector.tensor_tensor(xp_l[:, t, :], PT[t][:, :], xp_h[:, t, :].bitcast(F32),
                                            ALU.subtract).then_inc(xpt_lo, 1)

            def xo_lo_part(h):
                for d in range(2):
                    dve.wait_ge(xo_hi, 2 * h + d + 1)
                    nc.vector.tensor_tensor(ox_l[:, 2 * h + d, :], OB[d][:, :],
                                            ox_h[:, 2 * h + d, :].bitcast(F32), ALU.subtract).then_inc(xo_lo, 1)

            w_split_dve(dve, WQ0 + 2)
            xq_lo_part(0)
            w_split_dve(dve, WQ0 + 3)
            xq_lo_part(1)
            for m in range(NX * NT + 2):
                h, i = divmod(m, NT)
                if m < NX * NT:
                    xmins(m)
                    xnorm(m)
                if i == 0 and h >= 1:
                    xpt_split(h - 1)
                if i == 1 and h >= 1:
                    xo_lo_part(h - 1)
                if h < NX - 1:
                    if i == 1:
                        w_split_dve(dve, WQ0 + 2 * (h + 1) + 2)
                        xq_lo_part(2 * (h + 1))
                    if i == 3:
                        w_split_dve(dve, WQ0 + 2 * (h + 1) + 3)
                        xq_lo_part(2 * (h + 1) + 1)
            for c in range(XO0 + 2, UP0):
                w_split_dve(dve, c)
                if c == XO0 + KT // 2 + 2:
                    add_tiles(1, 0)
            turn_lo_dve(dve, S_H2, range(KT // 2))
            w_split_dve(dve, UP0)
            add_tiles(1, 1)
            turn_lo_dve(dve, S_H2, range(KT // 2, KT))
            w_split_dve(dve, UP0 + 1)
            halves_dve(dve, S_H2)
            spread_r_dve(dve, S_H2, scaled[:, :])
            dve.wait_ge(r_row_ready, 2)

            def g_norm(j):
                dve.wait_ge(w_used, UP0 + 2 * j + 1)
                if j >= 2:
                    dve.wait_ge(g_conv2, j - 1)
                nc.vector.tensor_tensor(gr[:, j % 2, :], bank[(2 * j) % 4][:, :], r_row[:, :], ALU.mult)\
                  .then_inc(g_normed, 1)

            def conv(j):
                g, b = gc[:, j % 2, :], gr[:, j % 2, :]
                dve.wait_ge(g_scaled, j + 1)
                nc.vector.scalar_tensor_tensor(out=g[:, 1:SEQ], in0=b[:, 0:SEQ - 1], scalar=col("cw", FT + j),
                                               in1=g[:, 1:SEQ], op0=ALU.mult, op1=ALU.add).then_inc(g_conv1, 1)
                dve.wait_ge(g_conv1, j + 1)
                nc.vector.scalar_tensor_tensor(out=g[:, 2:SEQ], in0=b[:, 0:SEQ - 2], scalar=col("cw", j),
                                               in1=g[:, 2:SEQ], op0=ALU.mult, op1=ALU.add).then_inc(g_conv2, 1)

            def u_norm(j):
                dve.wait_ge(w_used, UP0 + 2 * j + 2)
                if j >= 2:
                    dve.wait_ge(h_lo, j - 1)
                nc.vector.tensor_tensor(ur[:, j % 2, :], bank[(2 * j + 1) % 4][:, :], r_row[:, :], ALU.mult)\
                  .then_inc(u_normed, 1)

            def gated(j):
                dve.wait_ge(g_silu, j + 1)
                dve.wait_ge(u_normed, j + 1)
                nc.vector.tensor_tensor(ur[:, j % 2, :], ur[:, j % 2, :], gs[:, j % 2, :],
                                        ALU.mult).then_inc(h_ready, 1)

            def hidden_lo(j):
                dve.wait_ge(h_hi, j + 1)
                nc.vector.tensor_tensor(ff_l[:, j, :], ur[:, j % 2, :], ff_h[:, j, :].bitcast(F32),
                                        ALU.subtract).then_inc(h_lo, 1)

            for j in range(FT + 2):
                if j < FT:
                    g_norm(j)
                    w_split_dve(dve, UP0 + 2 * j + 2)
                    conv(j)
                if 1 <= j <= FT:
                    gated(j - 1)
                if j >= 2:
                    hidden_lo(j - 2)
                if j < FT:
                    u_norm(j)
                    w_split_dve(dve, UP0 + 2 * j + 3)

            def gain_half(half):
                for i in range(NT):
                    t = slice(half * 512, (half + 1) * 512)
                    dve.wait_ge(added[2], NT * half + i + 1)
                    nc.vector.tensor_tensor(misc[:, i, t], tok[:, i, t], row[:, t], ALU.mult).then_inc(gained, 1)

            for c in range(DN0 + 2, NCH):
                w_split_dve(dve, c)
                if c == DN0 + FT // 2 + 2:
                    add_tiles(2, 0)
                    dve.wait_ge(gf_landed, 16)
                    gain_half(0)
            add_tiles(2, 1)
            gain_half(1)
            halves_dve(dve, S_FIN)
            dve.wait_ge(gained, NT * H2)
            for i in range(1, NT, 2):
                nc.vector.tensor_scalar(tok[:, i, :], misc[:, i, :], inv(S_FIN, i), None, ALU.mult)\
                  .then_inc(fin_dve, 1)

        @block.tensor
        def _(pe):
            def f_triples(c, o, a, w, ks, fresh=None):
                for k in ks:
                    if fresh is not None:
                        pe.wait_ge(fresh, k + 1)
                    wh, wl = w_tile(c, k, P)
                    last = mm3(o, wh, wl, a[0][:, k, 0:w], a[1][:, k, 0:w], k == 0, k == KT - 1)
                if k == KT - 1:
                    last.then_inc(w_used, 1)

            def t_triples(c, outs, a, k0, k_first, k_end, signal=None, late=None):
                for i, o in enumerate(outs):
                    if late is not None and i == 2:
                        pe.wait_ge(late, MT * H2)
                    for k in range(2):
                        wh, wl = w_tile(c, k, 512)
                        t = slice(i * P, (i + 1) * P)
                        last = mm3(o[:, :], a[0][:, k0 + k, t], a[1][:, k0 + k, t], wh, wl,
                                   k0 + k == k_first, k0 + k == k_end - 1)
                    if i == len(outs) - 1:
                        last.then_inc(w_used, 1)
                    elif signal is not None and k0 + 2 == k_end:
                        last.then_inc(signal, 1)

            def v_turn(pair):
                pe.wait_ge(v_scaled, pair + 1)
                pe.wait_ge(proj_scaled, 2 * pair + 2)
                for i in range(NT):
                    last = nc.tensor.transpose(PJ[1][:, i * P:(i + 1) * P], v_raw[:, i * P:(i + 1) * P],
                                               ident[:, :])
                last.then_inc(v_turned, 1)

            acts, mem_acts = (act_h, act_l), (mn_h, mn_l)

            mix = KT
            pe.wait_ge(ident_ready, 2)
            pe.wait_ge(mix_landed, 16)
            nc.tensor.transpose(bank[7][:, 0:mix], vec_rows[0:mix, :], ident[0:mix, 0:mix]).then_inc(vec_turned, 1)
            for i in range(NT):
                pe.wait_ge(x_landed[i], 16)
                for k in range(KT):
                    if (i, k) == (0, KT - 1):
                        pe.wait_ge(vec_ready, 1)
                    last = nc.tensor.transpose(turn_bank(S_X, k)[:, i * P:(i + 1) * P],
                                               tok[:, i, k * P:(k + 1) * P], ident[:, :])
                    if i == NT - 1:
                        last.then_inc(turned[S_X], 1)

            pe.wait_ge(w_lo, 1)
            f_triples(0, PJ[0][:, :], acts, SEQ, range(KT), fresh=act_lo[S_X])
            pe.wait_ge(vec_landed, 16 * (len(VEC) - 1))
            nc.tensor.transpose(bank[4][:, 0:VROWS], vec_rows[0:VROWS, :], ident[0:VROWS, 0:VROWS])\
              .then_inc(vec_turned, 1)
            turn_r_pe(pe, 1, bank[3], scaled)
            pe.wait_ge(wf_lo, 1)
            for k in range(KT):
                last = mm3(SC[0][0:NH, :], wf_h[:, k, :], wf_l[:, k, :], act_h[:, k, :], act_l[:, k, :],
                           k == 0, k == KT - 1)
            last.then_inc(z_done, 1)
            pe.wait_ge(w_lo, 2)
            f_triples(1, PJ[1][:, :], acts, SEQ, range(KT))
            pe.wait_ge(w_lo, 3)
            f_triples(2, VB[:, :], acts, SEQ, range(KT))
            pe.wait_ge(z_scaled, 1)
            pe.wait_ge(vec_ready, 2)
            pe.wait_ge(nrm_act, 1)
            pe.wait_ge(nrm_dve, 1)
            turn_pe(pe, S_MEM, range(KT))
            v_turn(0)
            pe.wait_ge(act_lo[S_MEM], KT)

            def scores(n):
                pair, hh, i = unit(n)
                pe.wait_ge(proj_lo, 2 * pair + 2)
                if n >= 2:
                    pe.wait_ge(lg_ready, n - 1)
                r, t, w = slice(hh * HD, (hh + 1) * HD), slice(i * P, (i + 1) * P), P * (i + 1)
                s = pair % 2
                mm3(SC[n % 2][:, 0:w], qk_h[r, s, 0, t], qk_l[r, s, 0, t], qk_h[r, s, 1, 0:w],
                    qk_l[r, s, 1, 0:w], True, True).then_inc(s_done, 1)

            def p_turn(n):
                _, _, i = unit(n)
                pe.wait_ge(p_norm, n + 1)
                if n >= 2:
                    pe.wait_ge(pt_lo, n - 1)
                for k in range(i + 1):
                    last = nc.tensor.transpose(PT[n % 2][:, k * P:(k + 1) * P],
                                               pr[:, n % 2, k * P:(k + 1) * P], ident[:, :])
                last.then_inc(p_turned, 1)

            def pv(h):
                pair, hh = divmod(h, 2)
                pe.wait_ge(pt_lo, NT * (h + 1))
                pe.wait_ge(v_lo, pair + 1)
                if h >= 1:
                    pe.wait_ge(y_ready, h)
                d = slice(hh * HD, (hh + 1) * HD)
                for k in range(NT):
                    t = slice(k * P, SEQ)
                    last = mm3(YB[0:HD, t], v_h[:, pair % 2, k, d], v_l[:, pair % 2, k, d],
                               pt_h[:, k, t], pt_l[:, k, t], k == 0, k == NT - 1)
                last.then_inc(pv_done, 1)

            def project(pair, lo, hi):
                for m in range(lo, hi):
                    j, k = divmod(m, KT)
                    if k == 0:
                        pe.wait_ge(w_lo, 3 * pair + j + 1)
                        if j == 0:
                            pe.wait_ge(proj_scaled, 2 * pair - 1)
                        if j == 1:
                            pe.wait_ge(v_lo, pair)
                        if j == 2:
                            pe.wait_ge(v_scaled, pair)
                    f_triples(3 * pair + j, (PJ[0], PJ[1], VB)[j][:, :], acts, SEQ, [k])

            def mem_chunk(c):
                kind, m = mem_chunks[c]
                pe.wait_ge(w_lo, c + 1)
                if kind == "k":
                    if m == 0:
                        pe.wait_ge(v_scaled, NPAIR)
                    if m >= 1:
                        pe.wait_ge(km_lo, m)
                    f_triples(c, km_bank(m), mem_acts, MEM, range(KT))
                else:
                    h, k = divmod(m, KT // 2)
                    if m == 0:
                        pe.wait_ge(v_lo, NPAIR)
                        pe.wait_ge(proj_scaled, 2 * NPAIR)
                    if m == KT // 2:
                        pe.wait_ge(vm_lo, MT)
                    t_triples(c, PJ, mem_acts, 2 * k, 0, KT)

            for n in range(NU):
                pair, u = divmod(n, UNITS)
                lo = PER_STEP * u
                scores(n)
                if pair < NPAIR - 1:
                    project(pair + 1, lo, lo + 2)
                else:
                    mem_chunk(first_chunk(n))
                if u == 0 and pair >= 1:
                    v_turn(pair)
                if n >= 1:
                    p_turn(n - 1)
                if n % NT == 1 and n >= NT:
                    pv(n // NT - 1)
                if pair < NPAIR - 1:
                    project(pair + 1, lo + 2, lo + PER_STEP)
                else:
                    mem_chunk(first_chunk(n) + 1)

            def mix_out(c):
                half, k = divmod(c, KT // 2)
                group = k // (KT // 4)
                pe.wait_ge(w_lo, WO0 + c + 1)
                if half == 0:
                    pe.wait_ge(act_lo[S_Y], 2 * k + 2)
                elif k % (KT // 4) == 0:
                    pe.wait_ge(added[0], NT * (group + 1))
                if c == KT // 4:
                    pe.wait_ge(rms[S_Y], 1)
                t_triples(WO0 + c, [mix_bank(group, i) for i in range(NT)], acts, 2 * k, 4 * group,
                          4 * group + 4, out_done[0], late=vm_lo if c == 0 else None)

            p_turn(NU - 1)
            mix_out(0)
            pv(2 * NPAIR - 1)
            mix_out(1)
            pe.wait_ge(y_summed, NPAIR - 2)
            pe.wait_ge(y_ready, 2 * NPAIR)
            for g in range(2):
                for i in range(NT):
                    e = NT * g + i
                    last = nc.tensor.matmul(bank[7][:, e:e + 1], y_acc[:, g, i * P:(i + 1) * P],
                                            ones[:, :], start=True, stop=True)
            last.then_inc(y_stat, 1)
            for c in range(2, KT):
                mix_out(c)
                if c == KT - 2:
                    pe.wait_ge(added[0], 3 * NT)
                    turn_pe(pe, S_H1, range(KT // 2))

            def token_out(s, a, ready, turn=None):
                for c in range(2 * OUT_K[s]):
                    half, k = divmod(c, OUT_K[s])
                    pe.wait_ge(w_lo, OUT0[s] + c + 1)
                    if half == 0:
                        pe.wait_ge(ready, 2 * k + 2)
                    if turn is not None and c == 2 * OUT_K[s] - 1:
                        pe.wait_ge(added[s], NT)
                        turn_pe(pe, turn, range(KT // 2))
                    t_triples(OUT0[s] + c, [out_bank(s, half, i) for i in range(NT)], a, 2 * k, 0,
                              2 * OUT_K[s], out_done[s])

            pe.wait_ge(w_lo, WQ0 + 1)
            pe.wait_ge(act_lo[S_H1], KT // 2)
            f_triples(WQ0, PJ[0][:, :], acts, SEQ, range(KT // 2))
            pe.wait_ge(added[0], 4 * NT)
            turn_pe(pe, S_H1, range(KT // 2, KT))
            f_triples(WQ0, PJ[0][:, :], acts, SEQ, range(KT // 2, KT), fresh=act_lo[S_H1])
            pe.wait_ge(w_lo, WQ0 + 2)
            f_triples(WQ0 + 1, PJ[1][:, :], acts, SEQ, range(KT))

            def xscores(m):
                h, i = divmod(m, NT)
                pe.wait_ge(xq_lo, 2 * h + 2)
                if m >= 2:
                    pe.wait_ge(xp_ready, m - 1)
                t = slice(i * P, (i + 1) * P)
                for d in range(2):
                    last = mm3(SC[m % 2][:, 0:MEM], qk_h[:, h % 2, d, t], qk_l[:, h % 2, d, t],
                               km_h[:, 2 * h + d, :], km_l[:, 2 * h + d, :], d == 0, d == 1)
                last.then_inc(xs_done, 1)

            def xp_turn(m):
                h, i = divmod(m, NT)
                pe.wait_ge(xp_norm, m + 1)
                if i == 0 and h >= 1:
                    pe.wait_ge(xpt_lo, MT * h)
                for t in range(MT):
                    last = nc.tensor.transpose(PT[t][:, i * P:(i + 1) * P], pr[:, m % 2, t * P:(t + 1) * P],
                                               ident[:, :])
                last.then_inc(xp_turned, 1)

            def xpv(h):
                pe.wait_ge(xpt_lo, MT * (h + 1))
                if h >= 1:
                    pe.wait_ge(xo_lo, 2 * h)
                for d in range(2):
                    f = slice((2 * h + d) * P, (2 * h + d + 1) * P)
                    for t in range(MT):
                        last = mm3(OB[d][:, :], vm_h[:, t, f], vm_l[:, t, f], xp_h[:, t, :], xp_l[:, t, :],
                                   t == 0, t == MT - 1)
                    last.then_inc(xo_done, 1)

            for m in range(NX * NT + 2):
                h, i = divmod(m, NT)
                t = 2 * (h + 1) + i // 2
                ks = range((i % 2) * KT // 2, (i % 2 + 1) * KT // 2)
                if m < NX * NT:
                    xscores(m)
                if h < NX - 1:
                    if i % 2 == 0:
                        pe.wait_ge(w_lo, WQ0 + t + 1)
                        pe.wait_ge(xq_lo, t - 1)
                    f_triples(WQ0 + t, PJ[t % 2][:, :], acts, SEQ, ks)
                if 1 <= m <= NX * NT:
                    xp_turn(m - 1)
                if i == 1 and h >= 1:
                    xpv(h - 1)
            token_out(1, (ox_h, ox_l), xo_lo, turn=S_H2)

            for j in range(FT):
                for g in range(2):
                    c = UP0 + 2 * j + g
                    pe.wait_ge(w_lo, c + 1)
                    if j >= 2:
                        pe.wait_ge(u_normed if g else g_normed, j - 1)
                    b = bank[(2 * j + g) % 4][:, :]
                    if j or g:
                        f_triples(c, b, acts, SEQ, range(KT))
                        continue
                    pe.wait_ge(act_lo[S_H2], KT // 2)
                    f_triples(c, b, acts, SEQ, range(KT // 2))
                    pe.wait_ge(added[1], 2 * NT)
                    turn_pe(pe, S_H2, range(KT // 2, KT))
                    f_triples(c, b, acts, SEQ, range(KT // 2, KT), fresh=act_lo[S_H2])
                if j == 0:
                    turn_r_pe(pe, 2, bank[7], scaled)
            token_out(2, (ff_h, ff_l), h_lo)


_INS = ["x", "mem", "g_mix", "w_in", "b_forget", "g_fox", "g_moba", "w_out", "g_cross", "g_mem", "w_q_mem",
        "w_kv_mem", "w_o_mem", "g_ffn", "w_up", "conv_w", "conv_b", "w_down", "g_final"]


def kernel(**inputs):
    import numpy as _np
    import concourse.bacc as _bacc
    from concourse.bass_utils import run_bass_kernel_spmd as _run

    nc = _bacc.Bacc("TRN2", target_bir_lowering=False, num_devices=1)
    arrays, args = {}, []
    for name in _INS:
        a = _np.ascontiguousarray(inputs[name])
        arrays[f"in_{name}"] = a
        args.append(nc.dram_tensor(f"in_{name}", a.shape, mybir.dt.from_np(a.dtype), kind="ExternalInput").ap())
    args.append(nc.dram_tensor("out_0", inputs["x"].shape, F32, kind="ExternalOutput").ap())
    hymba_layer(nc, *args)
    r = _run(nc, [arrays], core_ids=[0])
    return r.results[0]["out_0"]
```

```python
from contextlib import ExitStack

import concourse.bass as bass
from concourse.bass import ds
from concourse import mybir

F32 = mybir.dt.float32
F32R = mybir.dt.float32r
I32 = mybir.dt.int32
ALU = mybir.AluOpType
ACT = mybir.ActivationFunctionType
AX_X = mybir.AxisListType.X

P = 128
EPS = 1e-6
BIG = 1.0e30
FLT_MAX = 3.0e38


def hymba_layer(nc, x, mem, g_mix, w_in, b_forget, g_fox, g_moba, w_out, g_cross, g_mem, w_q_mem,
                w_kv_mem, w_o_mem, g_ffn, w_up, conv_w, conv_b, w_down, g_final, out):
    SEQ, D = x.shape[1], x.shape[2]
    MEM = mem.shape[1]
    NH = b_forget.shape[1]
    GW = g_fox.shape[1]
    HD = GW // NH
    FF = conv_b.shape[1]
    TAPS = conv_w.shape[1]
    NT = SEQ // P
    MT = MEM // P
    KT = D // P
    FT = FF // P
    CROSS_D = 256
    NX = D // CROSS_D
    NPAIR = 2 * GW // P
    FOXP = GW // P
    UNITS = 2 * NT
    H2 = D // 512
    assert (SEQ, D, MEM, HD, NH, NT, KT, H2) == (512, 1024, 256, 64, 8, 4, 8, 2) and TAPS == 3

    x_t = x[0].rearrange("(i p) d -> p i d", p=P)
    mem_t = mem[0].rearrange("(i p) d -> p i d", p=P)
    out_t = out[0].rearrange("(i p) d -> p i d", p=P)
    w_in, w_out, w_q_mem, w_kv_mem, w_o_mem = w_in[0], w_out[0], w_q_mem[0], w_kv_mem[0], w_o_mem[0]
    w_up, w_down = w_up[0], w_down[0]

    CH = 1024

    def f_chunk(w, col):
        return w[:, col:col + P].rearrange("(k p) n -> p k n", p=P)

    def t_chunk(w, k, half):
        return w[k * P:(k + 2) * P, half * 512:half * 512 + 512].rearrange("(k p) n -> p k n", p=P)

    MOBA0 = 3 * GW + NH
    chunks = []
    for pair in range(NPAIR):
        base = pair * P if pair < FOXP else MOBA0 + (pair - FOXP) * P
        chunks += [f_chunk(w_in, base + j * GW) for j in range(3)]
    KV0 = len(chunks)

    def km_pos(m):
        return KV0 + max(2 * m - 1, 0)

    def vm_pos(v):
        return KV0 + min(2 * v + 2, 2 * KT - 1)

    mem_chunks = {km_pos(m): ("k", m) for m in range(KT)}
    mem_chunks.update({vm_pos(v): ("v", v) for v in range(KT)})
    for c in range(KV0, KV0 + 2 * KT):
        kind, m = mem_chunks[c]
        chunks += [f_chunk(w_kv_mem, m * P) if kind == "k" else
                   t_chunk(w_kv_mem[:, D:], 2 * (m % (KT // 2)), m // (KT // 2))]
    WO0 = len(chunks)
    chunks += [t_chunk(w_out, k, h) for h in range(H2) for k in range(0, KT, 2)]
    WQ0 = len(chunks)
    chunks += [f_chunk(w_q_mem, m * P) for m in range(KT)]
    XO0 = len(chunks)
    chunks += [t_chunk(w_o_mem, k, h) for h in range(H2) for k in range(0, KT, 2)]
    UP0 = len(chunks)
    for j in range(FT):
        chunks += [f_chunk(w_up, j * P), f_chunk(w_up, FF + j * P)]
    DN0 = len(chunks)
    chunks += [t_chunk(w_down, k, h) for h in range(H2) for k in range(0, FT, 2)]
    NCH = len(chunks)
    RING = 3

    c_dram = nc.dram_tensor("c_scratch", (NH, SEQ), F32, kind="Internal").ap()

    with ExitStack() as ctx:
        def sb(name, shape, dt=F32):
            return ctx.enter_context(nc.sbuf_tensor(name, shape, dt))

        def sem(name):
            return ctx.enter_context(nc.semaphore(name))

        bank = [ctx.enter_context(nc.psum_tensor(f"bank{b}", [P, 512], F32)) for b in range(8)]
        PJ, SC, PT, OB = bank[0:2], bank[2:4], bank[4:6], bank[6:8]
        YB, VB = bank[6], bank[7]

        tok = sb("tok", [P, NT, D])
        misc = sb("misc", [P, NT, D])
        act_h = sb("act_h", [P, KT, SEQ], F32R)
        act_l = sb("act_l", [P, KT, SEQ], F32R)
        w_raw = sb("w_raw", [P, RING, CH])
        w_h = sb("w_h", [P, RING, CH], F32R)
        w_l = sb("w_l", [P, RING, CH], F32R)
        big = sb("big", [P, 2 * FT * SEQ], F32R)
        row = sb("row", [P, D])
        v_raw = row[:, 0:SEQ]
        dist = row[:, SEQ:2 * SEQ]
        fmask = sb("fmask", [P, P])
        ident = sb("ident", [P, P])
        ones = sb("ones", [P, 1])
        r_row = sb("r_row", [P, SEQ])
        scaled = sb("scaled", [P, SEQ])
        y_sq = sb("y_sq", [P, SEQ])
        y_acc = sb("y_acc", [P, 2, SEQ])
        vec = sb("vec", [P, P])
        wf_raw = sb("wf_raw", [P, KT, NH])
        wf_h = sb("wf_h", [P, KT, NH], F32R)
        wf_l = sb("wf_l", [P, KT, NH], F32R)
        b_col = sb("b_col", [NH, 1])
        minima = sb("minima", [P, NPAIR * UNITS])
        sums = sb("sums", [P, NPAIR * UNITS])
        inv_sums = sb("inv_sums", [P, NPAIR * UNITS])
        NSTAGE = 6
        ss = sb("ss", [P, NSTAGE, 8])
        s_sum = sb("s_sum", [P, NSTAGE, 8])
        ms = sb("ms", [P, NSTAGE, 8])
        seed = sb("seed", [P, NSTAGE, 8], I32)
        NEWTON = 3
        rs = sb("rs", [P, NSTAGE, NEWTON + 1, 8])
        t_rr = sb("t_rr", [P, NSTAGE, 8])
        t_ms = sb("t_ms", [P, NSTAGE, 8])
        FIN_RMS = 4 + 2 * NEWTON
        fin_m = sb("fin_m", [P, NT, 2])
        fin_seed = sb("fin_seed", [P, NT], I32)
        fin_r = sb("fin_r", [P, NT, NEWTON + 1])
        fin_t = sb("fin_t", [P, NT, NEWTON])
        past_min = sb("past_min", [P, NPAIR * UNITS])
        rneg = sb("rneg", [P, NT])
        xbias = sb("xbias", [P, NX * NT])

        def part(lo, shape):
            n = 1
            for s in shape:
                n *= s
            v = big[:, lo:lo + n]
            if len(shape) == 2:
                v = v.rearrange("p (a b) -> p a b", a=shape[0])
            if len(shape) == 3:
                v = v.rearrange("p (a b c) -> p a b c", a=shape[0], b=shape[1])
            return v

        qk_h, qk_l = part(0, [2, 2, SEQ]), part(2048, [2, 2, SEQ])
        km_h, km_l = part(4096, [KT, MEM]), part(6144, [KT, MEM])
        vm_h, vm_l = part(8192, [MT, D]), part(10240, [MT, D])
        v_h, v_l = part(12288, [2, NT, P]), part(13312, [2, NT, P])
        mn_h, mn_l = part(14336, [KT, MEM]), part(16384, [KT, MEM])
        ox_h, ox_l = part(12288, [KT, SEQ]), part(16384, [KT, SEQ])
        pt_h, pt_l = part(18432, [NT, SEQ]), part(20480, [NT, SEQ])
        xp_h, xp_l = part(20480, [MT, SEQ]), part(21504, [MT, SEQ])
        ff_h, ff_l = part(0, [FT, SEQ]), part(FT * SEQ, [FT, SEQ])

        flat = misc[:, :, :].rearrange("p a b -> p (a b)")
        lg = flat[:, 0:1024].rearrange("p (a b) -> p a b", a=2)
        pr = flat[:, 1024:2048].rearrange("p (a b) -> p a b", a=2)
        cb = flat[:, 2048:3072].rearrange("p (a b) -> p a b", a=2)
        cbd = flat[:, 3072:4096].rearrange("p (a b) -> p a b", a=2)
        gr, gc, gs, ur = (flat[:, 1024 * j:1024 * (j + 1)].rearrange("p (a b) -> p a b", a=2) for j in range(4))
        vec_rows = y_acc[:, 1, 0:P]
        y_fm = tok[:, :, :].rearrange("p a b -> p (a b)").rearrange("p (k t) -> p k t", k=KT)
        fz = [flat[0:NH, 2048 + 512 * j:2560 + 512 * j] for j in range(4)]

        VEC = {}
        at = 0
        for name, src in (("mix", g_mix), ("mem", g_mem), ("fox", g_fox), ("moba", g_moba),
                          ("cross", g_cross), ("ffn", g_ffn), ("cw", conv_w), ("cb", conv_b)):
            n = 1
            for s in src.shape:
                n *= s
            VEC[name] = (at, n // P, src)
            at += n // P
        assert at <= P
        VROWS = at

        def col(name, k):
            return vec[:, VEC[name][0] + k:VEC[name][0] + k + 1]

        def vec_col(name, k):
            return vec[:, ds(VEC[name][0] + k, 1)]

        def hidden(lo, j):
            return big[:, ds(lo * FT * SEQ + j * SEQ, SEQ)]

        w_landed = [sem(f"w_landed{s}") for s in range(RING)]
        w_hi, w_lo, w_used = sem("w_hi"), sem("w_lo"), sem("w_used")
        x_landed = [sem(f"x_landed{i}") for i in range(NT)]
        mem_landed, mix_landed, vec_landed = sem("mem_landed"), sem("mix_landed"), sem("vec_landed")
        wf_landed, b_landed = sem("wf_landed"), sem("b_landed")
        c_stored = sem("c_stored")
        c_landed = [sem(f"c_landed{s}") for s in range(2)]
        x2_landed, gf_landed, out_stored = sem("x2_landed"), sem("gf_landed"), sem("out_stored")
        ident_ready, masks_ready = sem("ident_ready"), sem("masks_ready")
        vec_turned, vec_ready = sem("vec_turned"), sem("vec_ready")
        sq_act = [sem(f"sq_act{s}") for s in range(NSTAGE)]
        sq_dve = [sem(f"sq_dve{s}") for s in range(NSTAGE)]
        rms = [sem(f"rms{s}") for s in range(NSTAGE)]
        nrm_act, nrm_dve = sem("nrm_act"), sem("nrm_dve")
        turned = [sem(f"turned{s}") for s in range(NSTAGE)]
        act_hi = [sem(f"act_hi{s}") for s in range(NSTAGE)]
        act_lo = [sem(f"act_lo{s}") for s in range(NSTAGE)]
        wf_hi, wf_lo = sem("wf_hi"), sem("wf_lo")
        r_spread, r_turned, r_row_ready = sem("r_spread"), sem("r_turned"), sem("r_row_ready")
        z_done, z_scaled = sem("z_done"), sem("z_scaled")
        f_act, f_dve = sem("f_act"), sem("f_dve")
        proj_scaled, proj_hi, proj_lo = sem("proj_scaled"), sem("proj_hi"), sem("proj_lo")
        v_scaled, v_turned, v_hi, v_lo = sem("v_scaled"), sem("v_turned"), sem("v_hi"), sem("v_lo")
        s_done, bias_ready, lg_ready = sem("s_done"), sem("bias_ready"), sem("lg_ready")
        off_ready = sem("off_ready")
        p_ready, p_turned = sem("p_ready"), sem("p_turned")
        pt_hi, pt_lo, pv_done = sem("pt_hi"), sem("pt_lo"), sem("pv_done")
        inv_ready, p_norm, y_ready = sem("inv_ready"), sem("p_norm"), sem("y_ready")
        y_squared, y_summed, y_stat = sem("y_squared"), sem("y_summed"), sem("y_stat")
        km_hi, km_lo = sem("km_hi"), sem("km_lo")
        vm_hi, vm_lo = sem("vm_hi"), sem("vm_lo")
        out_done = [sem(f"out_done{s}") for s in range(3)]
        added = [sem(f"added{s}") for s in range(3)]
        xq_hi, xq_lo = sem("xq_hi"), sem("xq_lo")
        xs_done, xmin, xb_ready, xp_ready = sem("xs_done"), sem("xmin"), sem("xb_ready"), sem("xp_ready")
        xinv, xp_norm, xp_turned = sem("xinv"), sem("xp_norm"), sem("xp_turned")
        xpt_hi, xpt_lo = sem("xpt_hi"), sem("xpt_lo")
        xo_done, xo_hi, xo_lo = sem("xo_done"), sem("xo_hi"), sem("xo_lo")
        g_normed, u_normed, g_scaled = sem("g_normed"), sem("u_normed"), sem("g_scaled")
        g_conv1, g_conv2 = sem("g_conv1"), sem("g_conv2")
        g_silu, h_ready, h_hi, h_lo = sem("g_silu"), sem("h_ready"), sem("h_hi"), sem("h_lo")
        gained, fin_rms, fin_act, fin_dve = sem("gained"), sem("fin_rms"), sem("fin_act"), sem("fin_dve")

        S_X, S_MEM, S_Y, S_H1, S_H2, S_FIN = range(NSTAGE)
        TILES = {S_X: NT, S_MEM: MT, S_H1: NT, S_H2: NT}
        COL = {S_X: 0, S_MEM: NT}
        SRC = {S_X: tok, S_MEM: misc, S_H1: tok, S_H2: tok}

        def gain(s, k):
            if s == S_Y:
                return col("fox", k) if k < FOXP else col("moba", k - FOXP)
            return col({S_X: "mix", S_MEM: "mem", S_H1: "cross", S_H2: "ffn"}[s], k)

        def dst(s, k):
            return (mn_h[:, k, :], mn_l[:, k, :]) if s == S_MEM else (act_h[:, k, :], act_l[:, k, :])

        def turn_bank(s, k):
            if s == S_MEM:
                return bank[(4, 5, 6, 3)[k % 4]]
            return bank[k]

        def src_ready(eng, s, e):
            if s == S_X:
                eng.wait_ge(x_landed[e], 16)
            else:
                eng.wait_ge(mem_landed, 16)

        def row_stats_act(act, s):
            for e in range(TILES[s] // 2):
                src_ready(act, s, e)
                nc.scalar.activation(misc[:, e, :], tok[:, e, :], ACT.Square,
                                     accum_out=ss[:, S_X, COL[s] + e:COL[s] + e + 1]).then_inc(sq_act[s], 1)

        def row_stats_dve(dve, s, tiles):
            for e in tiles:
                src_ready(dve, s, e)
                nc.vector.tensor_tensor_reduce(misc[:, e, :], tok[:, e, :], tok[:, e, :], 1.0, 0.0,
                                               ALU.mult, ALU.add, ss[:, S_X, COL[s] + e:COL[s] + e + 1])\
                  .then_inc(sq_dve[s], 1)

        def half_stats_act(act, s, half, tiles=range(NT)):
            for i in tiles:
                e = NT * half + i
                act.wait_ge(added[s - S_H1], ADDS[s - S_H1] // H2 * (half + 1) - NT + i + 1)
                o = out_bank(2, half, i)[:, :] if s == S_FIN else misc[:, i, half * 512:(half + 1) * 512]
                nc.scalar.activation(o, tok[:, i, half * 512:(half + 1) * 512], ACT.Square,
                                     accum_out=ss[:, s, e:e + 1]).then_inc(sq_act[s], 1)

        def inv_rms_dve(dve, s, sums_in, n, width):
            m = ms[:, s, 0:n]
            nc.vector.tensor_scalar(m, sums_in, 1.0 / width, EPS, ALU.mult, ALU.add).then_inc(rms[s], 1)
            dve.wait_ge(rms[s], 1)
            nc.vector.tensor_scalar(seed[:, s, 0:n], m.bitcast(I32), 1, None, ALU.logical_shift_right)\
              .then_inc(rms[s], 1)
            dve.wait_ge(rms[s], 2)
            nc.vector.tensor_scalar(rs[:, s, 0, 0:n].bitcast(I32), seed[:, s, 0:n], -1.0, float(0x5f3759df),
                                    ALU.mult, ALU.add).then_inc(rms[s], 1)
            for t in range(NEWTON):
                r = rs[:, s, t, 0:n]
                dve.wait_ge(rms[s], 3 * t + 3)
                nc.vector.tensor_tensor(t_rr[:, s, 0:n], r, r, ALU.mult).then_inc(rms[s], 1)
                dve.wait_ge(rms[s], 3 * t + 4)
                nc.vector.scalar_tensor_tensor(out=t_ms[:, s, 0:n], in0=t_rr[:, s, 0:n], scalar=-0.5, in1=m,
                                               op0=ALU.mult, op1=ALU.mult).then_inc(rms[s], 1)
                dve.wait_ge(rms[s], 3 * t + 5)
                nc.vector.scalar_tensor_tensor(out=rs[:, s, t + 1, 0:n], in0=t_ms[:, s, 0:n], scalar=1.5,
                                               in1=r, op0=ALU.add, op1=ALU.mult).then_inc(rms[s], 1)
            dve.wait_ge(rms[s], RMS_DONE)

        RMS_DONE = 3 + 3 * NEWTON

        def inv(s, e):
            if s == S_MEM:
                s, e = S_X, NT + e
            return rs[:, s, NEWTON, e:e + 1]

        def halves_dve(dve, s):
            dve.wait_ge(sq_act[s], H2 * NT)
            nc.vector.tensor_tensor(s_sum[:, s, 0:NT], ss[:, s, 0:NT], ss[:, s, NT:2 * NT],
                                    ALU.add).then_inc(sq_dve[s], 1)
            dve.wait_ge(sq_dve[s], 1)
            inv_rms_dve(dve, s, s_sum[:, s, 0:NT], NT, D)

        def turn_pe(pe, s, ks):
            for k in ks:
                if k >= 4 and s == S_MEM:
                    pe.wait_ge(act_lo[s], k - 3)
                for i in range(TILES[s]):
                    last = nc.tensor.transpose(turn_bank(s, k)[:, i * P:(i + 1) * P],
                                               SRC[s][:, i, k * P:(k + 1) * P], ident[:, :])
                last.then_inc(turned[s], 1)

        def turn_hi_act(act, s, ks):
            w = TILES[s] * P
            for k in ks:
                act.wait_ge(turned[s], k + 1)
                nc.scalar.activation(dst(s, k)[0], turn_bank(s, k)[:, 0:w], ACT.Copy,
                                     scale=gain(s, k)).then_inc(act_hi[s], 1)

        def turn_lo_dve(dve, s, ks):
            w = TILES[s] * P
            for k in ks:
                dve.wait_ge(act_hi[s], k + 1)
                nc.vector.scalar_tensor_tensor(out=dst(s, k)[1], in0=turn_bank(s, k)[:, 0:w], scalar=gain(s, k),
                                               in1=dst(s, k)[0].bitcast(F32), op0=ALU.mult,
                                               op1=ALU.subtract).then_inc(act_lo[s], 1)

        def spread_r_dve(dve, s, scratch):
            nc.vector.tensor_copy(scratch.rearrange("p (i j) -> p i j", i=NT),
                                  rs[:, s, NEWTON, 0:NT].unsqueeze(2).to_broadcast([P, NT, P]))\
              .then_inc(r_spread, 1)

        def turn_r_pe(pe, count, o, scratch):
            pe.wait_ge(r_spread, count)
            for i in range(NT):
                last = nc.tensor.transpose(o[:, i * P:(i + 1) * P], scratch[:, i * P:(i + 1) * P],
                                           ident[:, :])
            last.then_inc(r_turned, 1)

        def copy_r_act(act, count, o):
            act.wait_ge(r_turned, count)
            nc.scalar.activation(r_row[:, :], o[:, :], ACT.Copy).then_inc(r_row_ready, 1)

        MLP_TURN = 6
        MLP_FIRST = 3
        MLP_TURNS = (FT - MLP_FIRST) // MLP_TURN
        MLP_BODY = range(MLP_FIRST, MLP_FIRST + MLP_TURN)
        MLP_AFTER = MLP_FIRST + MLP_TURN * MLP_TURNS
        assert MLP_TURN % 2 == 0 and 2 * MLP_TURN % 4 == 0 and 2 * MLP_TURN % RING == 0

        def w_split_act(act, c, t=0):
            act.wait_ge(w_landed[c % RING], 16 * (c // RING + 1) + 16 * (2 * MLP_TURN // RING) * t)
            if c >= RING:
                act.wait_ge(w_used, c - RING + 1 + 2 * MLP_TURN * t)
            nc.scalar.activation(w_h[:, c % RING, :], w_raw[:, c % RING, :], ACT.Copy).then_inc(w_hi, 1)

        def w_split_dve(dve, c, t=0):
            dve.wait_ge(w_hi, c + 1 + 2 * MLP_TURN * t)
            nc.vector.tensor_tensor(w_l[:, c % RING, :], w_raw[:, c % RING, :],
                                    w_h[:, c % RING, :].bitcast(F32), ALU.subtract).then_inc(w_lo, 1)

        def mm3(o, sh, sl, mh, ml, start, stop):
            nc.tensor.matmul(o, sl, mh, start=start, stop=False)
            nc.tensor.matmul(o, sh, ml, start=False, stop=False)
            return nc.tensor.matmul(o, sh, mh, start=False, stop=stop)

        OUT0, OUT_K = (WO0, XO0, DN0), (KT // 2, KT // 2, FT // 2)

        ADDS = (2 * H2 * NT, H2 * NT, H2 * NT)

        def out_bank(s, half, i):
            return bank[4 * half + i] if s < 2 else bank[4 * (1 - half) + i]

        def w_tile(c, k, w):
            return (w_h[:, c % RING, k * w:(k + 1) * w], w_l[:, c % RING, k * w:(k + 1) * w])

        STEPS = [3 * KT * u // UNITS for u in range(UNITS + 1)]
        BEFORE = [3 if u % NT == 0 else 2 for u in range(UNITS)]

        def unit(n):
            pair, u = divmod(n, UNITS)
            return pair, u // NT, u % NT

        NU = NPAIR * UNITS

        SPLIT_STEPS = {}
        for pair in range(NPAIR - 1):
            SPLIT_STEPS[pair * UNITS + 1] = 3 * (pair + 1) + 2
            SPLIT_STEPS[pair * UNITS + 4] = 3 * (pair + 2)
            SPLIT_STEPS[pair * UNITS + 7] = 3 * (pair + 2) + 1

        LAST = NU - UNITS

        def first_chunk(n):
            return KV0 + 2 * (n - LAST)

        XSPLIT = {1: WQ0 + 4, 3: WQ0 + 5, 5: WQ0 + 6, 7: WQ0 + 7, 9: XO0, 10: XO0 + 1, 11: XO0 + 2}

        def km_bank(m):
            return (VB if m else PJ[0])[:, 0:MEM]

        def mix_bank(group, i):
            return bank[4 * group + (i + 2) % NT]

        block = ctx.enter_context(nc.Block())

        @block.sync
        def _(sp):
            def load_up(j, t=0):
                for g in range(2):
                    c = UP0 + 2 * j + g
                    sp.wait_ge(w_lo, c - RING + 1 + 2 * MLP_TURN * t)
                    src = w_up[:, ds((j + MLP_TURN * t) * P + g * FF, P)].rearrange("(k p) n -> p k n", p=P)
                    sp.dma_start(w_raw[:, c % RING, :].rearrange("p (k n) -> p k n", k=KT), src)\
                      .then_inc(w_landed[c % RING], 16)

            for i in range(NT - 1):
                sp.dma_start(tok[:, i, :], x_t[:, i, :]).then_inc(x_landed[i], 16)
            for c in range(NCH):
                if c == UP0 + 2 * MLP_FIRST:
                    with sp.Fori(0, MLP_TURNS) as t:
                        for j in MLP_BODY:
                            load_up(j, t)
                if UP0 + 2 * MLP_FIRST <= c < UP0 + 2 * MLP_AFTER:
                    continue
                if c == 1:
                    sp.dma_start(tok[:, NT - 1, :], x_t[:, NT - 1, :]).then_inc(x_landed[NT - 1], 16)
                if c == RING:
                    sp.dma_start(wf_raw[:, :, :], w_in[:, 3 * GW:3 * GW + NH].rearrange("(k p) n -> p k n", p=P))\
                      .then_inc(wf_landed, 16)
                    sp.dma_start(b_col[:, :], b_forget.rearrange("a n -> n a")).then_inc(b_landed, 16)
                    for name, (r, n, src) in VEC.items():
                        rows = src.rearrange("a (k p) -> (a k) p", p=P) if len(src.shape) == 2 else \
                            src.rearrange("a b (k p) -> (a b k) p", p=P)
                        if name != "mix":
                            sp.dma_start(vec_rows[r:r + n, :], rows).then_inc(vec_landed, 16)
                if c >= RING:
                    sp.wait_ge(w_lo, c - RING + 1)
                v = w_raw[:, c % RING, :].rearrange("p (k n) -> p k n", k=chunks[c].shape[1])
                sp.dma_start(v, chunks[c]).then_inc(w_landed[c % RING], 16)
            for i in range(NT):
                sp.wait_ge(fin_act, i + 1)
                sp.wait_ge(fin_dve, i + 1)
                sp.dma_start(out_t[:, i, :], tok[:, i, :]).then_inc(out_stored, 16)
            sp.wait_ge(out_stored, 16 * NT)

        @block.gpsimd
        def _(pool):
            nc.gpsimd.memset(ident[:, :], 0.0).then_inc(ident_ready, 1)
            pool.wait_ge(ident_ready, 1)
            nc.gpsimd.affine_select(out=ident[:, :], in_=ident[:, :], compare_op=ALU.not_equal, fill=1.0,
                                    base=0, pattern=[[-1, P]], channel_multiplier=1).then_inc(ident_ready, 1)
            nc.gpsimd.iota(dist[:, :], pattern=[[-1, SEQ]], base=SEQ - P, channel_multiplier=1,
                           allow_small_or_imprecise_dtypes=True).then_inc(masks_ready, 1)
            nc.gpsimd.memset(fmask[:, :], 0.0).then_inc(masks_ready, 1)
            pool.wait_ge(masks_ready, 2)
            nc.gpsimd.affine_select(out=dist[:, :], in_=dist[:, :], compare_op=ALU.is_ge, fill=BIG,
                                    base=SEQ - P, pattern=[[-1, SEQ]], channel_multiplier=1).then_inc(masks_ready, 1)
            nc.gpsimd.affine_select(out=fmask[:, :], in_=fmask[:, :], compare_op=ALU.is_ge, fill=BIG,
                                    base=0, pattern=[[-1, P]], channel_multiplier=1).then_inc(masks_ready, 1)
            nc.gpsimd.memset(ones[:, :], 1.0).then_inc(masks_ready, 1)
            pool.wait_ge(turned[S_X], KT)
            pool.wait_ge(sq_act[S_X], NT // 2)
            pool.dma_start(tok[:, 0:MT, :], mem_t).then_inc(mem_landed, 16)
            pool.wait_ge(f_dve, 4)
            pool.dma_start(c_dram, fz[3]).then_inc(c_stored, 16)
            pool.wait_ge(c_stored, 16)

            def bias(h):
                if h >= 2:
                    pool.wait_ge(lg_ready, NT * (h - 1))
                if h < NH:
                    pool.dma_start(cb[:, h % 2, :], c_dram[h, :].partition_broadcast(P))\
                        .then_inc(c_landed[h % 2], 16)
                    pool.wait_ge(c_landed[h % 2], 16 * (h // 2 + 1))
                    nc.gpsimd.tensor_tensor(cbd[:, h % 2, :].rearrange("p (i j) -> p i j", j=P),
                                            cb[:, h % 2, :].rearrange("p (i j) -> p i j", j=P),
                                            fmask[:, :].unsqueeze(1).to_broadcast([P, NT, P]),
                                            ALU.add).then_inc(bias_ready, 1)
                else:
                    nc.gpsimd.tensor_scalar(cb[:, h % 2, :], dist[:, :], 2.0 ** (-8.0 * (h - NH + 1) / NH), 0.0,
                                            ALU.mult, ALU.add).then_inc(bias_ready, 1)

            def sum_squares(pair):
                pool.wait_ge(y_ready, 2 * (pair + 1))
                first, g = pair % FOXP == 0, pair // FOXP
                if not first and pair % FOXP >= 2:
                    pool.wait_ge(y_summed, pair - 1 - g)
                o = y_acc[:, g, :] if first else y_sq[:, :]
                nc.gpsimd.tensor_tensor(o, y_fm[:, pair, :], y_fm[:, pair, :], ALU.mult)\
                  .then_inc(y_squared, 1)
                if first:
                    return
                pool.wait_ge(y_squared, pair + 1)
                nc.gpsimd.tensor_tensor(y_acc[:, g, :], y_acc[:, g, :], y_sq[:, :], ALU.add)\
                  .then_inc(y_summed, 1)

            pool.wait_ge(masks_ready, 5)
            bias(0)
            bias(1)
            for pair in range(NPAIR):
                if pair < NPAIR - 1:
                    bias(2 * pair + 2)
                    bias(2 * pair + 3)
                sum_squares(pair)
            pool.wait_ge(act_lo[S_Y], KT)
            pool.wait_ge(y_squared, NPAIR)
            pool.dma_start(tok[:, :, :], x_t).then_inc(x2_landed, 16)
            pool.wait_ge(v_turned, NPAIR)
            pool.wait_ge(bias_ready, 2 * NH)
            pool.dma_start(row[:, :], g_final.partition_broadcast(P)).then_inc(gf_landed, 16)

        @block.scalar
        def _(act):
            act.dma_start(vec_rows[0:KT, :], g_mix.rearrange("a (k p) -> (a k) p", p=P)).then_inc(mix_landed, 16)

            def proj_hi_part(pair, j):
                act.wait_ge(proj_scaled, 2 * pair + j + 1)
                if pair >= 2:
                    act.wait_ge(s_done, UNITS * (pair - 1))
                nc.scalar.activation(qk_h[:, pair % 2, j, :], scaled[:, :], ACT.Copy,
                                     scale=-HD ** -0.5 if j == 0 else 1.0).then_inc(proj_hi, 1)

            def v_hi_part(pair):
                act.wait_ge(v_turned, pair + 1)
                if pair >= 2:
                    act.wait_ge(pv_done, 2 * (pair - 1))
                nc.scalar.activation(v_h[:, pair % 2, :, :].rearrange("p a b -> p (a b)"), PJ[1][:, :],
                                     ACT.Copy).then_inc(v_hi, 1)

            row_stats_act(act, S_X)
            act.wait_ge(vec_ready, 1)
            w_split_act(act, 0)
            turn_hi_act(act, S_X, range(KT))
            act.wait_ge(wf_landed, 16)
            nc.scalar.activation(wf_h[:, :, :], wf_raw[:, :, :], ACT.Copy).then_inc(wf_hi, 1)
            w_split_act(act, 1)
            row_stats_act(act, S_MEM)
            act.wait_ge(rms[S_X], RMS_DONE)
            nc.scalar.activation(misc[:, 0, :], tok[:, 0, :], ACT.Copy, scale=inv(S_MEM, 0)).then_inc(nrm_act, 1)
            copy_r_act(act, 1, bank[3])
            w_split_act(act, 2)
            proj_hi_part(0, 0)
            act.wait_ge(z_scaled, 1)
            act.wait_ge(b_landed, 16)
            nc.scalar.activation(fz[0], fz[3], ACT.Abs, bias=b_col[:, :]).then_inc(f_act, 1)
            act.wait_ge(f_act, 1)
            nc.scalar.activation(fz[1], fz[0], ACT.Exp, scale=-1.0).then_inc(f_act, 1)
            act.wait_ge(f_act, 2)
            nc.scalar.activation(fz[0], fz[1], ACT.Ln, bias=1.0).then_inc(f_act, 1)
            turn_hi_act(act, S_MEM, range(KT // 2))
            proj_hi_part(0, 1)
            w_split_act(act, 3)
            turn_hi_act(act, S_MEM, range(KT // 2, KT))
            v_hi_part(0)
            w_split_act(act, 4)

            def probs(n):
                _, _, i = unit(n)
                w = P * (i + 1)
                act.wait_ge(lg_ready, n + 1)
                if n >= 2:
                    act.wait_ge(p_turned, n - 1)
                nc.scalar.activation(pr[:, n % 2, 0:w], lg[:, n % 2, 0:w], ACT.Exp, scale=-1.0,
                                     bias=minima[:, n:n + 1], accum_out=sums[:, n:n + 1]).then_inc(p_ready, 1)

            def probs_norm(n):
                _, _, i = unit(n)
                w = P * (i + 1)
                act.wait_ge(inv_ready, n + 1)
                nc.scalar.activation(pr[:, n % 2, 0:w], pr[:, n % 2, 0:w], ACT.Copy,
                                     scale=inv_sums[:, n:n + 1]).then_inc(p_norm, 1)

            def pt_split(n):
                i = n % NT
                act.wait_ge(p_turned, n + 1)
                if i == 0 and n >= NT:
                    act.wait_ge(pv_done, n // NT)
                nc.scalar.activation(pt_h[:, 0:i + 1, i * P:(i + 1) * P],
                                     PT[n % 2][:, 0:(i + 1) * P].rearrange("p (k j) -> p k j", j=P),
                                     ACT.Copy).then_inc(pt_hi, 1)

            def y_copy(h):
                act.wait_ge(pv_done, h + 1)
                if h == 0:
                    act.wait_ge(nrm_act, 1)
                    act.wait_ge(nrm_dve, 1)
                hh = h % 2
                nc.scalar.activation(y_fm[hh * HD:(hh + 1) * HD, h // 2, :], YB[0:HD, :],
                                     ACT.Copy).then_inc(y_ready, 1)

            def y_hi(pair):
                act.wait_ge(y_ready, 2 * (pair + 1))
                if pair == 0:
                    act.wait_ge(w_used, KV0)
                nc.scalar.activation(act_h[:, pair, :], y_fm[:, pair, :], ACT.Copy,
                                     scale=gain(S_Y, pair)).then_inc(act_hi[S_Y], 1)

            def km_hi_part(m):
                act.wait_ge(w_used, km_pos(m) + 1)
                nc.scalar.activation(km_h[:, m, :], km_bank(m), ACT.Copy).then_inc(km_hi, 1)

            def vm_hi_part(h):
                act.wait_ge(w_used, vm_pos(KT // 2 * (h + 1) - 1) + 1)
                for m in range(MT):
                    nc.scalar.activation(vm_h[:, m, h * 512:(h + 1) * 512], PJ[m][:, :], ACT.Copy)\
                       .then_inc(vm_hi, 1)

            for n in range(NU):
                pair, u = divmod(n, UNITS)
                probs(n)
                if n >= LAST:
                    w_split_act(act, first_chunk(n + 1))
                if n == LAST + KT // 2:
                    vm_hi_part(0)
                if n >= 1:
                    pt_split(n - 1)
                probs_norm(n)
                if u == 0 and pair >= 1:
                    v_hi_part(pair)
                if pair < NPAIR - 1 and u == 2:
                    proj_hi_part(pair + 1, 0)
                if pair < NPAIR - 1 and u == 5:
                    proj_hi_part(pair + 1, 1)
                if n in SPLIT_STEPS:
                    w_split_act(act, SPLIT_STEPS[n])
                if n == LAST:
                    km_hi_part(0)
                if n >= LAST:
                    w_split_act(act, first_chunk(n + 1) + 1)
                if LAST <= n < NU - 1:
                    km_hi_part(u + 1)
                if n % NT == 1 and n >= NT:
                    y_copy(n // NT - 1)
                if n >= LAST and u >= 1:
                    y_hi(u - 1)
            vm_hi_part(1)
            pt_split(NU - 1)
            w_split_act(act, WO0 + 2)
            y_copy(2 * NPAIR - 1)
            y_hi(NPAIR - 1)
            for c in range(WO0 + 3, WQ0):
                w_split_act(act, c)
            half_stats_act(act, S_H1, 0)
            turn_hi_act(act, S_H1, range(KT // 2))
            w_split_act(act, WQ0)
            half_stats_act(act, S_H1, 1)
            turn_hi_act(act, S_H1, range(KT // 2, KT))
            w_split_act(act, WQ0 + 1)

            def xq_hi_part(t):
                act.wait_ge(w_used, WQ0 + t + 1)
                if t >= 4:
                    act.wait_ge(xs_done, NT * (t // 2 - 1))
                nc.scalar.activation(qk_h[:, (t // 2) % 2, t % 2, :], PJ[t % 2][:, :], ACT.Copy,
                                     scale=-CROSS_D ** -0.5).then_inc(xq_hi, 1)

            def xprobs(m):
                act.wait_ge(xb_ready, m + 2)
                if m >= 2:
                    act.wait_ge(xp_turned, m - 1)
                nc.scalar.activation(pr[:, m % 2, 0:MEM], SC[m % 2][:, 0:MEM], ACT.Exp,
                                     scale=rneg[:, m % NT:m % NT + 1], bias=xbias[:, m:m + 1],
                                     accum_out=sums[:, m:m + 1]).then_inc(xp_ready, 1)

            def xpt_split(h):
                act.wait_ge(xp_turned, NT * (h + 1))
                if h >= 1:
                    act.wait_ge(xo_done, 2 * h)
                for t in range(MT):
                    nc.scalar.activation(xp_h[:, t, :], PT[t][:, :], ACT.Copy).then_inc(xpt_hi, 1)

            def xo_hi_part(h):
                for d in range(2):
                    act.wait_ge(xo_done, 2 * h + d + 1)
                    nc.scalar.activation(ox_h[:, 2 * h + d, :], OB[d][:, :], ACT.Copy).then_inc(xo_hi, 1)

            w_split_act(act, WQ0 + 2)
            xq_hi_part(0)
            xq_hi_part(1)
            w_split_act(act, WQ0 + 3)
            for m in range(NX * NT + 2):
                h, i = divmod(m, NT)
                if m < NX * NT:
                    xprobs(m)
                if m in XSPLIT:
                    w_split_act(act, XSPLIT[m])
                if m % 2 == 0 and m // 2 + 2 < 2 * NX:
                    xq_hi_part(m // 2 + 2)
                if i == 0 and h >= 1:
                    xpt_split(h - 1)
                if h >= 1 and i == (2 if h < NX - 1 else 1):
                    xo_hi_part(h - 1)
            for c in range(XO0 + 3, UP0):
                w_split_act(act, c)
                if c == XO0 + KT // 2 + 2:
                    half_stats_act(act, S_H2, 0)
            turn_hi_act(act, S_H2, range(KT // 2))
            w_split_act(act, UP0)
            half_stats_act(act, S_H2, 1)
            turn_hi_act(act, S_H2, range(KT // 2, KT))
            w_split_act(act, UP0 + 1)
            w_split_act(act, UP0 + 2)
            copy_r_act(act, 2, bank[7])

            def gate_scale(j, t=0):
                tile = j + MLP_TURN * t
                act.wait_ge(g_normed, tile + 1)
                if j >= 2:
                    act.wait_ge(g_silu, tile - 1)
                nc.scalar.activation(gc[:, j % 2, :], gr[:, j % 2, :], ACT.Identity,
                                     scale=vec_col("cw", 2 * FT + tile), bias=vec_col("cb", tile))\
                  .then_inc(g_scaled, 1)

            def gate_silu(j, t=0):
                tile = j + MLP_TURN * t
                act.wait_ge(g_conv2, tile + 1)
                if j >= 2:
                    act.wait_ge(h_ready, tile - 1)
                nc.scalar.activation(gs[:, j % 2, :], gc[:, j % 2, :], ACT.Silu).then_inc(g_silu, 1)

            def hidden_hi(j, t=0):
                tile = j + MLP_TURN * t
                act.wait_ge(h_ready, tile + 1)
                nc.scalar.activation(hidden(0, tile), ur[:, j % 2, :], ACT.Copy).then_inc(h_hi, 1)

            def gate_step(j, t=0):
                w_split_act(act, UP0 + 2 * j + 3, t)
                gate_scale(j, t)
                if j >= 1:
                    gate_silu(j - 1, t)
                if j >= 2:
                    hidden_hi(j - 2, t)
                w_split_act(act, UP0 + 2 * j + 4, t)

            for j in range(MLP_FIRST):
                gate_step(j)
            with act.Fori(0, MLP_TURNS) as t:
                for j in MLP_BODY:
                    gate_step(j, t)
            for j in range(MLP_AFTER, FT):
                gate_step(j)
            gate_silu(FT - 1)
            hidden_hi(FT - 2)
            hidden_hi(FT - 1)
            for c in range(DN0 + 3, NCH):
                w_split_act(act, c)
                if c == DN0 + FT // 2 + 2:
                    half_stats_act(act, S_FIN, 0)
            for i in range(NT):
                half_stats_act(act, S_FIN, 1, [i])
                act.wait_ge(fin_rms, FIN_RMS * (i + 1))
                act.wait_ge(gained, NT + i + 1)
                nc.scalar.activation(tok[:, i, 0:512], misc[:, i, 0:512], ACT.Copy,
                                     scale=fin_r[:, i, NEWTON:NEWTON + 1]).then_inc(fin_act, 1)

        @block.vector
        def _(dve):
            def proj_scale(pair, j):
                dve.wait_ge(w_used, 3 * pair + j + 1)
                if pair or j:
                    dve.wait_ge(proj_lo, 2 * pair + j)
                nc.vector.tensor_tensor(scaled[:, :], PJ[j][:, :], r_row[:, :], ALU.mult)\
                  .then_inc(proj_scaled, 1)

            def proj_lo_part(pair, j):
                dve.wait_ge(proj_hi, 2 * pair + j + 1)
                o, hi = qk_l[:, pair % 2, j, :], qk_h[:, pair % 2, j, :].bitcast(F32)
                if j == 0:
                    nc.vector.scalar_tensor_tensor(out=o, in0=scaled[:, :], scalar=-HD ** -0.5, in1=hi,
                                                   op0=ALU.mult, op1=ALU.subtract).then_inc(proj_lo, 1)
                else:
                    nc.vector.tensor_tensor(o, scaled[:, :], hi, ALU.subtract).then_inc(proj_lo, 1)

            def v_scale(pair):
                dve.wait_ge(w_used, 3 * pair + 3)
                if pair >= 1:
                    dve.wait_ge(v_turned, pair)
                nc.vector.tensor_tensor(v_raw, VB[:, :], r_row[:, :], ALU.mult).then_inc(v_scaled, 1)

            def v_lo_part(pair):
                dve.wait_ge(v_hi, pair + 1)
                nc.vector.tensor_tensor(v_l[:, pair % 2, :, :].rearrange("p a b -> p (a b)"), PJ[1][:, :],
                                        v_h[:, pair % 2, :, :].rearrange("p a b -> p (a b)").bitcast(F32),
                                        ALU.subtract).then_inc(v_lo, 1)

            nc.vector.memset(y_sq[0:NH, :], 1.0).then_inc(f_dve, 1)
            dve.wait_ge(vec_turned, 1)
            nc.vector.tensor_copy(vec[:, 0:KT], bank[7][:, 0:KT]).then_inc(vec_ready, 1)
            row_stats_dve(dve, S_X, [NT - 2])
            dve.wait_ge(vec_ready, 1)
            w_split_dve(dve, 0)
            turn_lo_dve(dve, S_X, range(KT))
            row_stats_dve(dve, S_X, [NT - 1])
            dve.wait_ge(wf_hi, 1)
            nc.vector.tensor_tensor(wf_l[:, :, :], wf_raw[:, :, :], wf_h[:, :, :].bitcast(F32),
                                    ALU.subtract).then_inc(wf_lo, 1)
            dve.wait_ge(sq_act[S_X], NT // 2)
            row_stats_dve(dve, S_MEM, [MT - 1])
            w_split_dve(dve, 1)
            dve.wait_ge(sq_dve[S_X], NT // 2)
            dve.wait_ge(sq_act[S_MEM], MT // 2)
            dve.wait_ge(sq_dve[S_MEM], MT // 2)
            inv_rms_dve(dve, S_X, ss[:, S_X, 0:NT + MT], NT + MT, D)
            spread_r_dve(dve, S_X, scaled[:, :])
            dve.wait_ge(vec_turned, 2)
            nc.vector.tensor_copy(vec[:, KT:VROWS], bank[4][:, KT:VROWS]).then_inc(vec_ready, 1)
            nc.vector.tensor_scalar(misc[:, 1, :], tok[:, 1, :], inv(S_MEM, 1), None, ALU.mult).then_inc(nrm_dve, 1)
            dve.wait_ge(r_turned, 1)
            dve.wait_ge(r_row_ready, 1)
            proj_scale(0, 0)
            dve.wait_ge(z_done, 1)
            nc.vector.tensor_tensor(fz[3], SC[0][0:NH, :], r_row[0:NH, :], ALU.mult).then_inc(z_scaled, 1)
            w_split_dve(dve, 2)
            dve.wait_ge(z_scaled, 1)
            dve.wait_ge(b_landed, 16)
            nc.vector.tensor_scalar(fz[2], fz[3], b_col[:, :], 0.0, ALU.add, ALU.min).then_inc(f_dve, 1)
            proj_lo_part(0, 0)
            dve.wait_ge(f_dve, 2)
            dve.wait_ge(f_act, 3)
            nc.vector.tensor_tensor(fz[2], fz[2], fz[0], ALU.subtract).then_inc(f_dve, 1)
            dve.wait_ge(f_dve, 3)
            nc.vector.tensor_tensor_scan(fz[3], y_sq[0:NH, :], fz[2], 0.0, ALU.mult, ALU.add).then_inc(f_dve, 1)
            proj_scale(0, 1)
            turn_lo_dve(dve, S_MEM, range(KT // 2))
            proj_lo_part(0, 1)
            w_split_dve(dve, 3)
            v_scale(0)
            turn_lo_dve(dve, S_MEM, range(KT // 2, KT))
            v_lo_part(0)
            w_split_dve(dve, 4)

            def logits(n):
                pair, hh, i = unit(n)
                h = 2 * pair + hh
                w = P * (i + 1)
                dve.wait_ge(s_done, n + 1)
                dve.wait_ge(bias_ready, h + 1)
                if n >= 2:
                    dve.wait_ge(p_ready, n - 1)
                if pair >= FOXP:
                    nc.vector.tensor_tensor_reduce(lg[:, n % 2, 0:w], SC[n % 2][:, 0:w],
                                                   cb[:, h % 2, SEQ - w:SEQ], 1.0, FLT_MAX, ALU.add, ALU.min,
                                                   minima[:, n:n + 1]).then_inc(lg_ready, 1)
                    return
                init = FLT_MAX
                if i:
                    nc.vector.tensor_tensor_reduce(lg[:, n % 2, 0:w - P], SC[n % 2][:, 0:w - P],
                                                   cb[:, h % 2, 0:w - P], 1.0, FLT_MAX, ALU.add, ALU.min,
                                                   past_min[:, n:n + 1]).then_inc(off_ready, 1)
                    dve.wait_ge(off_ready, (n // NT) * (NT - 1) + i)
                    init = past_min[:, n:n + 1]
                nc.vector.tensor_tensor_reduce(lg[:, n % 2, w - P:w], SC[n % 2][:, w - P:w],
                                               cbd[:, h % 2, w - P:w], 1.0, init, ALU.add, ALU.min,
                                               minima[:, n:n + 1]).then_inc(lg_ready, 1)

            def inv_sum(n):
                dve.wait_ge(p_ready, n + 1)
                nc.vector.reciprocal(inv_sums[:, n:n + 1], sums[:, n:n + 1]).then_inc(inv_ready, 1)

            def pt_split(n):
                i = n % NT
                dve.wait_ge(pt_hi, n + 1)
                t = slice(i * P, (i + 1) * P)
                nc.vector.tensor_tensor(pt_l[:, 0:i + 1, t],
                                        PT[n % 2][:, 0:(i + 1) * P].rearrange("p (k j) -> p k j", j=P),
                                        pt_h[:, 0:i + 1, t].bitcast(F32), ALU.subtract).then_inc(pt_lo, 1)

            def y_lo(pair):
                dve.wait_ge(act_hi[S_Y], pair + 1)
                nc.vector.scalar_tensor_tensor(out=act_l[:, pair, :], in0=y_fm[:, pair, :], scalar=gain(S_Y, pair),
                                               in1=act_h[:, pair, :].bitcast(F32), op0=ALU.mult,
                                               op1=ALU.subtract).then_inc(act_lo[S_Y], 1)

            def km_lo_part(m):
                dve.wait_ge(km_hi, m + 1)
                nc.vector.tensor_tensor(km_l[:, m, :], km_bank(m), km_h[:, m, :].bitcast(F32),
                                        ALU.subtract).then_inc(km_lo, 1)

            def vm_lo_part(h):
                for m in range(MT):
                    dve.wait_ge(vm_hi, MT * h + m + 1)
                    nc.vector.tensor_tensor(vm_l[:, m, h * 512:(h + 1) * 512], PJ[m][:, :],
                                            vm_h[:, m, h * 512:(h + 1) * 512].bitcast(F32),
                                            ALU.subtract).then_inc(vm_lo, 1)

            for n in range(NU):
                pair, u = divmod(n, UNITS)
                logits(n)
                if pair < NPAIR - 1 and u == 3:
                    proj_lo_part(pair + 1, 0)
                if pair < NPAIR - 1 and u == 6:
                    proj_lo_part(pair + 1, 1)
                inv_sum(n)
                if n >= LAST:
                    w_split_dve(dve, first_chunk(n + 1))
                if n == LAST + KT // 2:
                    vm_lo_part(0)
                if n >= 1:
                    pt_split(n - 1)
                if u == 0 and pair >= 1:
                    v_lo_part(pair)
                if pair < NPAIR - 1 and u == 2:
                    proj_scale(pair + 1, 0)
                if pair < NPAIR - 1 and u == 5:
                    proj_scale(pair + 1, 1)
                if pair < NPAIR - 1 and u == 7:
                    v_scale(pair + 1)
                if n in SPLIT_STEPS:
                    w_split_dve(dve, SPLIT_STEPS[n])
                if n == LAST:
                    km_lo_part(0)
                if n >= LAST:
                    w_split_dve(dve, first_chunk(n + 1) + 1)
                if LAST <= n < NU - 1:
                    km_lo_part(u + 1)
                if n >= LAST and u >= 1:
                    y_lo(u - 1)
            vm_lo_part(1)
            pt_split(NU - 1)
            w_split_dve(dve, WO0 + 2)
            y_lo(NPAIR - 1)

            def add_tiles(s, half, group=None, tiles=range(NT)):
                if s == 0:
                    step, last = 2 * half + group, WO0 + (KT // 2) * half + (KT // 4) * (group + 1)
                    if step == 0:
                        dve.wait_ge(x2_landed, 16)
                else:
                    step, last = half, OUT0[s] + (half + 1) * OUT_K[s]
                for i in tiles:
                    if i < NT - 1:
                        dve.wait_ge(out_done[s], (NT - 1) * step + i + 1)
                    else:
                        dve.wait_ge(w_used, last)
                    t = tok[:, i, half * 512:(half + 1) * 512]
                    if s == 0:
                        if group == 1:
                            dve.wait_ge(added[0], NT * (step - 1) + i + 1)
                        nc.vector.scalar_tensor_tensor(out=t, in0=mix_bank(group, i)[:, :],
                                                       scalar=inv(S_Y, NT * group + i), in1=t, op0=ALU.mult,
                                                       op1=ALU.add).then_inc(added[0], 1)
                    else:
                        nc.vector.tensor_tensor(t, out_bank(s, half, i)[:, :], t, ALU.add).then_inc(added[s], 1)

            for half in range(H2):
                for group in range(2):
                    for k in range(KT // 4):
                        c = WO0 + 3 + half * KT // 2 + group * KT // 4 + k
                        if c == WO0 + 4:
                            dve.wait_ge(y_stat, 1)
                            inv_rms_dve(dve, S_Y, bank[7][:, 0:2 * NT], 2 * NT, GW)
                        if c < WQ0:
                            w_split_dve(dve, c)
                    if (half, group) == (1, 1):
                        turn_lo_dve(dve, S_H1, range(KT // 2))
                        w_split_dve(dve, WQ0)
                    add_tiles(0, half, group)
            turn_lo_dve(dve, S_H1, range(KT // 2, KT))
            w_split_dve(dve, WQ0 + 1)
            halves_dve(dve, S_H1)
            nc.vector.tensor_scalar(rneg[:, :], rs[:, S_H1, NEWTON, 0:NT], -1.0, None, ALU.mult)\
              .then_inc(xb_ready, 1)

            def xq_lo_part(t):
                dve.wait_ge(xq_hi, t + 1)
                nc.vector.scalar_tensor_tensor(out=qk_l[:, (t // 2) % 2, t % 2, :], in0=PJ[t % 2][:, :],
                                               scalar=-CROSS_D ** -0.5,
                                               in1=qk_h[:, (t // 2) % 2, t % 2, :].bitcast(F32),
                                               op0=ALU.mult, op1=ALU.subtract).then_inc(xq_lo, 1)

            def xmins(m):
                dve.wait_ge(xs_done, m + 1)
                nc.vector.tensor_reduce(minima[:, m:m + 1], SC[m % 2][:, 0:MEM], AX_X, ALU.min).then_inc(xmin, 1)
                dve.wait_ge(xmin, m + 1)
                nc.vector.tensor_scalar(xbias[:, m:m + 1], minima[:, m:m + 1], inv(S_H1, m % NT), None,
                                        ALU.mult).then_inc(xb_ready, 1)

            def xnorm(m):
                dve.wait_ge(xp_ready, m + 1)
                nc.vector.reciprocal(inv_sums[:, m:m + 1], sums[:, m:m + 1]).then_inc(xinv, 1)
                dve.wait_ge(xinv, m + 1)
                nc.vector.tensor_scalar(pr[:, m % 2, 0:MEM], pr[:, m % 2, 0:MEM], inv_sums[:, m:m + 1], None,
                                        ALU.mult).then_inc(xp_norm, 1)

            def xpt_split(h):
                for t in range(MT):
                    dve.wait_ge(xpt_hi, MT * h + t + 1)
                    nc.vector.tensor_tensor(xp_l[:, t, :], PT[t][:, :], xp_h[:, t, :].bitcast(F32),
                                            ALU.subtract).then_inc(xpt_lo, 1)

            def xo_lo_part(h):
                for d in range(2):
                    dve.wait_ge(xo_hi, 2 * h + d + 1)
                    nc.vector.tensor_tensor(ox_l[:, 2 * h + d, :], OB[d][:, :],
                                            ox_h[:, 2 * h + d, :].bitcast(F32), ALU.subtract).then_inc(xo_lo, 1)

            w_split_dve(dve, WQ0 + 2)
            xq_lo_part(0)
            xq_lo_part(1)
            w_split_dve(dve, WQ0 + 3)
            for m in range(NX * NT + 2):
                h, i = divmod(m, NT)
                if m < NX * NT:
                    xmins(m)
                    xnorm(m)
                if m in XSPLIT:
                    w_split_dve(dve, XSPLIT[m])
                if m % 2 == 0 and m // 2 + 2 < 2 * NX:
                    xq_lo_part(m // 2 + 2)
                if i == 0 and h >= 1:
                    xpt_split(h - 1)
                if h >= 1 and i == (2 if h < NX - 1 else 1):
                    xo_lo_part(h - 1)
            for c in range(XO0 + 3, UP0):
                w_split_dve(dve, c)
                if c == XO0 + KT // 2 + 2:
                    add_tiles(1, 0)
            turn_lo_dve(dve, S_H2, range(KT // 2))
            w_split_dve(dve, UP0)
            add_tiles(1, 1)
            turn_lo_dve(dve, S_H2, range(KT // 2, KT))
            w_split_dve(dve, UP0 + 1)
            halves_dve(dve, S_H2)
            spread_r_dve(dve, S_H2, scaled[:, :])
            w_split_dve(dve, UP0 + 2)
            dve.wait_ge(r_row_ready, 2)

            def g_norm(j, t=0):
                tile = j + MLP_TURN * t
                dve.wait_ge(w_used, UP0 + 1 + 2 * tile)
                if j >= 2:
                    dve.wait_ge(g_conv2, tile - 1)
                nc.vector.tensor_tensor(gr[:, j % 2, :], bank[(2 * j) % 4][:, :], r_row[:, :], ALU.mult)\
                  .then_inc(g_normed, 1)

            def conv(j, t=0):
                tile = j + MLP_TURN * t
                g, b = gc[:, j % 2, :], gr[:, j % 2, :]
                dve.wait_ge(g_scaled, tile + 1)
                nc.vector.scalar_tensor_tensor(out=g[:, 1:SEQ], in0=b[:, 0:SEQ - 1], scalar=vec_col("cw", FT + tile),
                                               in1=g[:, 1:SEQ], op0=ALU.mult, op1=ALU.add).then_inc(g_conv1, 1)
                dve.wait_ge(g_conv1, tile + 1)
                nc.vector.scalar_tensor_tensor(out=g[:, 2:SEQ], in0=b[:, 0:SEQ - 2], scalar=vec_col("cw", tile),
                                               in1=g[:, 2:SEQ], op0=ALU.mult, op1=ALU.add).then_inc(g_conv2, 1)

            def u_norm(j, t=0):
                tile = j + MLP_TURN * t
                dve.wait_ge(w_used, UP0 + 2 + 2 * tile)
                if j >= 2:
                    dve.wait_ge(h_lo, tile - 1)
                nc.vector.tensor_tensor(ur[:, j % 2, :], bank[(2 * j + 1) % 4][:, :], r_row[:, :], ALU.mult)\
                  .then_inc(u_normed, 1)

            def gated(j, t=0):
                tile = j + MLP_TURN * t
                dve.wait_ge(g_silu, tile + 1)
                dve.wait_ge(u_normed, tile + 1)
                nc.vector.tensor_tensor(ur[:, j % 2, :], ur[:, j % 2, :], gs[:, j % 2, :],
                                        ALU.mult).then_inc(h_ready, 1)

            def hidden_lo(j, t=0):
                tile = j + MLP_TURN * t
                dve.wait_ge(h_hi, tile + 1)
                nc.vector.tensor_tensor(hidden(1, tile), ur[:, j % 2, :], hidden(0, tile).bitcast(F32),
                                        ALU.subtract).then_inc(h_lo, 1)

            def mlp_step(j, t=0):
                g_norm(j, t)
                w_split_dve(dve, UP0 + 2 * j + 3, t)
                conv(j, t)
                if j >= 1:
                    gated(j - 1, t)
                if j >= 2:
                    hidden_lo(j - 2, t)
                u_norm(j, t)
                w_split_dve(dve, UP0 + 2 * j + 4, t)

            for j in range(MLP_FIRST):
                mlp_step(j)
            with dve.Fori(0, MLP_TURNS) as t:
                for j in MLP_BODY:
                    mlp_step(j, t)
            for j in range(MLP_AFTER, FT):
                mlp_step(j)
            gated(FT - 1)
            hidden_lo(FT - 2)
            hidden_lo(FT - 1)

            def gain_part(half, i):
                t = slice(half * 512, (half + 1) * 512)
                dve.wait_ge(added[2], NT * half + i + 1)
                nc.vector.tensor_tensor(misc[:, i, t], tok[:, i, t], row[:, t], ALU.mult).then_inc(gained, 1)

            def fin_inv_rms(i):
                f0 = FIN_RMS * i
                m, m2, g = fin_m[:, i, 0:1], fin_m[:, i, 1:2], fin_seed[:, i:i + 1]
                dve.wait_ge(sq_act[S_FIN], NT + i + 1)
                nc.vector.scalar_tensor_tensor(out=m, in0=ss[:, S_FIN, NT + i:NT + i + 1], scalar=1.0 / D,
                                               in1=ms[:, S_FIN, i:i + 1], op0=ALU.mult, op1=ALU.add)\
                  .then_inc(fin_rms, 1)
                dve.wait_ge(fin_rms, f0 + 1)
                nc.vector.tensor_scalar(g, m.bitcast(I32), 1, None, ALU.logical_shift_right).then_inc(fin_rms, 1)
                nc.vector.tensor_scalar(m2, m, -0.5, None, ALU.mult).then_inc(fin_rms, 1)
                dve.wait_ge(fin_rms, f0 + 2)
                nc.vector.tensor_scalar(fin_r[:, i, 0:1].bitcast(I32), g, -1.0, float(0x5f3759df),
                                        ALU.mult, ALU.add).then_inc(fin_rms, 1)
                for t in range(NEWTON):
                    r = fin_r[:, i, t:t + 1]
                    dve.wait_ge(fin_rms, f0 + 4 + 2 * t)
                    nc.vector.scalar_tensor_tensor(out=fin_t[:, i, t:t + 1], in0=m2, scalar=r, in1=r,
                                                   op0=ALU.mult, op1=ALU.mult).then_inc(fin_rms, 1)
                    dve.wait_ge(fin_rms, f0 + 5 + 2 * t)
                    nc.vector.scalar_tensor_tensor(out=fin_r[:, i, t + 1:t + 2], in0=fin_t[:, i, t:t + 1],
                                                   scalar=1.5, in1=r, op0=ALU.add, op1=ALU.mult)\
                      .then_inc(fin_rms, 1)

            for c in range(DN0 + 3, NCH):
                w_split_dve(dve, c)
                if c == DN0 + FT // 2 + 2:
                    add_tiles(2, 0)
                    dve.wait_ge(gf_landed, 16)
                    for i in range(NT):
                        gain_part(0, i)
                    dve.wait_ge(sq_act[S_FIN], NT)
                    nc.vector.tensor_scalar(ms[:, S_FIN, 0:NT], ss[:, S_FIN, 0:NT], 1.0 / D, EPS, ALU.mult,
                                            ALU.add).then_inc(sq_dve[S_FIN], 1)
            dve.wait_ge(sq_dve[S_FIN], 1)
            for i in range(NT):
                add_tiles(2, 1, tiles=[i])
                gain_part(1, i)
                fin_inv_rms(i)
                dve.wait_ge(fin_rms, FIN_RMS * (i + 1))
                dve.wait_ge(gained, NT + i + 1)
                nc.vector.tensor_scalar(tok[:, i, 512:D], misc[:, i, 512:D], fin_r[:, i, NEWTON:NEWTON + 1],
                                        None, ALU.mult).then_inc(fin_dve, 1)

        @block.tensor
        def _(pe):
            def f_triples(c, o, a, w, ks, fresh=None):
                for k in ks:
                    if fresh is not None:
                        pe.wait_ge(fresh, k + 1)
                    wh, wl = w_tile(c, k, P)
                    last = mm3(o, wh, wl, a[0][:, k, 0:w], a[1][:, k, 0:w], k == 0, k == KT - 1)
                if k == KT - 1:
                    last.then_inc(w_used, 1)

            def t_triples(c, outs, a, k0, k_first, k_end, signal=None, late=None):
                for i, o in enumerate(outs):
                    if late is not None and i == 2:
                        pe.wait_ge(late, MT * H2)
                    for k in range(2):
                        wh, wl = w_tile(c, k, 512)
                        t = slice(i * P, (i + 1) * P)
                        last = mm3(o[:, :], a[0][:, k0 + k, t], a[1][:, k0 + k, t], wh, wl,
                                   k0 + k == k_first, k0 + k == k_end - 1)
                    if i == len(outs) - 1:
                        last.then_inc(w_used, 1)
                    elif signal is not None and k0 + 2 == k_end:
                        last.then_inc(signal, 1)

            def v_turn(pair):
                pe.wait_ge(v_scaled, pair + 1)
                pe.wait_ge(proj_scaled, 2 * pair + 2)
                for i in range(NT):
                    last = nc.tensor.transpose(PJ[1][:, i * P:(i + 1) * P], v_raw[:, i * P:(i + 1) * P],
                                               ident[:, :])
                last.then_inc(v_turned, 1)

            acts, mem_acts = (act_h, act_l), (mn_h, mn_l)

            mix = KT
            pe.wait_ge(ident_ready, 2)
            pe.wait_ge(mix_landed, 16)
            nc.tensor.transpose(bank[7][:, 0:mix], vec_rows[0:mix, :], ident[0:mix, 0:mix]).then_inc(vec_turned, 1)
            for i in range(NT):
                pe.wait_ge(x_landed[i], 16)
                for k in range(KT):
                    if (i, k) == (0, KT - 1):
                        pe.wait_ge(vec_ready, 1)
                    last = nc.tensor.transpose(turn_bank(S_X, k)[:, i * P:(i + 1) * P],
                                               tok[:, i, k * P:(k + 1) * P], ident[:, :])
                    if i == NT - 1:
                        last.then_inc(turned[S_X], 1)

            pe.wait_ge(w_lo, 1)
            f_triples(0, PJ[0][:, :], acts, SEQ, range(KT), fresh=act_lo[S_X])
            pe.wait_ge(vec_landed, 16 * (len(VEC) - 1))
            nc.tensor.transpose(bank[4][:, 0:VROWS], vec_rows[0:VROWS, :], ident[0:VROWS, 0:VROWS])\
              .then_inc(vec_turned, 1)
            pe.wait_ge(wf_lo, 1)
            for k in range(KT):
                last = mm3(SC[0][0:NH, :], wf_h[:, k, :], wf_l[:, k, :], act_h[:, k, :], act_l[:, k, :],
                           k == 0, k == KT - 1)
            last.then_inc(z_done, 1)
            turn_r_pe(pe, 1, bank[3], scaled)
            pe.wait_ge(w_lo, 2)
            f_triples(1, PJ[1][:, :], acts, SEQ, range(KT))
            pe.wait_ge(vec_ready, 2)
            pe.wait_ge(r_row_ready, 1)
            pe.wait_ge(nrm_act, 1)
            pe.wait_ge(nrm_dve, 1)
            turn_pe(pe, S_MEM, range(KT // 2))
            pe.wait_ge(w_lo, 3)
            f_triples(2, VB[:, :], acts, SEQ, range(KT))
            turn_pe(pe, S_MEM, range(KT // 2, KT))
            v_turn(0)
            pe.wait_ge(z_scaled, 1)

            def scores(n):
                pair, hh, i = unit(n)
                pe.wait_ge(proj_lo, 2 * pair + 2)
                if n >= 2:
                    pe.wait_ge(lg_ready, n - 1)
                r, t, w = slice(hh * HD, (hh + 1) * HD), slice(i * P, (i + 1) * P), P * (i + 1)
                s = pair % 2
                mm3(SC[n % 2][:, 0:w], qk_h[r, s, 0, t], qk_l[r, s, 0, t], qk_h[r, s, 1, 0:w],
                    qk_l[r, s, 1, 0:w], True, True).then_inc(s_done, 1)

            def p_turn(n):
                _, _, i = unit(n)
                pe.wait_ge(p_norm, n + 1)
                if n >= 2:
                    pe.wait_ge(pt_lo, n - 1)
                for k in range(i + 1):
                    last = nc.tensor.transpose(PT[n % 2][:, k * P:(k + 1) * P],
                                               pr[:, n % 2, k * P:(k + 1) * P], ident[:, :])
                last.then_inc(p_turned, 1)

            def pv(h):
                pair, hh = divmod(h, 2)
                pe.wait_ge(pt_lo, NT * (h + 1))
                pe.wait_ge(v_lo, pair + 1)
                if h >= 1:
                    pe.wait_ge(y_ready, h)
                d = slice(hh * HD, (hh + 1) * HD)
                for k in range(NT):
                    t = slice(k * P, SEQ)
                    last = mm3(YB[0:HD, t], v_h[:, pair % 2, k, d], v_l[:, pair % 2, k, d],
                               pt_h[:, k, t], pt_l[:, k, t], k == 0, k == NT - 1)
                last.then_inc(pv_done, 1)

            def project(pair, lo, hi):
                for m in range(lo, hi):
                    j, k = divmod(m, KT)
                    if k == 0:
                        pe.wait_ge(w_lo, 3 * pair + j + 1)
                        if j == 0:
                            pe.wait_ge(proj_scaled, 2 * pair - 1)
                        if j == 1:
                            pe.wait_ge(v_lo, pair)
                        if j == 2:
                            pe.wait_ge(v_scaled, pair)
                    f_triples(3 * pair + j, (PJ[0], PJ[1], VB)[j][:, :], acts, SEQ, [k])

            def mem_chunk(c):
                kind, m = mem_chunks[c]
                pe.wait_ge(w_lo, c + 1)
                if kind == "k":
                    if m == 0:
                        pe.wait_ge(proj_scaled, 2 * NPAIR - 1)
                    if m == 1:
                        pe.wait_ge(v_scaled, NPAIR)
                    if m >= 2:
                        pe.wait_ge(km_lo, m)
                    f_triples(c, km_bank(m), mem_acts, MEM, range(KT))
                else:
                    h, k = divmod(m, KT // 2)
                    if m == 0:
                        pe.wait_ge(v_lo, NPAIR)
                        pe.wait_ge(km_lo, 1)
                    if m == KT // 2:
                        pe.wait_ge(vm_lo, MT)
                    t_triples(c, PJ, mem_acts, 2 * k, 0, KT)

            for n in range(NU):
                pair, u = divmod(n, UNITS)
                lo, mid, hi = STEPS[u], STEPS[u] + BEFORE[u], STEPS[u + 1]
                scores(n)
                if n == 0:
                    pe.wait_ge(act_lo[S_MEM], KT)
                if pair < NPAIR - 1:
                    project(pair + 1, lo, mid)
                else:
                    mem_chunk(first_chunk(n))
                if u == 0 and pair >= 1:
                    v_turn(pair)
                if n >= 1:
                    p_turn(n - 1)
                if n % NT == 1 and n >= NT:
                    pv(n // NT - 1)
                if pair < NPAIR - 1:
                    project(pair + 1, mid, hi)
                else:
                    mem_chunk(first_chunk(n) + 1)

            def mix_out(c):
                half, k = divmod(c, KT // 2)
                group = k // (KT // 4)
                pe.wait_ge(w_lo, WO0 + c + 1)
                if half == 0:
                    pe.wait_ge(act_lo[S_Y], 2 * k + 2)
                elif k % (KT // 4) == 0:
                    pe.wait_ge(added[0], NT * (group + 1))
                if c == KT // 4:
                    pe.wait_ge(rms[S_Y], 1)
                t_triples(WO0 + c, [mix_bank(group, i) for i in range(NT)], acts, 2 * k, 4 * group,
                          4 * group + 4, out_done[0], late=vm_lo if c == 0 else None)

            p_turn(NU - 1)
            mix_out(0)
            pv(2 * NPAIR - 1)
            mix_out(1)
            pe.wait_ge(y_summed, NPAIR - 2)
            pe.wait_ge(y_ready, 2 * NPAIR)
            for g in range(2):
                for i in range(NT):
                    e = NT * g + i
                    last = nc.tensor.matmul(bank[7][:, e:e + 1], y_acc[:, g, i * P:(i + 1) * P],
                                            ones[:, :], start=True, stop=True)
            last.then_inc(y_stat, 1)
            for c in range(2, KT):
                mix_out(c)
                if c == KT - 2:
                    pe.wait_ge(added[0], 3 * NT)
                    turn_pe(pe, S_H1, range(KT // 2))

            def token_out(s, a, ready, turn=None, first=0, end=0):
                for c in range(first, 2 * OUT_K[s] - end):
                    half, k = divmod(c, OUT_K[s])
                    pe.wait_ge(w_lo, OUT0[s] + c + 1)
                    if half == 0:
                        pe.wait_ge(ready, 2 * k + 2)
                    if turn is not None and c == 2 * OUT_K[s] - 1:
                        pe.wait_ge(added[s], NT)
                        turn_pe(pe, turn, range(KT // 2))
                    t_triples(OUT0[s] + c, [out_bank(s, half, i) for i in range(NT)], a, 2 * k, 0,
                              2 * OUT_K[s], out_done[s])

            pe.wait_ge(w_lo, WQ0 + 1)
            pe.wait_ge(act_lo[S_H1], KT // 2)
            f_triples(WQ0, PJ[0][:, :], acts, SEQ, range(KT // 2))
            pe.wait_ge(added[0], 4 * NT)
            turn_pe(pe, S_H1, range(KT // 2, KT))
            f_triples(WQ0, PJ[0][:, :], acts, SEQ, range(KT // 2, KT), fresh=act_lo[S_H1])
            pe.wait_ge(w_lo, WQ0 + 2)
            f_triples(WQ0 + 1, PJ[1][:, :], acts, SEQ, range(KT))

            def xscores(m):
                h, i = divmod(m, NT)
                pe.wait_ge(xq_lo, 2 * h + 2)
                if m >= 2:
                    pe.wait_ge(xp_ready, m - 1)
                t = slice(i * P, (i + 1) * P)
                for d in range(2):
                    last = mm3(SC[m % 2][:, 0:MEM], qk_h[:, h % 2, d, t], qk_l[:, h % 2, d, t],
                               km_h[:, 2 * h + d, :], km_l[:, 2 * h + d, :], d == 0, d == 1)
                last.then_inc(xs_done, 1)

            def xp_turn(m):
                h, i = divmod(m, NT)
                pe.wait_ge(xp_norm, m + 1)
                if i == 0 and h >= 1:
                    pe.wait_ge(xpt_lo, MT * h)
                for t in range(MT):
                    last = nc.tensor.transpose(PT[t][:, i * P:(i + 1) * P], pr[:, m % 2, t * P:(t + 1) * P],
                                               ident[:, :])
                last.then_inc(xp_turned, 1)

            def xpv(h):
                pe.wait_ge(xpt_lo, MT * (h + 1))
                if h >= 1:
                    pe.wait_ge(xo_lo, 2 * h)
                for d in range(2):
                    f = slice((2 * h + d) * P, (2 * h + d + 1) * P)
                    for t in range(MT):
                        last = mm3(OB[d][:, :], vm_h[:, t, f], vm_l[:, t, f], xp_h[:, t, :], xp_l[:, t, :],
                                   t == 0, t == MT - 1)
                    last.then_inc(xo_done, 1)

            def xproject(half):
                t, part = half // 2 + 2, half % 2
                if part == 0:
                    pe.wait_ge(w_lo, WQ0 + t + 1)
                    pe.wait_ge(xq_lo, t - 1)
                f_triples(WQ0 + t, PJ[t % 2][:, :], acts, SEQ, range(part * KT // 2, (part + 1) * KT // 2))

            def xout(c, i):
                pe.wait_ge(w_lo, XO0 + c + 1)
                pe.wait_ge(xo_lo, 2 * c + 2)
                for k in range(2):
                    wh, wl = w_tile(XO0 + c, k, 512)
                    t = slice(i * P, (i + 1) * P)
                    last = mm3(out_bank(1, 0, i)[:, :], ox_h[:, 2 * c + k, t], ox_l[:, 2 * c + k, t], wh, wl,
                               c + k == 0, False)
                if i == NT - 1:
                    last.then_inc(w_used, 1)

            XOUT = {11: [(0, 0), (0, 1)], 12: [(1, 0)], 13: [(1, 1)], 14: [(2, 0)], 15: [(2, 1)],
                    16: [(0, 2), (0, 3)]}
            xproject(0)
            for m in range(NX * NT + 2):
                h, i = divmod(m, NT)
                if m < NX * NT:
                    xscores(m)
                if m + 1 < 2 * 2 * (NX - 1):
                    xproject(m + 1)
                if m == NX * NT:
                    xp_turn(m - 1)
                    pe.wait_ge(xp_ready, NX * NT)
                for c, t in XOUT.get(m, []):
                    if m == 11:
                        pe.wait_ge(xq_lo, 2 * NX)
                    xout(c, t)
                if 1 <= m < NX * NT:
                    xp_turn(m - 1)
                if i == 1 and h >= 1:
                    xpv(h - 1)
            for c in (1, 2):
                for i in (2, 3):
                    xout(c, i)
            token_out(1, (ox_h, ox_l), xo_lo, turn=S_H2, first=3)

            pe.wait_ge(w_lo, UP0 + 1)
            pe.wait_ge(act_lo[S_H2], KT // 2)
            f_triples(UP0, bank[0][:, :], acts, SEQ, range(KT // 2))
            pe.wait_ge(added[1], 2 * NT)
            turn_pe(pe, S_H2, range(KT // 2, KT))
            f_triples(UP0, bank[0][:, :], acts, SEQ, range(KT // 2, KT), fresh=act_lo[S_H2])
            pe.wait_ge(w_lo, UP0 + 2)
            f_triples(UP0 + 1, bank[1][:, :], acts, SEQ, range(KT // 2))
            turn_r_pe(pe, 2, bank[7], scaled)
            f_triples(UP0 + 1, bank[1][:, :], acts, SEQ, range(KT // 2, KT))

            def up_project(j, t=0):
                for g in range(2):
                    c = UP0 + 2 * j + g
                    pe.wait_ge(w_lo, c + 1 + 2 * MLP_TURN * t)
                    if j >= 2:
                        pe.wait_ge(u_normed if g else g_normed, j - 1 + MLP_TURN * t)
                    f_triples(c, bank[(2 * j + g) % 4][:, :], acts, SEQ, range(KT))

            for j in range(1, MLP_FIRST):
                up_project(j)
            with pe.Fori(0, MLP_TURNS) as t:
                for j in MLP_BODY:
                    up_project(j, t)
            for j in range(MLP_AFTER, FT):
                up_project(j)
            token_out(2, (ff_h, ff_l), h_lo, end=RING)
            for i in range(NT):
                t = slice(i * P, (i + 1) * P)
                for c in range(NCH - RING, NCH):
                    pe.wait_ge(w_lo, c + 1)
                    for k in range(FT - 2 * (NCH - c), FT - 2 * (NCH - c) + 2):
                        wh, wl = w_tile(c, k % 2, 512)
                        last = mm3(out_bank(2, 1, i)[:, :], ff_h[:, k, t], ff_l[:, k, t], wh, wl, False, k == FT - 1)
                    if i == NT - 1:
                        last.then_inc(w_used, 1)
                    elif c == NCH - 1:
                        last.then_inc(out_done[2], 1)


_INS = ["x", "mem", "g_mix", "w_in", "b_forget", "g_fox", "g_moba", "w_out", "g_cross", "g_mem", "w_q_mem",
        "w_kv_mem", "w_o_mem", "g_ffn", "w_up", "conv_w", "conv_b", "w_down", "g_final"]


def kernel(**inputs):
    import numpy as _np
    import concourse.bacc as _bacc
    from concourse.bass_utils import run_bass_kernel_spmd as _run

    nc = _bacc.Bacc("TRN2", target_bir_lowering=False, num_devices=1)
    arrays, args = {}, []
    for name in _INS:
        a = _np.ascontiguousarray(inputs[name])
        arrays[f"in_{name}"] = a
        args.append(nc.dram_tensor(f"in_{name}", a.shape, mybir.dt.from_np(a.dtype), kind="ExternalInput").ap())
    args.append(nc.dram_tensor("out_0", inputs["x"].shape, F32, kind="ExternalOutput").ap())
    hymba_layer(nc, *args)
    r = _run(nc, [arrays], core_ids=[0])
    return r.results[0]["out_0"]
```
